# Optimizing a Trainium2 kernel written in Bass

```python
import jax, jax.numpy as jnp
from jax import lax
import numpy as np

D_MODEL = 1024
BATCH = 1
SEQ = 512
DEPTH = 2

GRID_W = 64
CTX_LEN = 256
N_MOD = 6
NORM_EPS = 1e-6
HEAD_DIM = 64
RWKV_HEADS = 6
RWKV_W = RWKV_HEADS * HEAD_DIM
DECAY_LORA = 64
ICLR_LORA = 64
GATE_LORA = 160
GN_EPS = 64e-5
MLA_HEADS = 6
MLA_NOPE = 64
MLA_ROPE = 32
MLA_V = 64
MLA_W = MLA_HEADS * MLA_V
Q_LORA = 256
KV_LORA = 128
MLA_SCALE = (MLA_NOPE + MLA_ROPE) ** -0.5
ROPE_BASE = 10000.0
Q_BLOCK = 128
FOURIER_GROUPS = 4
FOURIER_CH = 64
FOURIER_W = FOURIER_GROUPS * FOURIER_CH
D_MIX = RWKV_W + MLA_W + FOURIER_W
IN_SIZES = (RWKV_W, RWKV_W, RWKV_W, DECAY_LORA, ICLR_LORA, GATE_LORA, Q_LORA, KV_LORA, MLA_ROPE, FOURIER_W)
D_IN = 3 * RWKV_W + DECAY_LORA + ICLR_LORA + GATE_LORA + Q_LORA + KV_LORA + MLA_ROPE + FOURIER_W
N_EXPERTS = 16
EC_CAPACITY = 2
EXPERT_FF = 1024

kernel_name = "hybrid_rwkv7_mla_fnet_ec_moe_diffusion"

def rmsnorm(x, g):
    xf = x.astype(jnp.float32)
    y = xf * lax.rsqrt(jnp.mean(xf * xf, axis=-1, keepdims=True) + NORM_EPS)
    return (y * g.astype(jnp.float32)).astype(x.dtype)

def split_cols(u):
    return jnp.split(u, np.cumsum(IN_SIZES)[:-1].tolist(), axis=-1)

def rope_1d(x, pos):
    n = x.shape[-1] // 2
    inv = ROPE_BASE ** (-jnp.arange(n, dtype=jnp.float32) / n)
    ang = pos.astype(jnp.float32)[:, None] * inv[None, :]
    cos = jnp.cos(ang)[None, :, None, :]
    sin = jnp.sin(ang)[None, :, None, :]
    xf = x.astype(jnp.float32)
    x1, x2 = xf[..., :n], xf[..., n:]
    return jnp.concatenate([x1 * cos - x2 * sin, x2 * cos + x1 * sin], axis=-1).astype(x.dtype)

def rope_2d(x):
    rows = x.shape[1] // GRID_W
    row = jnp.repeat(jnp.arange(rows), GRID_W)
    col = jnp.tile(jnp.arange(GRID_W), rows)
    half = x.shape[-1] // 2
    return jnp.concatenate([rope_1d(x[..., :half], row), rope_1d(x[..., half:], col)], axis=-1)

def short_conv(u, w):
    up = jnp.pad(u, ((0, 0), (1, 1), (0, 0)))
    return up[:, :-2] * w[0] + up[:, 1:-1] * w[1] + up[:, 2:] * w[2]

def rwkv_scan(r, w, k, v, a_vec, b_vec, s0, reverse):
    def step(S, inp):
        rt, wt, kt, vt, at, bt = inp
        S = (S * wt[:, :, None, :]
             + jnp.einsum("bhvk,bhk->bhv", S, at)[..., None] * bt[:, :, None, :]
             + vt[..., None] * kt[:, :, None, :])
        return S, jnp.einsum("bhvk,bhk->bhv", S, rt)
    xs = tuple(jnp.moveaxis(t, 1, 0) for t in (r, w, k, v, a_vec, b_vec))
    s_final, ys = lax.scan(step, s0, xs, reverse=reverse)
    return jnp.moveaxis(ys, 0, 1), s_final

def rwkv_prep(u, conv_w, w0, w2, a0, a2, g2, k_k, k_a):
    r, k, v, wd, ad, gd = u
    B, L, _ = r.shape
    hd = lambda t: t.reshape(B, L, RWKV_HEADS, HEAD_DIM)
    rkv = short_conv(jnp.concatenate([r, k, v], axis=-1), conv_w).astype(jnp.float32)
    r, k, v = jnp.split(rkv, 3, axis=-1)
    kk = hd(k * k_k)
    kk = kk / jnp.maximum(jnp.sqrt(jnp.sum(kk * kk, axis=-1, keepdims=True)), 1e-12)
    wd_t = jnp.tanh(wd.astype(jnp.float32))
    ad = ad.astype(jnp.float32)
    dirs = []
    for d in range(2):
        wlog = -jax.nn.softplus(-(w0[d] + wd_t @ w2[d])) - 0.5
        decay = jnp.exp(-jnp.exp(wlog))
        a = jax.nn.sigmoid(a0[d] + ad @ a2[d])
        kd = k * (1.0 + (a - 1.0) * k_a)
        dirs.append((hd(decay), hd(kd), -kk, kk * hd(a)))
    g = jax.nn.sigmoid(gd.astype(jnp.float32)) @ g2
    return hd(r), hd(v), dirs, g

def rwkv_post(y, r, v, dirs, g, r_k, lnx_w, lnx_b):
    B, L = y.shape[:2]
    mu = jnp.mean(y, axis=-1, keepdims=True)
    var = jnp.mean(jnp.square(y - mu), axis=-1, keepdims=True)
    yn = (y - mu) * lax.rsqrt(var + GN_EPS) * lnx_w.reshape(RWKV_HEADS, HEAD_DIM) + lnx_b.reshape(RWKV_HEADS, HEAD_DIM)
    bonus = sum(jnp.sum(r * kd * r_k, axis=-1, keepdims=True) * v for (_, kd, _, _) in dirs)
    return (yn + bonus).reshape(B, L, RWKV_W) * g

def rwkv_mixer(uc, ux, conv_w, w0, w2, a0, a2, g2, k_k, k_a, r_k, lnx_w, lnx_b, need_ctx):
    rc, vc, dc, gc = rwkv_prep(uc, conv_w, w0, w2, a0, a2, g2, k_k, k_a)
    rx, vx, dx, gx = rwkv_prep(ux, conv_w, w0, w2, a0, a2, g2, k_k, k_a)
    s0 = jnp.zeros((rx.shape[0], RWKV_HEADS, HEAD_DIM, HEAD_DIM), jnp.float32)
    ycs, yxs = [], []
    for d, rev in enumerate((False, True)):
        wc, kc, ac, bc = dc[d]
        yc_d, s_ctx = rwkv_scan(rc, wc, kc, vc, ac, bc, s0, rev)
        wx, kx, ax, bx = dx[d]
        yx_d, _ = rwkv_scan(rx, wx, kx, vx, ax, bx, s_ctx, rev)
        ycs.append(yc_d)
        yxs.append(yx_d)
    out_x = rwkv_post(yxs[0] + yxs[1], rx, vx, dx, gx, r_k, lnx_w, lnx_b).astype(ux[0].dtype)
    out_c = rwkv_post(ycs[0] + ycs[1], rc, vc, dc, gc, r_k, lnx_w, lnx_b).astype(uc[0].dtype) if need_ctx else None
    return out_c, out_x

def mla_project(qd, kvd, kr, g_q, w_qup, g_kv, w_kvup, rotary):
    B, L, _ = qd.shape
    q = (rmsnorm(qd, g_q) @ w_qup).reshape(B, L, MLA_HEADS, MLA_NOPE + MLA_ROPE)
    kv = (rmsnorm(kvd, g_kv) @ w_kvup).reshape(B, L, MLA_HEADS, MLA_NOPE + MLA_V)
    q_nope, q_rope = q[..., :MLA_NOPE], q[..., MLA_NOPE:]
    k_nope, v = kv[..., :MLA_NOPE], kv[..., MLA_NOPE:]
    k_rope = kr[:, :, None, :]
    if rotary:
        q_rope = rope_2d(q_rope)
        k_rope = rope_2d(k_rope)
    q = jnp.concatenate([q_nope, q_rope], axis=-1)
    k = jnp.concatenate([k_nope, jnp.broadcast_to(k_rope, (B, L, MLA_HEADS, MLA_ROPE))], axis=-1)
    return q, k, v

def attend(q, k, v):
    s = jnp.einsum("bqhd,bkhd->bhqk", q, k).astype(jnp.float32) * MLA_SCALE
    p = jax.nn.softmax(s, axis=-1)
    return jnp.einsum("bhqk,bkhd->bqhd", p.astype(v.dtype), v)

def mla_mixer(uc, ux, g_q, w_qup, g_kv, w_kvup, need_ctx):
    qc, kc, vc = mla_project(*uc, g_q, w_qup, g_kv, w_kvup, False)
    qx, kx, vx = mla_project(*ux, g_q, w_qup, g_kv, w_kvup, True)
    B, L = qx.shape[:2]
    keys = jnp.concatenate([kc, kx], axis=1)
    vals = jnp.concatenate([vc, vx], axis=1)
    nb = L // Q_BLOCK
    qb = jnp.moveaxis(qx.reshape(B, nb, Q_BLOCK, MLA_HEADS, MLA_NOPE + MLA_ROPE), 1, 0)
    ob = lax.map(lambda q_blk: attend(q_blk, keys, vals), qb)
    out_x = jnp.moveaxis(ob, 0, 1).reshape(B, L, MLA_W)
    out_c = attend(qc, kc, vc).reshape(B, qc.shape[1], MLA_W) if need_ctx else None
    return out_c, out_x

def fourier_mixer(u, w_f):
    B, L, _ = u.shape
    z = u.astype(jnp.float32).reshape(B, L, FOURIER_GROUPS, FOURIER_CH)
    z = jnp.fft.fft2(z, axes=(1, 3), norm="ortho").real
    return z.reshape(B, L, FOURIER_W).astype(u.dtype) @ w_f

def ec_moe(h, w_router, w_gate, w_up, w_down):
    B, L, D = h.shape
    cap = max(1, EC_CAPACITY * L // N_EXPERTS)
    aff = jax.nn.softmax((h @ w_router).astype(jnp.float32), axis=-1)
    vals, idx = lax.top_k(jnp.swapaxes(aff, 1, 2), cap)
    xs = jax.vmap(lambda hb, ib: hb[ib])(h, idx)
    hid = jax.nn.silu(jnp.einsum("becd,edf->becf", xs, w_gate)) * jnp.einsum("becd,edf->becf", xs, w_up)
    out = jnp.einsum("becf,efd->becd", hid, w_down) * vals[..., None].astype(h.dtype)
    return jax.vmap(lambda ib, ob: jnp.zeros((L, D), h.dtype).at[ib.reshape(-1)].add(ob.reshape(-1, D)))(idx, out)

def layer(x, h, c, c_ctx, p, last):
    mod_x = (jax.nn.silu(c) @ p["w_mod"] + p["b_mod"])[:, None, :]
    mod_c = jax.nn.silu(c_ctx) @ p["w_mod"] + p["b_mod"]
    sx = jnp.split(mod_x, N_MOD, axis=-1)
    sc = jnp.split(mod_c, N_MOD, axis=-1)

    def mix_in(t, m):
        return rmsnorm(t, p["g_pre_mix"]) * (1.0 + m[1]) + m[0]

    def mix_out(t, parts, m):
        return t + m[2] * rmsnorm(jnp.concatenate(parts, axis=-1) @ p["w_out"], p["g_post_mix"])

    def ffn(t, m):
        tn = rmsnorm(t, p["g_pre_ffn"]) * (1.0 + m[4]) + m[3]
        y = ec_moe(tn, p["w_router"], p["w_expert_gate"], p["w_expert_up"], p["w_expert_down"])
        return t + m[5] * rmsnorm(y, p["g_post_ffn"])

    ux = split_cols(mix_in(x, sx) @ p["w_in"])
    uh = split_cols(mix_in(h, sc) @ p["w_in"])
    need_ctx = not last
    rc, rx = rwkv_mixer(uh[:6], ux[:6], p["conv_rkv"], p["rwkv_w0"], p["rwkv_w2"], p["rwkv_a0"], p["rwkv_a2"],
                        p["rwkv_g2"], p["rwkv_k_k"], p["rwkv_k_a"], p["rwkv_r_k"], p["rwkv_lnx_w"], p["rwkv_lnx_b"],
                        need_ctx)
    mc, mx = mla_mixer(uh[6:9], ux[6:9], p["mla_g_q"], p["mla_w_qup"], p["mla_g_kv"], p["mla_w_kvup"], need_ctx)
    fx = fourier_mixer(ux[9], p["w_fourier"])
    x = ffn(mix_out(x, (rx, mx, fx), sx), sx)
    if need_ctx:
        fc = fourier_mixer(uh[9], p["w_fourier"])
        h = ffn(mix_out(h, (rc, mc, fc), sc), sc)
    return x, h

def setup_inputs(seed: int = 0) -> dict:
    key = jax.random.key(seed)
    ks = iter(jax.random.split(key, 40))
    nrm = lambda shape, s: s * jax.random.normal(next(ks), shape, jnp.float32)
    D = D_MODEL
    return {
        "x": nrm((BATCH, SEQ, D), 1.0),
        "c": nrm((BATCH, D), 1.0),
        "ctx": nrm((BATCH, CTX_LEN, D), 1.0),
        "c_ctx": nrm((D,), 1.0),
        "w_mod": nrm((DEPTH, D, N_MOD * D), 0.5 * D ** -0.5),
        "b_mod": nrm((DEPTH, N_MOD * D), 0.01),
        "g_pre_mix": 1.0 + nrm((DEPTH, D), 0.02),
        "g_post_mix": 1.0 + nrm((DEPTH, D), 0.02),
        "g_pre_ffn": 1.0 + nrm((DEPTH, D), 0.02),
        "g_post_ffn": 1.0 + nrm((DEPTH, D), 0.02),
        "w_in": nrm((DEPTH, D, D_IN), D ** -0.5),
        "w_out": nrm((DEPTH, D_MIX, D), D_MIX ** -0.5),
        "conv_rkv": jnp.array([0.25, 1.0, 0.25], jnp.float32)[None, :, None] + nrm((DEPTH, 3, 3 * RWKV_W), 0.05),
        "rwkv_w0": jax.random.uniform(next(ks), (DEPTH, 2, RWKV_W), jnp.float32, -6.0, -1.0),
        "rwkv_w2": nrm((DEPTH, 2, DECAY_LORA, RWKV_W), 0.1 * DECAY_LORA ** -0.5),
        "rwkv_a0": nrm((DEPTH, 2, RWKV_W), 0.5),
        "rwkv_a2": nrm((DEPTH, 2, ICLR_LORA, RWKV_W), 0.5 * ICLR_LORA ** -0.5),
        "rwkv_g2": nrm((DEPTH, GATE_LORA, RWKV_W), GATE_LORA ** -0.5),
        "rwkv_k_k": 1.0 + nrm((DEPTH, RWKV_W), 0.1),
        "rwkv_k_a": 1.0 + nrm((DEPTH, RWKV_W), 0.1),
        "rwkv_r_k": nrm((DEPTH, RWKV_HEADS, HEAD_DIM), 0.1),
        "rwkv_lnx_w": 1.0 + nrm((DEPTH, RWKV_W), 0.02),
        "rwkv_lnx_b": nrm((DEPTH, RWKV_W), 0.01),
        "mla_g_q": 1.0 + nrm((DEPTH, Q_LORA), 0.02),
        "mla_w_qup": nrm((DEPTH, Q_LORA, MLA_HEADS * (MLA_NOPE + MLA_ROPE)), Q_LORA ** -0.5),
        "mla_g_kv": 1.0 + nrm((DEPTH, KV_LORA), 0.02),
        "mla_w_kvup": nrm((DEPTH, KV_LORA, MLA_HEADS * (MLA_NOPE + MLA_V)), KV_LORA ** -0.5),
        "w_fourier": nrm((DEPTH, FOURIER_W, FOURIER_W), FOURIER_W ** -0.5),
        "w_router": nrm((DEPTH, D, N_EXPERTS), D ** -0.5),
        "w_expert_gate": nrm((DEPTH, N_EXPERTS, D, EXPERT_FF), D ** -0.5),
        "w_expert_up": nrm((DEPTH, N_EXPERTS, D, EXPERT_FF), D ** -0.5),
        "w_expert_down": nrm((DEPTH, N_EXPERTS, EXPERT_FF, D), EXPERT_FF ** -0.5),
    }

def reference(x, c, ctx, c_ctx, w_mod, b_mod, g_pre_mix, g_post_mix, g_pre_ffn, g_post_ffn, w_in, w_out,
              conv_rkv, rwkv_w0, rwkv_w2, rwkv_a0, rwkv_a2, rwkv_g2, rwkv_k_k, rwkv_k_a, rwkv_r_k,
              rwkv_lnx_w, rwkv_lnx_b, mla_g_q, mla_w_qup, mla_g_kv, mla_w_kvup, w_fourier,
              w_router, w_expert_gate, w_expert_up, w_expert_down):
    h = ctx
    for l in range(DEPTH):
        p = {
            "w_mod": w_mod[l], "b_mod": b_mod[l],
            "g_pre_mix": g_pre_mix[l], "g_post_mix": g_post_mix[l],
            "g_pre_ffn": g_pre_ffn[l], "g_post_ffn": g_post_ffn[l],
            "w_in": w_in[l], "w_out": w_out[l], "conv_rkv": conv_rkv[l],
            "rwkv_w0": rwkv_w0[l], "rwkv_w2": rwkv_w2[l], "rwkv_a0": rwkv_a0[l], "rwkv_a2": rwkv_a2[l],
            "rwkv_g2": rwkv_g2[l], "rwkv_k_k": rwkv_k_k[l], "rwkv_k_a": rwkv_k_a[l], "rwkv_r_k": rwkv_r_k[l],
            "rwkv_lnx_w": rwkv_lnx_w[l], "rwkv_lnx_b": rwkv_lnx_b[l],
            "mla_g_q": mla_g_q[l], "mla_w_qup": mla_w_qup[l], "mla_g_kv": mla_g_kv[l], "mla_w_kvup": mla_w_kvup[l],
            "w_fourier": w_fourier[l], "w_router": w_router[l],
            "w_expert_gate": w_expert_gate[l], "w_expert_up": w_expert_up[l], "w_expert_down": w_expert_down[l],
        }
        x, h = layer(x, h, c, c_ctx, p, l == DEPTH - 1)
    return x


_drawn_inputs = setup_inputs


def setup_inputs(seed=0):
    import zlib

    import numpy as np

    out = dict(_drawn_inputs(seed))
    spreads = {}
    factors = {'g_post_ffn': 2.864,
     'rwkv_w2': 6.446,
     'rwkv_lnx_b': 6.386,
     'mla_g_q': 5.196,
     'mla_g_kv': 3.848}
    for name, (base, spread) in spreads.items():
        noise = np.random.default_rng([zlib.crc32(name.encode()), seed]).standard_normal(out[name].shape)
        drawn = base * np.exp(spread * noise) if base else spread * noise
        out[name] = __import__('jax').numpy.asarray(drawn.astype(out[name].dtype))
    for name, factor in factors.items():
        out[name] = (out[name] * factor).astype(out[name].dtype)
    return out
```

```python
from contextlib import ExitStack

import concourse.bass as bass
from concourse import mybir

F32 = mybir.dt.float32
ALU = mybir.AluOpType
ACT = mybir.ActivationFunctionType
AX_X = mybir.AxisListType.X

P = 128
D = 1024
KT = D // P
SEQ, CTX = 512, 256
NTOK = SEQ + CTX
NT = NTOK // P
CT_TILES = CTX // P
DEPTH = 2
EPS = 1e-6
HD = 64
HEADS = 6
PAIRS = HEADS // 2
RW = HEADS * HD
GN_EPS = 64e-5
GATE_LORA = 160
MLA_SCALE = 96.0 ** -0.5
NE = 16
FF = 1024
CAP_X = 2 * SEQ // NE
CAP_C = 2 * CTX // NE
SLOTS = CAP_X + CAP_C
DECAY = 0.6065306597126334
CH = 64
NCH = NTOK // CH
NCH_C = CTX // CH
LEVELS = 6

C_RKV, C_LORA, C_GD, C_GD2, C_QD, C_KVD, C_KR, C_F = 0, 9, 10, 11, 12, 14, 15, 16
NCHUNK_IN = 18
MOD_PIECES, IN_PIECES, OUT_PIECES, EX_PIECES = 24, 9, 4, 12
HEAD_PIECES = MOD_PIECES + IN_PIECES + OUT_PIECES
LAYER_PIECES = HEAD_PIECES + NE * EX_PIECES
RING = 6

CONST = {}
_at = 0
for _name, _n in (("ident", P), ("ones", P), ("headones", P), ("tri", 2 * 3 * P), ("upto", P), ("ident2", HD),
                  ("iota", SLOTS), ("level", 2 * LEVELS * P)):
    CONST[_name] = (_at, _at + _n)
    _at += _n
NCONST = _at

VEC = {}
_at = 0
for _name, _n in (("b_mod", 48), ("g_pre_mix", 8), ("g_pre_ffn", 8), ("g_post_mix", 8), ("g_post_ffn", 8),
                  ("conv", 27), ("k_k", 3), ("k_a", 3), ("r_k", 3), ("a0", 6), ("g_q", 2), ("g_kv", 1)):
    VEC[_name] = (_at, _at + _n)
    _at += _n
NVEC = _at

SCR = 15872
PROJ = 4608
S_QD, S_KVD, S_KROPE, S_F = 0, 1536, 2304, 3072
S_TAB = SCR - 1536
TOP8 = 8


def hybrid_layers(nc, x_in, ctx_in, cvec, consts, dft, rope, vecs, w_mod, w_in, w_out, lora, g2w0, lnx, w_q, w_kv,
                  w_f, w_r, w_eg, w_eu, w_ed, out, debug=None):
    with ExitStack() as ctx:
        def sb(name, shape):
            return ctx.enter_context(nc.sbuf_tensor(name, shape, F32))

        sems = {}

        def sem(name):
            if name not in sems:
                sems[name] = ctx.enter_context(nc.semaphore(name))
            return sems[name]

        ring = sb("ring", [P, RING, 2048])
        X = sb("X", [P, NT, D])
        T = sb("T", [P, NT * D])
        U = sb("U", [P, 12, NTOK])
        cst = sb("cst", [P, NCONST])
        vec = sb("vec", [P, NVEC])
        cv = sb("cv", [P, KT, 2])
        modc = sb("modc", [P, 48, 2])
        sc_mix = sb("sc_mix", [P, KT, 2])
        sc_ffn = sb("sc_ffn", [P, KT, 2])
        gt_mix = sb("gt_mix", [P, KT, 2])
        gt_ffn = sb("gt_ffn", [P, KT, 2])
        half_a0 = sb("half_a0", [P, 6])
        ss = sb("ss", [P, 8])
        rstd = sb("rstd", [P, 8])
        scr = sb("scr", [P, SCR])
        psum = ctx.enter_context(nc.psum_tensor("psum", [P, 8, 512], F32))

        def const(name):
            return cst[:, CONST[name][0]:CONST[name][1]]

        def v(name):
            return vec[:, VEC[name][0]:VEC[name][1]]

        ident, ones, headones = const("ident"), const("ones"), const("headones")
        tri = const("tri").rearrange("p (d k n) -> p d k n", d=2, k=3)
        upto, ident2, iota = const("upto"), const("ident2"), const("iota")
        level = const("level").rearrange("p (d j n) -> p d j n", d=2, j=LEVELS)

        def banks(b, n=1):
            return psum[:, b:b + n, :].rearrange("p b n -> p (b n)")

        def area(at, n):
            return scr[:, at:at + n]

        TT = T[:, :].rearrange("p (k n) -> p k n", k=KT)
        YA = T[:, :].rearrange("p (t n) -> p t n", t=NT)
        SEGS = ((0, 512), (512, 256))
        SEQS = ((0, CTX), (CTX, NTOK))
        LIVE = (tuple(range(NT)), tuple(range(CT_TILES, NT)))
        LIVE_SUM = (0, NT, NT + NT - CT_TILES)

        def kind(t):
            return 1 if t < CT_TILES else 0

        phase = {"pe": 0, "act": 0, "dve": 0, "pool": 0}

        def meet(eng, who):
            phase[who] += 1
            eng.drain().then_inc(sem("phase_over"), 1)
            eng.wait_ge(sem("phase_over"), 4 * phase[who])

        def piece_ready(eng, g, loop=0):
            eng.wait_ge(sem(f"ring_loaded{g % RING}"), loop * (16 * EX_PIECES // RING) + 16 * (g // RING + 1))

        def expert_piece(l, j):
            return l * LAYER_PIECES + HEAD_PIECES + j

        QD = area(S_QD, 1536).rearrange("p (c n) -> p c n", c=2)
        KVD = area(S_KVD, 768)
        KROPE = area(S_KROPE, 768)
        F = area(S_F, 1536).rearrange("p (c n) -> p c n", c=2)
        COS, SIN = area(S_TAB, 768), area(S_TAB + 768, 768)
        C512 = area(4608, 2048).rearrange("p (t n) -> p t n", t=4)
        S512 = area(6656, 2048).rearrange("p (t n) -> p t n", t=4)
        C256 = area(8704, 512).rearrange("p (t n) -> p t n", t=2)
        S256 = area(9216, 512).rearrange("p (t n) -> p t n", t=2)
        CS64 = area(9728, 256)
        WF = area(9984, 512).rearrange("p (k n) -> p k n", k=2)
        Y1 = area(10496, 3072).rearrange("p (t n) -> p t n", t=NT)
        FO = T[:, 0:1536].rearrange("p (c n) -> p c n", c=2)
        WQ = area(3072, 1536).rearrange("p (k n) -> p k n", k=2)
        WKV = area(4608, 768)
        QT = [area(5376, 768), area(6144, 768)]
        KTH = [area(6912, 768), area(7680, 768)]
        PR = [area(8448, 768), area(9216, 768)]
        PT = [area(9984, 768).rearrange("p (k n) -> p k n", k=NT), area(10752, 768).rearrange("p (k n) -> p k n", k=NT)]
        OQ = area(11520, 2304).rearrange("p (t n) -> p t n", t=NT)
        smx = area(13824, 48)
        smn = area(13872, 48)
        ssum = area(13920, 48)
        sinv = area(13968, 48)
        VT = T[:, 0:2304].rearrange("p (t n) -> p t n", t=NT)
        R3, K3, V3 = U[:, 0:3, :], U[:, 3:6, :], U[:, 6:9, :]
        LOR = U[:, C_LORA, :]
        GD = U[:, C_GD:C_GD + 2, :]
        Y3 = T[:, 0:2304].rearrange("p (q n) -> p q n", q=PAIRS)
        at = 0

        def take(n):
            nonlocal at
            at += n
            return area(at - n, n)

        W2A2 = take(768).rearrange("p (d n) -> p d n", d=2)
        G2W0 = take(768).rearrange("p (d n) -> p d n", d=2)
        KK = take(2304).rearrange("p (q n) -> p q n", q=PAIRS)
        FM = [take(1536).rearrange("p (q k n) -> p q k n", q=PAIRS, k=4) for _ in range(2)]
        MA = [take(1536).rearrange("p (q k n) -> p q k n", q=PAIRS, k=4) for _ in range(2)]
        XT = [take(384).rearrange("p (q n) -> p q n", q=PAIRS) for _ in range(2)]
        XN = [take(384).rearrange("p (q n) -> p q n", q=PAIRS) for _ in range(2)]
        BKT = [take(768).rearrange("p (k q n) -> p k q n", k=2, q=PAIRS) for _ in range(2)]
        GB = [take(192).rearrange("p (q n) -> p q n", q=PAIRS) for _ in range(2)]
        UB = [take(192).rearrange("p (q n) -> p q n", q=PAIRS) for _ in range(2)]
        ST = [take(192).rearrange("p (q n) -> p q n", q=PAIRS) for _ in range(2)]
        LC = take(64)
        LW = take(384)
        AA = take(192).rearrange("p (q n) -> p q n", q=PAIRS)
        EX = take(384).rearrange("p (q k n) -> p q k n", q=PAIRS, k=2)
        EN = take(192).rearrange("p (q n) -> p q n", q=PAIRS)
        T1 = take(192).rearrange("p (q n) -> p q n", q=PAIRS)
        T2 = take(192).rearrange("p (q n) -> p q n", q=PAIRS)
        assert at <= SCR
        wend = sb("wend", [P, 2, PAIRS])
        bonus = sb("bonus", [P, 2, PAIRS, NCH])
        gstat = sb("gstat", [P, 2, PAIRS * NCH])
        SQ3 = scr[:, 4224:4224 + 2304].rearrange("p (q n) -> p q n", q=PAIRS)
        GT = scr[:, 6528:6528 + 2304].rearrange("p (q n) -> p q n", q=PAIRS)
        LNX = area(8832, 384).rearrange("p (w q n) -> p w q n", w=2, q=PAIRS)
        GBC = [U[:, 8:12, :].rearrange("p a n -> p (a n)")[:, 1024 * s:1024 * s + 1024] for s in range(2)]
        ZN = [area(0, 1024), area(1024, 1024)]
        DG = [area(2048, 1024), area(3072, 1024)]
        XH = U[:, 0:8, :].rearrange("p a n -> p (a n)").rearrange("p (t n) -> p t n", t=NT)
        TNT = area(0, 1024).rearrange("p (k n) -> p k n", k=KT)
        WR = area(4096, 128).rearrange("p (k n) -> p k n", k=KT)
        AFF = area(4224, 96).rearrange("p (t n) -> p t n", t=NT)
        AFT = area(4320, 768)
        WORK = area(5088, 768)
        MASK = area(5856, 768)
        MASKT = area(6624, 96).rearrange("p (t n) -> p t n", t=NT)
        SLOT = area(6720, 96).rearrange("p (t n) -> p t n", t=NT)
        TOP = area(6816, 8)
        rmx, rsm = area(6824, 8), area(6832, 8)
        SLOTE, AFFE = area(6840, 6), area(6848, 6)
        OH = area(6856, 576).rearrange("p (t n) -> p t n", t=NT)
        OV = area(7432, 576).rearrange("p (t n) -> p t n", t=NT)
        OVT = area(8008, 768)
        SCB = area(8776, 768).rearrange("p (k n) -> p k n", k=KT)
        BIB = area(9544, 768).rearrange("p (k n) -> p k n", k=KT)
        XST = area(10312, 768).rearrange("p (k n) -> p k n", k=KT)
        HG = area(11080, 1024)
        HT = area(12104, 768).rearrange("p (k n) -> p k n", k=KT)
        OE = area(12872, 1024)

        block = ctx.enter_context(nc.Block())

        @block.sync
        def _(sp):
            sp.dma_start(cv[:, :, :], cvec).then_inc(sem("c_loaded"), 16)
            sp.dma_start(cst[:, :], consts).then_inc(sem("consts_loaded"), 16)
            for t in range(NT):
                src = ctx_in[t * P:(t + 1) * P, :] if t < CT_TILES else x_in[(t - CT_TILES) * P:(t - CT_TILES + 1) * P, :]
                sp.dma_start(X[:, t, :], src).then_inc(sem("x_loaded"), 16)

            def load(g, src, k, n, loop=0):
                if g >= RING:
                    sp.wait_ge(sem("ring_used"), loop * EX_PIECES + g - RING + 1)
                dst = ring[:, g % RING, 0:k * n].rearrange("p (k n) -> p k n", k=k)
                sp.dma_start(dst, src).then_inc(sem(f"ring_loaded{g % RING}"), 16)

            for l in range(DEPTH):
                g = l * LAYER_PIECES
                for j in range(MOD_PIECES):
                    load(g, w_mod[l].rearrange("(k p) n -> p k n", p=P)[:, :, 256 * j:256 * j + 256], KT, 256)
                    g += 1
                for j in range(IN_PIECES):
                    load(g, w_in[l].rearrange("(k p) n -> p k n", p=P)[:, :, 256 * j:256 * j + 256], KT, 256)
                    g += 1
                for j in range(OUT_PIECES):
                    load(g, w_out[l].rearrange("(k p) n -> p k n", p=P)[:, 2 * j:2 * j + 2, :], 2, D)
                    g += 1
                with sp.Fori(0, NE) as e:
                    for j in range(EX_PIECES):
                        w = (w_eg, w_eu, w_ed)[j // 4]
                        src = w[bass.ds(e + l * NE, 1), :, :].rearrange("e (k p) n -> p (e k) n", p=P)
                        load(g + j, src[:, 2 * (j % 4):2 * (j % 4) + 2, :], 2, D, loop=e)
            for i, t in enumerate(LIVE[1]):
                sp.wait_ge(sem("ffn_out"), LIVE_SUM[1] + i + 1)
                sp.dma_start(out[(t - CT_TILES) * P:(t - CT_TILES + 1) * P, :], X[:, t, :]).then_inc(sem("stored"), 16)
            sp.wait_ge(sem("stored"), 16 * len(LIVE[1]))

        @block.gpsimd
        def _(pool):
            who = "pool"
            for l in range(DEPTH):
                pool.dma_start(vec[:, :], vecs[l]).then_inc(sem("vec_loaded"), 16)
                pool.wait_ge(sem("vec_loaded"), 16 * (l + 1))
                meet(pool, who)
                pool.dma_start(area(S_TAB, 1536), rope).then_inc(sem("rope_loaded"), 16)
                pool.wait_ge(sem("rope_loaded"), 16 * (l + 1))
                meet(pool, who)
                meet(pool, who)
                pool.dma_start(area(4608, 5376), dft).then_inc(sem("dft_loaded"), 16)
                pool.dma_start(WF, w_f[l].rearrange("(k p) n -> p k n", p=P)).then_inc(sem("dft_loaded"), 16)
                pool.wait_ge(sem("dft_loaded"), 32 * (l + 1))
                meet(pool, who)
                pool.dma_start(WQ, w_q[l].rearrange("(k p) n -> p k n", p=P)).then_inc(sem("mlaw_loaded"), 16)
                pool.dma_start(WKV, w_kv[l]).then_inc(sem("mlaw_loaded"), 16)
                pool.wait_ge(sem("mlaw_loaded"), 32 * (l + 1))
                meet(pool, who)
                pool.dma_start(area(0, 768), lora[l]).then_inc(sem("rww_loaded"), 16)
                pool.dma_start(area(768, 768), g2w0[l]).then_inc(sem("rww_loaded"), 16)
                pool.memset(Y3, 0.0)
                pool.wait_ge(sem("rww_loaded"), 32 * (l + 1))
                meet(pool, who)
                meet(pool, who)
                pool.dma_start(area(8832, 384), lnx[l]).then_inc(sem("lnx_loaded"), 16)
                pool.wait_ge(sem("lnx_loaded"), 16 * (l + 1))
                meet(pool, who)
                meet(pool, who)
                pool.dma_start(WR, w_r[l].rearrange("(k p) n -> p k n", p=P)).then_inc(sem("wr_loaded"), 16)
                pool.memset(T[:, :], 0.0)
                pool.wait_ge(sem("wr_loaded"), 16 * (l + 1))
                meet(pool, who)
                tiles = LIVE[l]
                t0, n = tiles[0], len(tiles)
                with pool.Fori(0, NE) as e:
                    pool.wait_ge(sem("onehot_used"), e + l * (NE + 1) + 1)
                    pool.tensor_copy(SLOTE[:, t0:NT], SLOT[:, t0:NT, bass.ds(e, 1)].rearrange("p t o -> p (t o)"))
                    pool.tensor_copy(AFFE[:, t0:NT], AFF[:, t0:NT, bass.ds(e, 1)].rearrange("p t o -> p (t o)"))
                    pool.drain()
                    for t in tiles:
                        pool.tensor_scalar(OH[:, t, :], iota, SLOTE[:, t:t + 1], None, ALU.is_equal)
                        pool.tensor_scalar(OV[:, t, :], iota, SLOTE[:, t:t + 1], AFFE[:, t:t + 1], ALU.is_equal, ALU.mult)
                    pool.drain().then_inc(sem("onehot_ready"), 1)
                meet(pool, who)
                meet(pool, who)

        @block.scalar
        def _(act):
            who = "act"
            for l in range(DEPTH):
                if l == 0:
                    act.wait_ge(sem("c_loaded"), 16)
                    act.activation(cv[:, :, :], cv[:, :, :], ACT.Silu).then_inc(sem("silu_c"), 1)
                    act.wait_ge(sem("x_loaded"), 16 * NT)
                for t in range(NT):
                    act.activation(T[:, t * D:(t + 1) * D], X[:, t, :], ACT.Square, accum_out=ss[:, t:t + 1])\
                       .then_inc(sem("mix_ss"), 1)
                act.wait_ge(sem("mix_ms"), l + 1)
                act.activation(rstd[:, 0:NT], ss[:, 0:NT], ACT.Sqrt).then_inc(sem("mix_std"), 1)
                meet(act, who)

                for t in range(NT):
                    act.wait_ge(sem("mix_turned"), l * NT + t + 1)
                    src = banks(2 * (t % 4), 2).rearrange("p (k n) -> p k n", k=KT)
                    for k in range(KT // 2, KT):
                        ins = act.activation(TT[:, k, t * P:(t + 1) * P], src[:, k, :], ACT.Identity,
                                             bias=modc[:, k, kind(t):kind(t) + 1], scale=sc_mix[:, k, kind(t):kind(t) + 1])
                    ins.then_inc(sem("mix_out_act"), 1)
                meet(act, who)

                for c in range(C_LORA, NCHUNK_IN):
                    if c == C_KR:
                        continue
                    act.wait_ge(sem("in_mm"), l * NCHUNK_IN + c + 1)
                    src = banks(2 * (c % 4), 2)[:, 0:NTOK]
                    if c == C_LORA:
                        act.activation(LOR[0:64, :], src[0:64, :], ACT.Tanh)
                        ins = act.activation(LOR[64:128, :], src[64:128, :], ACT.Copy)
                    elif c == C_GD:
                        ins = act.activation(GD[:, 0, :], src, ACT.Tanh, scale=0.5)
                    elif c == C_GD2:
                        ins = act.activation(GD[0:32, 1, :], src[0:32, :], ACT.Tanh, scale=0.5)
                    elif c < C_KVD:
                        ins = act.activation(QD[:, c - C_QD, :], src, ACT.Copy)
                    elif c == C_KVD:
                        ins = act.activation(KVD, src, ACT.Copy)
                    else:
                        ins = act.activation(F[:, c - C_F, :], src, ACT.Copy)
                    ins.then_inc(sem("in_out_act"), 1)
                meet(act, who)

                for t in range(NT):
                    act.wait_ge(sem("dft64_mm"), l * NT + t + 1)
                    act.activation(Y1[:, t, :], banks(t), ACT.Copy).then_inc(sem("dft64_out"), 1)
                for j in range(2):
                    act.wait_ge(sem("dft_mm"), 2 * l + j + 1)
                    act.activation(FO[:, j, :], banks(2 * j, 2)[:, 0:NTOK], ACT.Copy).then_inc(sem("dft_out"), 1)
                for j in range(2):
                    act.wait_ge(sem("wf_mm"), 2 * l + j + 1)
                    act.activation(TT[:, 6 + j, :], banks(4 + 2 * j, 2)[:, 0:NTOK], ACT.Copy)
                meet(act, who)

                for j in range(2):
                    act.activation(QT[j], QD[:, j, :], ACT.Square)
                act.activation(KTH[0], KVD, ACT.Square).then_inc(sem("lat_sq"), 1)
                act.wait_ge(sem("lat_ms"), l + 1)
                act.activation(PR[0], PR[0], ACT.Sqrt)
                act.activation(PR[1], PR[1], ACT.Sqrt).then_inc(sem("lat_std"), 1)
                for t in range(NT):
                    act.wait_ge(sem("v_mm"), l * NT + t + 1)
                    act.activation(VT[:, t, :], banks(4 + t % 4)[:, 0:RW], ACT.Copy).then_inc(sem("v_out"), 1)
                units = [(h, q) for h in range(HEADS) for q in LIVE[l]]
                U0 = HEADS * LIVE_SUM[l]
                for i, (h, q) in enumerate(units):
                    nk = CTX if q < CT_TILES else NTOK
                    if q == LIVE[l][0]:
                        act.wait_ge(sem("q_mm"), l * HEADS + h + 1)
                        act.activation(QT[h % 2][0:64, :], banks(6, 2)[0:64, 0:NTOK], ACT.Copy).then_inc(sem("q_out_act"), 1)
                        act.wait_ge(sem("k_mm"), l * HEADS + h + 1)
                        act.activation(KTH[h % 2][0:64, :], banks(6, 2)[0:64, 0:NTOK], ACT.Copy).then_inc(sem("k_out_act"), 1)
                    act.wait_ge(sem("smax"), U0 + i + 1)
                    if i >= 2:
                        act.wait_ge(sem("p_turned"), U0 + i - 1)
                    act.activation(PR[i % 2][:, 0:nk], banks(2 * (i % 2), 2)[:, 0:nk], ACT.Exp, bias=smn[:, i:i + 1],
                                   scale=MLA_SCALE, accum_out=ssum[:, i:i + 1]).then_inc(sem("p_ready"), 1)
                    if i >= 1:
                        act.wait_ge(sem("p_turned"), U0 + i)
                        if i >= 3:
                            act.wait_ge(sem("pv_mm"), U0 + i - 2)
                        m = CTX if units[i - 1][1] < CT_TILES else NTOK
                        act.activation(PT[(i - 1) % 2].rearrange("p k n -> p (k n)")[:, 0:m], banks(4, 2)[:, 0:m],
                                       ACT.Copy).then_inc(sem("pt_ready"), 1)
                i = len(units)
                act.wait_ge(sem("p_turned"), U0 + i)
                act.wait_ge(sem("pv_mm"), U0 + i - 2)
                act.activation(PT[(i - 1) % 2].rearrange("p k n -> p (k n)"), banks(4, 2)[:, 0:NTOK], ACT.Copy)\
                   .then_inc(sem("pt_ready"), 1)
                for i, q in enumerate(LIVE[l]):
                    act.wait_ge(sem("o_turned"), LIVE_SUM[l] + i + 1)
                    act.activation(TT[:, 3:6, q * P:(q + 1) * P], banks(i)[:, 0:RW].rearrange("p (j n) -> p j n", j=3),
                                   ACT.Copy)
                meet(act, who)

                for p in range(PAIRS):
                    act.wait_ge(sem("kk_raw"), l * PAIRS + p + 1)
                    act.activation(SQ3[:, p, :], KK[:, p, :], ACT.Square).then_inc(sem("kk_sq"), 1)
                for p in range(PAIRS):
                    act.wait_ge(sem("kk_ss"), l * PAIRS + p + 1)
                    act.activation(GT[:, p, :], banks(2 * p, 2)[:, 0:NTOK], ACT.Sqrt).then_inc(sem("kk_norm"), 1)
                meet(act, who)

                def scan_step(n, chunk):
                    def k(d):
                        return n * 2 + (2 * NCH * l + d + 1)

                    for d in range(2):
                        c = chunk[d]
                        act.wait_ge(sem("lc_used"), k(d))
                        act.activation(LC, LOR[:, bass.ds(c * CH, CH)], ACT.Copy).then_inc(sem("lc_ready"), 1)
                        act.wait_ge(sem("gates_mm"), k(d))
                        act.activation(LW[0:64, :], psum[0:64, 6 + d, 0:RW], ACT.Tanh, scale=0.5)
                        for p in range(PAIRS):
                            ins = act.activation(AA[:, p, :], psum[:, 3 * d, p * CH:(p + 1) * CH], ACT.Tanh, scale=0.5,
                                                 bias=half_a0[:, 3 * d + p:3 * d + p + 1])
                        ins.then_inc(sem("gates_tanh"), 1)
                        act.wait_ge(sem("cum_mm"), k(d))
                        cum = psum[:, 6 + d, 0:384].rearrange("p (q k n) -> p q k n", q=PAIRS, k=2)
                        act.activation(EX, cum, ACT.Exp, scale=-DECAY)
                        act.activation(EN, cum[:, :, 1, :], ACT.Exp, scale=DECAY).then_inc(sem("decays_ready"), 1)
                    for d in range(2):
                        act.wait_ge(sem("bk_turned"), k(d))
                        act.activation(BKT[d].rearrange("p k q n -> p (k q n)"), banks(3 * d, 2)[:, 0:768], ACT.Copy)
                        act.activation(bonus[:, d, :, bass.ds(chunk[d], 1)], psum[:, 3 * d + 2, 0:PAIRS].unsqueeze(2), ACT.Copy)\
                           .then_inc(sem("bkt_ready"), 1)
                    for d in range(2):
                        act.wait_ge(sem("g_mm"), k(d))
                        act.activation(GB[d].rearrange("p q n -> p (q n)"), psum[:, 6 + d, 0:192], ACT.Copy)\
                           .then_inc(sem("g_ready"), 1)
                    for d in range(2):
                        act.wait_ge(sem("u_mm"), k(d))
                        act.activation(UB[d].rearrange("p q n -> p (q n)"), psum[:, 6 + d, 192:384], ACT.Copy)\
                           .then_inc(sem("u_ready"), 1)

                with act.Fori(0, NCH_C) as n:
                    scan_step(n, (n, n * -1 + (NCH_C - 1)))
                with act.Fori(NCH_C, NCH) as n:
                    scan_step(n, (n, n * -1 + (NCH_C + NCH - 1)))
                meet(act, who)

                act.wait_ge(sem("y_centred"), l + 1)
                for p in range(PAIRS):
                    ins = act.activation(SQ3[:, p, :], Y3[:, p, :], ACT.Square)
                ins.then_inc(sem("y_sq"), 1)
                act.wait_ge(sem("y_var"), l + 1)
                act.activation(gstat[:, 1, :], gstat[:, 1, :], ACT.Sqrt).then_inc(sem("y_std"), 1)
                for p in range(PAIRS):
                    act.wait_ge(sem("gate_mm"), l * PAIRS + p + 1)
                    act.activation(GT[:, p, :], banks(2 * p, 2)[:, 0:NTOK], ACT.Copy).then_inc(sem("gate_out"), 1)
                meet(act, who)

                for s in range(2 - l):
                    act.wait_ge(sem("gate_bc_mm"), (0, 4)[l] + s + 1)
                    act.activation(GBC[s], banks(4 + 2 * s, 2), ACT.Copy).then_inc(sem("gate_bc"), 1)
                for i, t in enumerate(LIVE[l]):
                    N = LIVE_SUM[l] + i + 1
                    act.wait_ge(sem("out_mm"), N)
                    act.activation(DG[0], banks(2 * (i % 2), 2), ACT.Square, accum_out=ss[:, t:t + 1]).then_inc(sem("out_ss"), 1)
                    act.wait_ge(sem("out_ms"), N)
                    act.activation(rstd[:, t:t + 1], ss[:, t:t + 1], ACT.Sqrt).then_inc(sem("out_std"), 1)
                meet(act, who)

                for i, t in enumerate(LIVE[l]):
                    act.activation(XH[:, t, :], X[:, t, :], ACT.Square, accum_out=ss[:, t:t + 1]).then_inc(sem("ffn_ss"), 1)
                act.wait_ge(sem("ffn_ms"), l + 1)
                act.activation(rstd[:, 0:NT], ss[:, 0:NT], ACT.Sqrt).then_inc(sem("ffn_std"), 1)
                for i, t in enumerate(LIVE[l]):
                    N = LIVE_SUM[l] + i + 1
                    act.wait_ge(sem("ffn_turned"), N)
                    if i >= 1:
                        act.wait_ge(sem("router_mm"), N - 1)
                    src = banks(0, 2).rearrange("p (k n) -> p k n", k=KT)
                    for k in range(KT):
                        ins = act.activation(TNT[:, k, :], src[:, k, :], ACT.Identity,
                                             bias=modc[:, 24 + k, kind(t):kind(t) + 1],
                                             scale=sc_ffn[:, k, kind(t):kind(t) + 1])
                    ins.then_inc(sem("tnt_ready"), 1)
                    act.wait_ge(sem("router_max"), N)
                    act.activation(AFF[:, t, :], banks(2)[:, 0:NE], ACT.Exp, bias=rmx[:, t:t + 1],
                                   accum_out=rsm[:, t:t + 1]).then_inc(sem("router_exp"), 1)
                for s in range(2 - l):
                    act.wait_ge(sem("gate_bc_mm"), (2, 5)[l] + s + 1)
                    act.activation(GBC[s], banks(4 + 2 * s, 2), ACT.Copy).then_inc(sem("gate_bc"), 1)
                meet(act, who)

                with act.Fori(0, NE) as e:
                    k = e + l * NE + 1
                    act.wait_ge(sem("ovt_mm"), k)
                    act.activation(OVT[0:SLOTS, :], banks(6, 2)[0:SLOTS, 0:NTOK], ACT.Copy).then_inc(sem("ovt_ready"), 1)
                    for h in range(2):
                        act.wait_ge(sem("gate_up_mm"), k)
                        ins = act.activation(HG[0:SLOTS, 512 * h:512 * h + 512], banks(2 + h)[0:SLOTS, :], ACT.Silu)
                        ins.then_inc(sem("silu_ready"), 1)
                    act.wait_ge(sem("down_mm"), k)
                    act.activation(OE[0:SLOTS, :], banks(2, 2)[0:SLOTS, :], ACT.Copy).then_inc(sem("oe_ready"), 1)
                meet(act, who)

                for i, t in enumerate(LIVE[l]):
                    act.activation(XH[:, t, :], YA[:, t, :], ACT.Square, accum_out=ss[:, t:t + 1]).then_inc(sem("y_ss"), 1)
                act.wait_ge(sem("y_ms"), l + 1)
                act.activation(rstd[:, 0:NT], ss[:, 0:NT], ACT.Sqrt).then_inc(sem("ys_std"), 1)
                meet(act, who)

        @block.vector
        def _(dve):
            who = "dve"

            def mean_square(width, want, got, n0=0):
                dve.tensor_scalar(ss[:, n0:NT], ss[:, n0:NT], 1.0 / width, EPS, ALU.mult, ALU.add).then_inc(sem(want), 1)

            for l in range(DEPTH):
                dve.wait_ge(sem("mix_ss"), NT * (l + 1))
                mean_square(D, "mix_ms", None)
                dve.wait_ge(sem("mix_std"), l + 1)
                dve.reciprocal(rstd[:, 0:NT], rstd[:, 0:NT])
                dve.wait_ge(sem("vec_loaded"), 16 * (l + 1))
                dve.wait_ge(sem("mod_mm"), l + 1)
                dve.tensor_tensor(modc[:, :, :], banks(0)[:, 0:96].rearrange("p (m s) -> p m s", s=2),
                                  v("b_mod").unsqueeze(2).to_broadcast([P, 48, 2]), ALU.add)
                dve.tensor_scalar(half_a0[:, :], v("a0"), 0.5, None, ALU.mult)
                dve.drain()
                for dst, m, add, g in ((sc_mix, 1, 1.0, "g_pre_mix"), (gt_mix, 2, 0.0, "g_post_mix"),
                                       (sc_ffn, 4, 1.0, "g_pre_ffn"), (gt_ffn, 5, 0.0, "g_post_ffn")):
                    dve.scalar_tensor_tensor(out=dst[:, :, :], in0=modc[:, 8 * m:8 * m + 8, :], scalar=add,
                                             in1=v(g).unsqueeze(2).to_broadcast([P, KT, 2]), op0=ALU.add, op1=ALU.mult)
                meet(dve, who)

                def normed(t):
                    if t >= 2:
                        dve.wait_ge(sem("mix_turned"), l * NT + t - 1)
                    dve.tensor_scalar(ZN[t % 2], X[:, t, :], rstd[:, t:t + 1], None, ALU.mult).then_inc(sem("mix_normed"), 1)

                normed(0)
                for t in range(NT):
                    if t + 1 < NT:
                        normed(t + 1)
                    dve.wait_ge(sem("mix_turned"), l * NT + t + 1)
                    src = banks(2 * (t % 4), 2).rearrange("p (k n) -> p k n", k=KT)
                    for k in range(KT // 2):
                        ins = dve.tensor_scalar(TT[:, k, t * P:(t + 1) * P], src[:, k, :], sc_mix[:, k, kind(t):kind(t) + 1],
                                                modc[:, k, kind(t):kind(t) + 1], ALU.mult, ALU.add)
                    ins.then_inc(sem("mix_out_dve"), 1)
                meet(dve, who)

                for c in range(NCHUNK_IN):
                    src = banks(2 * (c % 4), 2)[:, 0:NTOK]
                    if c < C_LORA:
                        dve.wait_ge(sem("in_mm"), l * NCHUNK_IN + c + 1)
                        tap = [v("conv")[:, 9 * j + c:9 * j + c + 1] for j in range(3)]
                        dve.tensor_scalar(U[:, c, :], src, tap[1], None, ALU.mult)
                        dve.drain()
                        for a, b in SEQS:
                            dve.scalar_tensor_tensor(out=U[:, c, a + 1:b], in0=src[:, a:b - 1], scalar=tap[0],
                                                     in1=U[:, c, a + 1:b], op0=ALU.mult, op1=ALU.add)
                        dve.drain()
                        for a, b in SEQS:
                            ins = dve.scalar_tensor_tensor(out=U[:, c, a:b - 1], in0=src[:, a + 1:b], scalar=tap[2],
                                                           in1=U[:, c, a:b - 1], op0=ALU.mult, op1=ALU.add)
                        ins.then_inc(sem("in_out_dve"), 1)
                    elif c == C_GD2:
                        dve.wait_ge(sem("in_mm"), l * NCHUNK_IN + c + 1)
                        dve.wait_ge(sem("in_out_act"), l * 8 + 3)
                        dve.tensor_tensor(area(PROJ, 768)[64:96, :], src[64:96, :], SIN[64:96, :], ALU.mult)
                        dve.tensor_scalar(GD[:, 0, :], GD[:, 0, :], 0.5, 0.5, ALU.mult, ALU.add)
                        dve.tensor_scalar(GD[0:32, 1, :], GD[0:32, 1, :], 0.5, 0.5, ALU.mult, ALU.add)\
                           .then_inc(sem("in_out_dve"), 1)
                    elif c == C_KR:
                        dve.wait_ge(sem("in_mm"), l * NCHUNK_IN + c + 1)
                        dve.tensor_tensor(KROPE[64:96, :], src[64:96, :], COS[64:96, :], ALU.mult)
                        dve.drain()
                        dve.tensor_tensor(KROPE[64:96, :], KROPE[64:96, :], area(PROJ, 768)[64:96, :], ALU.add)\
                           .then_inc(sem("in_out_dve"), 1)
                meet(dve, who)

                meet(dve, who)

                for j, w in ((0, 256), (1, 128)):
                    dve.wait_ge(sem("lat_ss"), 2 * l + j + 1)
                    ins = dve.tensor_scalar(PR[j], banks(2 * j, 2)[:, 0:NTOK], 1.0 / w, EPS, ALU.mult, ALU.add)
                ins.then_inc(sem("lat_ms"), 1)
                dve.wait_ge(sem("lat_std"), l + 1)
                dve.reciprocal(PR[0], PR[0])
                dve.reciprocal(PR[1], PR[1])
                dve.drain()
                dve.scalar_tensor_tensor(out=KVD, in0=KVD, scalar=v("g_kv"), in1=PR[1], op0=ALU.mult, op1=ALU.mult)
                for j in range(2):
                    dve.scalar_tensor_tensor(out=QD[:, j, :], in0=QD[:, j, :], scalar=v("g_q")[:, j:j + 1], in1=PR[0],
                                             op0=ALU.mult, op1=ALU.mult)
                dve.drain().then_inc(sem("lat_normed"), 1)
                for j in range(2):
                    dve.tensor_copy(KTH[j][64:96, :], KROPE[64:96, :])
                units = [(h, q) for h in range(HEADS) for q in LIVE[l]]
                U0 = HEADS * LIVE_SUM[l]

                def finish(i):
                    h, q = units[i]
                    dve.reciprocal(sinv[:, i:i + 1], ssum[:, i:i + 1])
                    dve.drain()
                    dve.wait_ge(sem("pv_mm"), U0 + i + 1)
                    dve.tensor_scalar(OQ[:, q, h * HD:(h + 1) * HD], banks(7)[:, 256:320],
                                      sinv[:, i:i + 1], None, ALU.mult).then_inc(sem("o_ready"), 1)

                for i, (h, q) in enumerate(units):
                    nk = CTX if q < CT_TILES else NTOK
                    if q == LIVE[l][0]:
                        dve.wait_ge(sem("q_mm"), l * HEADS + h + 1)
                        dve.tensor_tensor(QT[h % 2][64:96, :], banks(6, 2)[64:96, 0:NTOK], COS[64:96, :], ALU.mult)\
                           .then_inc(sem("q_cos"), 1)
                        dve.wait_ge(sem("q_sw_mm"), l * HEADS + h + 1)
                        dve.tensor_tensor(KROPE[64:96, :], banks(6, 2)[64:96, 0:NTOK], SIN[64:96, :], ALU.mult)\
                           .then_inc(sem("q_sin"), 1)
                        dve.drain()
                        dve.tensor_tensor(QT[h % 2][64:96, :], QT[h % 2][64:96, :], KROPE[64:96, :], ALU.add)\
                           .then_inc(sem("q_out_dve"), 1)
                    dve.wait_ge(sem("s_mm"), U0 + i + 1)
                    dve.reduce_max(smx[:, i:i + 1], banks(2 * (i % 2), 2)[:, 0:nk], AX_X)
                    dve.drain()
                    dve.tensor_scalar(smn[:, i:i + 1], smx[:, i:i + 1], -MLA_SCALE, None, ALU.mult).then_inc(sem("smax"), 1)
                    if i >= 2:
                        finish(i - 2)
                dve.wait_ge(sem("p_ready"), U0 + len(units))
                finish(len(units) - 2)
                finish(len(units) - 1)
                meet(dve, who)

                for p in range(PAIRS):
                    dve.tensor_scalar(KK[:, p, :], K3[:, p, :], v("k_k")[:, p:p + 1], None, ALU.mult).then_inc(sem("kk_raw"), 1)
                for p in range(PAIRS):
                    dve.wait_ge(sem("kk_norm"), l * PAIRS + p + 1)
                    dve.tensor_scalar(GT[:, p, :], GT[:, p, :], 1e-12, None, ALU.max)
                dve.drain()
                for p in range(PAIRS):
                    dve.reciprocal(GT[:, p, :], GT[:, p, :])
                dve.drain()
                for p in range(PAIRS):
                    dve.tensor_tensor(KK[:, p, :], KK[:, p, :], GT[:, p, :], ALU.mult)
                for p in range(PAIRS):
                    dve.wait_ge(sem("vst_mm"), l * PAIRS + p + 1)
                    dve.tensor_copy(V3[:, p, :], banks(6 if p == 0 else 2 * (p - 1), 2)[:, 0:NTOK])\
                       .then_inc(sem("vst_out"), 1)
                dve.drain()
                for d in range(2):
                    dve.memset(FM[d], 0.0)
                    dve.memset(ST[d], 0.0)
                    dve.memset(MA[d], 0.0)
                meet(dve, who)

                def scan_step(n, chunk):
                    def k(d):
                        return n * 2 + (2 * NCH * l + d + 1)

                    for d in range(2):
                        tok = bass.ds(chunk[d] * CH, CH)
                        fm = FM[d]
                        dve.wait_ge(sem("gates_tanh"), k(d))
                        dve.tensor_scalar(LW[0:64, :], LW[0:64, :], 0.5, 0.5, ALU.mult, ALU.add).then_inc(sem("lw_ready"), 1)
                        dve.tensor_scalar(AA, AA, 0.5, 0.5, ALU.mult, ALU.add)
                        dve.drain()
                        for p in range(PAIRS):
                            dve.tensor_scalar(T1[:, p, :], AA[:, p, :], 1.0, v("k_a")[:, p:p + 1], ALU.subtract, ALU.mult)
                        dve.tensor_tensor(T2, AA, KK[:, :, tok], ALU.mult)
                        dve.drain()
                        dve.scalar_tensor_tensor(out=T1, in0=T1, scalar=1.0, in1=K3[:, :, tok], op0=ALU.add, op1=ALU.mult)
                        dve.drain()
                        dve.wait_ge(sem("decays_ready"), k(d))
                        for h in range(2):
                            part, cols = slice(64 * h, 64 * h + 64), slice(64 * h, 64 * h + 64)
                            dve.scalar_tensor_tensor(out=fm[part, :, 0, cols], in0=KK[part, :, tok], scalar=-1.0,
                                                     in1=EX[part, :, 0, :], op0=ALU.mult, op1=ALU.mult)
                            dve.tensor_tensor(fm[part, :, 1, cols], EX[part, :, 1, :], R3[part, :, tok], ALU.mult)
                            dve.tensor_tensor(fm[part, :, 2, cols], T2[part], EN[part], ALU.mult)
                            dve.tensor_tensor(fm[part, :, 3, cols], T1[part], EN[part], ALU.mult)
                        end = (CH - 1, 0)[d]
                        dve.tensor_copy(wend[:, d, :], EX[:, :, 1, end:end + 1].rearrange("p q o -> p (q o)"))
                        dve.drain().then_inc(sem("fm_ready"), 1)
                        dve.tensor_tensor(BKT[d][:, 1], fm[:, :, 1, :], fm[:, :, 3, :], ALU.mult).then_inc(sem("prd_ready"), 1)
                    for d in range(2):
                        dve.wait_ge(sem("a_mm"), k(d))
                        pa = psum[:, 3 * d:3 * d + 3, :]
                        pq = psum[:, 6 + d, 0:384].rearrange("p (q n) -> p q n", q=PAIRS)
                        dve.tensor_tensor(MA[d][:, :, 1:4, :], pa[:, :, 128:512].rearrange("p q (k n) -> p q k n", k=3),
                                          tri[:, d].unsqueeze(1).to_broadcast([P, PAIRS, 3, P]), ALU.mult)
                        dve.tensor_tensor(XT[d], pa[:, :, 0:128], level[:, d, 0].unsqueeze(1).to_broadcast([P, PAIRS, P]), ALU.mult)
                        dve.tensor_tensor(XN[d], pq, level[:, 1 - d, 0].unsqueeze(1).to_broadcast([P, PAIRS, P]), ALU.mult)
                        dve.tensor_tensor(MA[d][:, :, 0, :], pq, tri[:, 1 - d, 1].unsqueeze(1).to_broadcast([P, PAIRS, P]), ALU.mult)
                        dve.drain()
                        dve.tensor_tensor(XT[d], XT[d], ident.unsqueeze(1).to_broadcast([P, PAIRS, P]), ALU.add)
                        dve.tensor_tensor(XN[d], XN[d], ident.unsqueeze(1).to_broadcast([P, PAIRS, P]), ALU.add)
                        dve.drain().then_inc(sem("masked"), 1)
                    for j in range(1, LEVELS):
                        kj = [n * (2 * (LEVELS - 1)) + (2 * NCH * l * (LEVELS - 1) + 2 * (j - 1) + d + 1) for d in range(2)]
                        for d in range(2):
                            dve.wait_ge(sem("m_mm"), kj[d])
                            dve.tensor_tensor(FM[d][:, :, 2, :], psum[:, 6 + d, 0:384].rearrange("p (q n) -> p q n", q=PAIRS),
                                              level[:, d, j].unsqueeze(1).to_broadcast([P, PAIRS, P]), ALU.mult)\
                               .then_inc(sem("m_ready"), 1)
                        for d in range(2):
                            dve.wait_ge(sem("x_mm"), kj[d])
                            if j < LEVELS - 1:
                                dve.tensor_tensor(XN[d], XN[d], psum[:, 3 * d, 0:384].rearrange("p (q n) -> p q n", q=PAIRS), ALU.add)
                            dve.tensor_tensor(XT[d], XT[d], psum[:, 3 * d + 2, 0:384].rearrange("p (q n) -> p q n", q=PAIRS), ALU.add)\
                               .then_inc(sem("x_ready"), 1)
                    for d in range(2):
                        dve.wait_ge(sem("scan_mm"), k(d))
                        dve.tensor_tensor(GB[d], ST[d], psum[:, 3 * d + 1, 192:384].rearrange("p (q n) -> p q n", q=PAIRS), ALU.add)
                        y = Y3[:, :, bass.ds(chunk[d] * CH, CH)]
                        dve.tensor_tensor(y, y, psum[:, 3 * d + 1, 0:192].rearrange("p (q n) -> p q n", q=PAIRS), ALU.add)
                        dve.drain()
                        dve.tensor_tensor(ST[d], GB[d], wend[:, d, :].unsqueeze(2).to_broadcast([P, PAIRS, HD]), ALU.mult)\
                           .then_inc(sem("state_ready"), 1)

                with dve.Fori(0, NCH_C) as n:
                    scan_step(n, (n, n * -1 + (NCH_C - 1)))
                with dve.Fori(NCH_C, NCH) as n:
                    scan_step(n, (n, n * -1 + (NCH_C + NCH - 1)))
                meet(dve, who)

                y4 = Y3.rearrange("p q (c n) -> p q c n", n=HD)
                s4 = SQ3.rearrange("p q (c n) -> p q c n", n=HD)
                v4 = V3.rearrange("p q (c n) -> p q c n", n=HD)
                st = [gstat[:, i, :].rearrange("p (q c) -> p q c", q=PAIRS) for i in range(2)]
                dve.tensor_reduce(st[0], y4, AX_X, ALU.add)
                dve.tensor_tensor(bonus[:, 0], bonus[:, 0], bonus[:, 1], ALU.add)
                dve.drain()
                dve.tensor_scalar(st[0], st[0], 1.0 / HD, None, ALU.mult)
                dve.drain()
                dve.tensor_tensor(y4, y4, st[0].unsqueeze(3).to_broadcast([P, PAIRS, NCH, HD]), ALU.subtract)\
                   .then_inc(sem("y_centred"), 1)
                dve.wait_ge(sem("y_sq"), l + 1)
                dve.tensor_reduce(st[1], s4, AX_X, ALU.add)
                dve.drain()
                dve.tensor_scalar(st[1], st[1], 1.0 / HD, GN_EPS, ALU.mult, ALU.add).then_inc(sem("y_var"), 1)
                dve.tensor_tensor(s4, v4, bonus[:, 0].unsqueeze(3).to_broadcast([P, PAIRS, NCH, HD]), ALU.mult)
                dve.wait_ge(sem("y_std"), l + 1)
                dve.reciprocal(gstat[:, 1, :], gstat[:, 1, :])
                dve.drain()
                dve.tensor_tensor(y4, y4, st[1].unsqueeze(3).to_broadcast([P, PAIRS, NCH, HD]), ALU.mult)
                dve.drain()
                dve.wait_ge(sem("lnx_loaded"), 16 * (l + 1))
                dve.tensor_tensor(y4, y4, LNX[:, 0].unsqueeze(2).to_broadcast([P, PAIRS, NCH, HD]), ALU.mult)
                dve.drain()
                dve.tensor_tensor(y4, y4, LNX[:, 1].unsqueeze(2).to_broadcast([P, PAIRS, NCH, HD]), ALU.add)
                dve.drain()
                dve.tensor_tensor(y4, y4, s4, ALU.add).then_inc(sem("y_done"), 1)
                for p in range(PAIRS):
                    dve.wait_ge(sem("gate_out"), l * PAIRS + p + 1)
                    dve.wait_ge(sem("y_turned"), l * PAIRS + p + 1)
                    b = 6 if p == 0 else 2 * (p - 1)
                    dve.tensor_tensor(Y3[:, p, :], banks(b, 2)[:, 0:NTOK], GT[:, p, :], ALU.mult)
                meet(dve, who)

                def gate_diagonals(gt, base):
                    for s in range(2 - l):
                        for k in range(KT):
                            ins = dve.tensor_scalar(DG[s][:, k * P:(k + 1) * P], ident, gt[:, k, s:s + 1], None, ALU.mult)
                        ins.then_inc(sem("gate_diag"), 1)

                gate_diagonals(gt_mix, 0)
                dve.wait_ge(sem("gate_bc"), (2, 5)[l])
                for i, t in enumerate(LIVE[l]):
                    N = LIVE_SUM[l] + i + 1
                    dve.wait_ge(sem("out_ss"), N)
                    dve.tensor_scalar(ss[:, t:t + 1], ss[:, t:t + 1], 1.0 / D, EPS, ALU.mult, ALU.add).then_inc(sem("out_ms"), 1)
                    dve.wait_ge(sem("out_std"), N)
                    dve.reciprocal(rstd[:, t:t + 1], rstd[:, t:t + 1])
                    dve.drain()
                    dve.scalar_tensor_tensor(out=ZN[0], in0=banks(2 * (i % 2), 2), scalar=rstd[:, t:t + 1], in1=GBC[kind(t)],
                                             op0=ALU.mult, op1=ALU.mult).then_inc(sem("out_out"), 1)
                    dve.drain()
                    dve.tensor_tensor(X[:, t, :], X[:, t, :], ZN[0], ALU.add)
                meet(dve, who)

                dve.wait_ge(sem("ffn_ss"), LIVE_SUM[l + 1])
                dve.tensor_scalar(ss[:, 0:NT], ss[:, 0:NT], 1.0 / D, EPS, ALU.mult, ALU.add).then_inc(sem("ffn_ms"), 1)
                dve.wait_ge(sem("ffn_std"), l + 1)
                dve.reciprocal(rstd[:, 0:NT], rstd[:, 0:NT])
                dve.drain()
                gate_diagonals(gt_ffn, 0)
                for i, t in enumerate(LIVE[l]):
                    dve.tensor_scalar(XH[:, t, :], X[:, t, :], rstd[:, t:t + 1], None, ALU.mult).then_inc(sem("xh_ready"), 1)
                dve.wait_ge(sem("wr_loaded"), 16 * (l + 1))
                for i, t in enumerate(LIVE[l]):
                    N = LIVE_SUM[l] + i + 1
                    dve.wait_ge(sem("router_mm"), N)
                    dve.reduce_max(rmx[:, t:t + 1], banks(2)[:, 0:NE], AX_X)
                    dve.drain()
                    dve.tensor_scalar(rmx[:, t:t + 1], rmx[:, t:t + 1], -1.0, None, ALU.mult).then_inc(sem("router_max"), 1)
                    dve.wait_ge(sem("router_exp"), N)
                    dve.reciprocal(rsm[:, t:t + 1], rsm[:, t:t + 1])
                    dve.drain()
                    dve.tensor_scalar(AFF[:, t, :], AFF[:, t, :], rsm[:, t:t + 1], None, ALU.mult).then_inc(sem("aff_ready"), 1)
                t0 = LIVE[l][0]
                dve.wait_ge(sem("aff_turned"), l + 1)
                dve.tensor_copy(AFT[0:NE, t0 * P:NTOK], banks(2, 2)[0:NE, t0 * P:NTOK])
                dve.drain()
                for a, b, cap in (() if l else ((0, CTX, CAP_C),)) + ((CTX, NTOK, CAP_X),):
                    src = AFT
                    for r in range(cap // TOP8):
                        dve.max(TOP[0:NE, :], src[0:NE, a:b])
                        dve.drain()
                        dve.match_replace(out=WORK[0:NE, a:b], in_to_replace=TOP[0:NE, :], in_values=src[0:NE, a:b], imm_value=-1.0)
                        dve.drain()
                        src = WORK
                dve.tensor_scalar(MASK[0:NE, t0 * P:NTOK], WORK[0:NE, t0 * P:NTOK], 0.0, None, ALU.is_lt)\
                   .then_inc(sem("mask_ready"), 1)
                dve.wait_ge(sem("mask_turned"), l + 1)
                dve.tensor_copy(MASKT[:, t0:NT, :], banks(0)[:, NE * t0:NE * NT].rearrange("p (t n) -> p t n", n=NE))\
                   .then_inc(sem("maskt_ready"), 1)
                dve.wait_ge(sem("count_mm"), l + 1)
                for t in LIVE[l]:
                    dve.scalar_tensor_tensor(out=SLOT[:, t, :], in0=banks(1)[:, NE * t:NE * t + NE],
                                             scalar=float(CAP_X * kind(t)), in1=MASKT[:, t, :], op0=ALU.add, op1=ALU.mult)
                dve.drain()
                dve.tensor_scalar(SLOT[:, t0:NT, :], SLOT[:, t0:NT, :], 1.0, None, ALU.subtract)
                for s, a, b in ((0, 0, CAP_X), (1, CAP_X, SLOTS)):
                    dve.tensor_copy(SCB[:, :, a:b], sc_ffn[:, :, s:s + 1].to_broadcast([P, KT, b - a]))
                    dve.tensor_copy(BIB[:, :, a:b], modc[:, 24:32, s:s + 1].to_broadcast([P, KT, b - a]))
                meet(dve, who)

                live = LIVE[l]
                with dve.Fori(0, NE) as e:
                    k = e + l * NE + 1
                    dve.wait_ge(sem("gather_mm"), k)
                    src = psum[:, 0:2, 0:4 * SLOTS].rearrange("p b (k n) -> p b k n", k=4)
                    dst = XST.rearrange("p (b k) n -> p b k n", b=2)
                    for b in range(2):
                        dve.tensor_tensor(dst[:, b], src[:, b], SCB[:, 4 * b:4 * b + 4, :], ALU.mult)
                    dve.drain()
                    dve.tensor_tensor(XST, XST, BIB, ALU.add).then_inc(sem("xst_ready"), 1)
                    for h in range(2):
                        dve.wait_ge(sem("silu_ready"), e * 2 + (2 * NE * l + h + 1))
                        hg = HG[0:SLOTS, 512 * h:512 * h + 512]
                        dve.tensor_tensor(hg, hg, banks(4 + h)[0:SLOTS, :], ALU.mult).then_inc(sem("hidden_ready"), 1)
                    dve.wait_ge(sem("ht_mm"), k)
                    for b in range(2):
                        ins = dve.tensor_copy(HT.rearrange("p (b k) n -> p b k n", b=2)[:, b], src[:, b])
                    ins.then_inc(sem("ht_ready"), 1)
                    for i, t in enumerate(live):
                        for h in range(2):
                            m = 2 * i + h
                            dve.wait_ge(sem("scatter_mm"), e * (2 * len(live)) + (2 * NE * LIVE_SUM[l] + m + 1))
                            ya = YA[:, t, 512 * h:512 * h + 512]
                            dve.tensor_tensor(ya, ya, banks(4 + m % 2), ALU.add).then_inc(sem("scatter_out"), 1)
                meet(dve, who)

                dve.wait_ge(sem("y_ss"), LIVE_SUM[l + 1])
                dve.tensor_scalar(ss[:, 0:NT], ss[:, 0:NT], 1.0 / D, EPS, ALU.mult, ALU.add).then_inc(sem("y_ms"), 1)
                dve.wait_ge(sem("ys_std"), l + 1)
                dve.reciprocal(rstd[:, 0:NT], rstd[:, 0:NT])
                dve.drain()
                for i, t in enumerate(live):
                    dve.scalar_tensor_tensor(out=YA[:, t, :], in0=YA[:, t, :], scalar=rstd[:, t:t + 1], in1=GBC[kind(t)],
                                             op0=ALU.mult, op1=ALU.mult)
                dve.drain()
                for i, t in enumerate(live):
                    dve.tensor_tensor(X[:, t, :], X[:, t, :], YA[:, t, :], ALU.add).then_inc(sem("ffn_out"), 1)
                meet(dve, who)

        @block.tensor
        def _(pe):
            who = "pe"

            def mm(dst, lhsT, rhs, start=True, stop=True):
                return pe.matmul(dst, lhsT, rhs, start=start, stop=stop)

            pe.wait_ge(sem("consts_loaded"), 16)
            pe.wait_ge(sem("silu_c"), 1)
            for l in range(DEPTH):
                g = l * LAYER_PIECES
                for j in range(MOD_PIECES):
                    piece_ready(pe, g)
                    w = ring[:, g % RING, :].rearrange("p (k n) -> p k n", k=KT)
                    for m in range(2):
                        at = 2 * (2 * j + m)
                        for k in range(KT):
                            ins = mm(banks(0)[:, at:at + 2], w[:, k, m * P:(m + 1) * P], cv[:, k, :], k == 0, k == KT - 1)
                    ins.then_inc(sem("ring_used"), 1)
                    g += 1
                pe.drain().then_inc(sem("mod_mm"), 1)
                meet(pe, who)

                for t in range(NT):
                    pe.wait_ge(sem("mix_normed"), l * NT + t + 1)
                    if t >= 4:
                        pe.wait_ge(sem("mix_out_act"), l * NT + t - 3)
                        pe.wait_ge(sem("mix_out_dve"), l * NT + t - 3)
                    dst = banks(2 * (t % 4), 2).rearrange("p (k n) -> p k n", k=KT)
                    for k in range(KT):
                        ins = pe.transpose(dst[:, k, :], ZN[t % 2][:, k * P:(k + 1) * P], ident)
                    ins.then_inc(sem("mix_turned"), 1)
                meet(pe, who)

                dve_chunks = [c for c in range(NCHUNK_IN) if c < C_LORA or c in (C_GD2, C_KR)]
                act_chunks = [c for c in range(C_LORA, NCHUNK_IN) if c != C_KR]
                for c in range(NCHUNK_IN):
                    if c % 2 == 0:
                        piece_ready(pe, g)
                    if c >= 4:
                        if c - 4 in dve_chunks:
                            pe.wait_ge(sem("in_out_dve"), l * len(dve_chunks) + dve_chunks.index(c - 4) + 1)
                        if c - 4 in act_chunks:
                            pe.wait_ge(sem("in_out_act"), l * len(act_chunks) + act_chunks.index(c - 4) + 1)
                    w = ring[:, g % RING, :].rearrange("p (k n) -> p k n", k=KT)[:, :, (c % 2) * P:(c % 2 + 1) * P]
                    for a, n in SEGS:
                        for k in range(KT):
                            ins = mm(banks(2 * (c % 4), 2)[:, a:a + n], w[:, k, :], TT[:, k, a:a + n], k == 0, k == KT - 1)
                    ins.then_inc(sem("in_mm"), 1)
                    if c % 2:
                        pe.drain().then_inc(sem("ring_used"), 1)
                        g += 1
                meet(pe, who)

                pe.wait_ge(sem("dft_loaded"), 32 * (l + 1))
                for t in range(NT):
                    dst = banks(t).rearrange("p (w q n) -> p w q n", w=2, q=2)
                    for q in range(2):
                        ins = mm(dst[:, :, q, :], F[:, q, t * P:(t + 1) * P], CS64.rearrange("p (w n) -> p w n", w=2))
                    ins.then_inc(sem("dft64_mm"), 1)
                pe.wait_ge(sem("dft64_out"), NT * (l + 1))
                for j in range(2):
                    dst = banks(2 * j, 2)
                    for a, b, c0, t_0, tabs in ((0, CTX, 0, 0, (C256, S256)), (CTX, 2 * CTX, 0, CT_TILES, (C512, S512)),
                                                (2 * CTX, 3 * CTX, CTX, CT_TILES, (C512, S512))):
                        nt = CT_TILES if t_0 == 0 else NT - CT_TILES
                        for w, tab in enumerate(tabs):
                            for t in range(nt):
                                ins = mm(dst[:, a:b], Y1[:, t_0 + t, 256 * w + j * P:256 * w + (j + 1) * P],
                                         tab[:, t, c0:c0 + CTX], w == 0 and t == 0, w == 1 and t == nt - 1)
                    ins.then_inc(sem("dft_mm"), 1)
                pe.wait_ge(sem("dft_out"), 2 * l + 2)
                for j in range(2):
                    for a, n in SEGS:
                        for k in range(2):
                            ins = mm(banks(4 + 2 * j, 2)[:, a:a + n], WF[:, k, j * P:(j + 1) * P], FO[:, k, a:a + n], k == 0, k == 1)
                    ins.then_inc(sem("wf_mm"), 1)
                meet(pe, who)

                pe.wait_ge(sem("mlaw_loaded"), 32 * (l + 1))
                pe.wait_ge(sem("lat_sq"), l + 1)
                for j, parts in ((0, QT), (1, KTH[:1])):
                    for a, n in SEGS:
                        for k, part in enumerate(parts):
                            ins = mm(banks(2 * j, 2)[:, a:a + n], ones, part[:, a:a + n], k == 0, k == len(parts) - 1)
                    ins.then_inc(sem("lat_ss"), 1)
                pe.wait_ge(sem("lat_normed"), l + 1)
                for t in range(NT):
                    if t >= 4:
                        pe.wait_ge(sem("v_out"), l * NT + t - 3)
                    mm(banks(4 + t % 4)[:, 0:RW], KVD[:, t * P:(t + 1) * P], WKV[:, RW:2 * RW]).then_inc(sem("v_mm"), 1)
                pe.wait_ge(sem("v_out"), l * NT + NT)
                units = [(h, q) for h in range(HEADS) for q in LIVE[l]]
                U0 = HEADS * LIVE_SUM[l]
                H0 = l * HEADS

                def project(h):
                    if h >= 1:
                        pe.wait_ge(sem("k_out_act"), H0 + h)
                    for a, n in SEGS:
                        for k in range(2):
                            ins = mm(banks(6, 2)[0:96, a:a + n], WQ[:, k, h * 96:(h + 1) * 96], QD[:, k, a:a + n], k == 0, k == 1)
                    ins.then_inc(sem("q_mm"), 1)
                    pe.wait_ge(sem("q_out_act"), H0 + h + 1)
                    pe.wait_ge(sem("q_cos"), H0 + h + 1)
                    for a, n in SEGS:
                        for k in range(2):
                            ins = mm(banks(6, 2)[64:96, a:a + n], WQ[:, k, 576 + h * 32:576 + (h + 1) * 32], QD[:, k, a:a + n],
                                     k == 0, k == 1)
                    ins.then_inc(sem("q_sw_mm"), 1)
                    for a, n in SEGS:
                        ins = mm(banks(6, 2)[0:64, a:a + n], WKV[:, h * HD:(h + 1) * HD], KVD[:, a:a + n])
                    ins.then_inc(sem("k_mm"), 1)
                    pe.wait_ge(sem("q_sin"), H0 + h + 1)

                def turn(i):
                    nk = (CTX if units[i][1] < CT_TILES else NTOK) // P
                    pe.wait_ge(sem("p_ready"), U0 + i + 1)
                    if i >= 1:
                        pe.wait_ge(sem("pt_ready"), U0 + i)
                    for k in range(nk):
                        ins = pe.transpose(banks(4, 2)[:, k * P:(k + 1) * P], PR[i % 2][:, k * P:(k + 1) * P], ident)
                    ins.then_inc(sem("p_turned"), 1)

                def values(i):
                    h, q = units[i]
                    nk = (CTX if q < CT_TILES else NTOK) // P
                    pe.wait_ge(sem("pt_ready"), U0 + i + 1)
                    if i >= 1:
                        pe.wait_ge(sem("o_ready"), U0 + i)
                    for k in range(nk):
                        ins = mm(banks(7)[:, 256:320], PT[i % 2][:, k, :],
                                 VT[:, k, h * HD:(h + 1) * HD], k == 0, k == nk - 1)
                    ins.then_inc(sem("pv_mm"), 1)

                for i, (h, q) in enumerate(units):
                    if q == LIVE[l][0]:
                        if i >= 3:
                            pe.wait_ge(sem("o_ready"), U0 + i - 2)
                        project(h)
                        pe.wait_ge(sem("q_out_dve"), H0 + h + 1)
                        pe.wait_ge(sem("k_out_act"), H0 + h + 1)
                    if i >= 2:
                        pe.wait_ge(sem("p_ready"), U0 + i - 1)
                    for a, n in (((0, CTX),) if q < CT_TILES else SEGS):
                        ins = mm(banks(2 * (i % 2), 2)[:, a:a + n], QT[h % 2][0:96, q * P:(q + 1) * P], KTH[h % 2][0:96, a:a + n])
                    ins.then_inc(sem("s_mm"), 1)
                    if i >= 1:
                        turn(i - 1)
                    if i >= 2:
                        values(i - 2)
                n = len(units)
                turn(n - 1)
                values(n - 2)
                values(n - 1)
                pe.wait_ge(sem("o_ready"), U0 + n)
                for i, q in enumerate(LIVE[l]):
                    for j in range(3):
                        ins = pe.transpose(banks(i)[:, j * P:(j + 1) * P], OQ[:, q, j * P:(j + 1) * P], ident)
                    ins.then_inc(sem("o_turned"), 1)
                meet(pe, who)

                for p in range(PAIRS):
                    pe.wait_ge(sem("kk_sq"), l * PAIRS + p + 1)
                    for a, n in SEGS:
                        ins = mm(banks(2 * p, 2)[:, a:a + n], headones, SQ3[:, p, a:a + n])
                    ins.then_inc(sem("kk_ss"), 1)
                for p in range(PAIRS):
                    b = 6 if p == 0 else 2 * (p - 1)
                    if p:
                        pe.wait_ge(sem("kk_norm"), l * PAIRS + p)
                    for c in range(NCH):
                        for h in range(2):
                            rows = slice(64 * h, 64 * h + 64)
                            ins = mm(banks(b, 2)[rows, c * CH:(c + 1) * CH], V3[rows, p, c * CH:(c + 1) * CH], ident2[rows, :])
                    ins.then_inc(sem("vst_mm"), 1)
                pe.nop().then_inc(sem("lc_used"), 1) if l == 0 else None
                meet(pe, who)

                def scan_step(n, chunk):
                    def k(d):
                        return n * 2 + (2 * NCH * l + d + 1)

                    for d in range(2):
                        pe.wait_ge(sem("lc_ready"), k(d))
                        for p in range(PAIRS):
                            mm(psum[:, 3 * d, p * CH:(p + 1) * CH], W2A2[64:128, d, p * P:(p + 1) * P], LC[64:128, :])
                        mm(psum[0:64, 6 + d, 0:RW], LC[0:64, :], W2A2[0:64, d, :], True, False)
                        row = 32 + 32 * d
                        ins = mm(psum[0:64, 6 + d, 0:RW], ones[row:row + 1, 0:64], G2W0[row:row + 1, 1, :], False, True)
                        ins.then_inc(sem("gates_mm"), 1)
                        pe.drain().then_inc(sem("lc_used"), 1)
                        pe.wait_ge(sem("lw_ready"), k(d))
                        for p in range(PAIRS):
                            ins = mm(psum[:, 6 + d, 128 * p:128 * p + 128].rearrange("p (k n) -> p k n", k=2),
                                     LW[0:64, p * P:(p + 1) * P], tri[0:64, d, 1:3, 0:64])
                        ins.then_inc(sem("cum_mm"), 1)
                        pe.wait_ge(sem("fm_ready"), k(d))
                        for p in range(PAIRS):
                            ar = FM[d][:, p, 0:2, :].rearrange("p k n -> p (k n)")
                            mm(psum[:, 3 * d + p, 0:256], FM[d][:, p, 2, :], ar)
                            mm(psum[:, 3 * d + p, 256:512], FM[d][:, p, 3, :], ar)
                            ins = mm(psum[:, 6 + d, p * P:(p + 1) * P], FM[d][:, p, 0, :], FM[d][:, p, 2, :])
                        ins.then_inc(sem("a_mm"), 1)
                    for d in range(2):
                        pe.wait_ge(sem("masked"), k(d))
                        pe.wait_ge(sem("prd_ready"), k(d))
                        for w in range(2):
                            for p in range(PAIRS):
                                i = 3 * w + p
                                pe.transpose(psum[:, 3 * d + i // 4, (i % 4) * P:(i % 4 + 1) * P], FM[d][:, p, 2 + w, :], ident)
                        for p in range(PAIRS):
                            ins = mm(psum[:, 3 * d + 2, p:p + 1], BKT[d][:, 1, p, :], v("r_k")[:, p:p + 1])
                        ins.then_inc(sem("bk_turned"), 1)
                    for j in range(1, LEVELS):
                        kj = [n * (2 * (LEVELS - 1)) + (2 * NCH * l * (LEVELS - 1) + 2 * (j - 1) + d + 1) for d in range(2)]
                        for d in range(2):
                            if j > 1:
                                pe.wait_ge(sem("x_ready"), kj[d] - 2)
                            for p in range(PAIRS):
                                ins = mm(psum[:, 6 + d, p * P:(p + 1) * P], MA[d][:, p, 0, :], XT[d][:, p, :])
                            ins.then_inc(sem("m_mm"), 1)
                        for d in range(2):
                            pe.wait_ge(sem("m_ready"), kj[d])
                            if j == 1:
                                pe.wait_ge(sem("bkt_ready"), k(d))
                            for p in range(PAIRS):
                                if j < LEVELS - 1:
                                    mm(psum[:, 3 * d, p * P:(p + 1) * P], FM[d][:, p, 2, :], XN[d][:, p, :])
                                ins = mm(psum[:, 3 * d + 2, p * P:(p + 1) * P], XN[d][:, p, :], FM[d][:, p, 2, :])
                            ins.then_inc(sem("x_mm"), 1)
                    for d in range(2):
                        tok = bass.ds(chunk[d] * CH, CH)
                        pe.wait_ge(sem("x_ready"), kj[d])
                        for p in range(PAIRS):
                            mm(psum[:, 6 + d, p * HD:(p + 1) * HD], FM[d][:, p, 0, :], ST[d][:, p, :], True, False)
                            ins = mm(psum[:, 6 + d, p * HD:(p + 1) * HD], MA[d][:, p, 2, :], V3[:, p, tok], False, True)
                        ins.then_inc(sem("g_mm"), 1)
                    for d in range(2):
                        pe.wait_ge(sem("g_ready"), k(d))
                        for p in range(PAIRS):
                            ins = mm(psum[:, 6 + d, 192 + p * HD:192 + (p + 1) * HD], XT[d][:, p, :], GB[d][:, p, :])
                        ins.then_inc(sem("u_mm"), 1)
                    for d in range(2):
                        tok = bass.ds(chunk[d] * CH, CH)
                        pe.wait_ge(sem("u_ready"), k(d))
                        for p in range(PAIRS):
                            y = psum[:, 3 * d + 1, p * HD:(p + 1) * HD]
                            mm(y, FM[d][:, p, 1, :], ST[d][:, p, :], True, False)
                            mm(y, MA[d][:, p, 1, :], UB[d][:, p, :], False, False)
                            mm(y, MA[d][:, p, 3, :], V3[:, p, tok], False, True)
                            s = psum[:, 3 * d + 1, 192 + p * HD:192 + (p + 1) * HD]
                            mm(s, BKT[d][:, 0, p, :], UB[d][:, p, :], True, False)
                            ins = mm(s, BKT[d][:, 1, p, :], V3[:, p, tok], False, True)
                        ins.then_inc(sem("scan_mm"), 1)
                    for d in range(2):
                        pe.wait_ge(sem("state_ready"), k(d))

                with pe.Fori(0, NCH_C) as n:
                    scan_step(n, (n, n * -1 + (NCH_C - 1)))
                with pe.Fori(NCH_C, NCH) as n:
                    scan_step(n, (n, n * -1 + (NCH_C + NCH - 1)))
                meet(pe, who)

                for p in range(PAIRS):
                    for a, n in SEGS:
                        mm(banks(2 * p, 2)[:, a:a + n], G2W0[:, 0, p * P:(p + 1) * P], GD[:, 0, a:a + n], True, False)
                        ins = mm(banks(2 * p, 2)[:, a:a + n], G2W0[0:32, 1, p * P:(p + 1) * P], GD[0:32, 1, a:a + n], False, True)
                    ins.then_inc(sem("gate_mm"), 1)
                pe.wait_ge(sem("y_done"), l + 1)
                for p in range(PAIRS):
                    b = 6 if p == 0 else 2 * (p - 1)
                    if p:
                        pe.wait_ge(sem("gate_out"), l * PAIRS + p)
                    for c in range(NCH):
                        for h in range(2):
                            rows = slice(64 * h, 64 * h + 64)
                            ins = mm(banks(b, 2)[rows, c * CH:(c + 1) * CH], Y3[rows, p, c * CH:(c + 1) * CH], ident2[rows, :])
                    ins.then_inc(sem("y_turned"), 1)
                meet(pe, who)

                def gate_on_all(base):
                    for s in range(2 - l):
                        pe.wait_ge(sem("gate_diag"), base + s + 1)
                        for k in range(KT):
                            ins = mm(banks(4 + 2 * s, 2)[:, k * P:(k + 1) * P], ones, DG[s][:, k * P:(k + 1) * P])
                        ins.then_inc(sem("gate_bc_mm"), 1)

                gate_on_all((0, 4)[l])
                for j in range(OUT_PIECES):
                    piece_ready(pe, g + j)
                for i, t in enumerate(LIVE[l]):
                    if i >= 2:
                        pe.wait_ge(sem("out_out"), LIVE_SUM[l] + i - 1)
                    for h in range(2):
                        for k in range(KT):
                            w = ring[:, (g + k // 2) % RING, :].rearrange("p (k n) -> p k n", k=2)
                            ins = mm(banks(2 * (i % 2) + h), TT[:, k, t * P:(t + 1) * P], w[:, k % 2, 512 * h:512 * h + 512],
                                     k == 0, k == KT - 1)
                    ins.then_inc(sem("out_mm"), 1)
                for j in range(OUT_PIECES):
                    pe.drain().then_inc(sem("ring_used"), 1)
                g += OUT_PIECES
                meet(pe, who)

                gate_on_all((2, 5)[l])
                for i, t in enumerate(LIVE[l]):
                    N = LIVE_SUM[l] + i + 1
                    pe.wait_ge(sem("xh_ready"), N)
                    if i >= 1:
                        pe.wait_ge(sem("tnt_ready"), N - 1)
                    for k in range(KT):
                        ins = pe.transpose(banks(0, 2)[:, k * P:(k + 1) * P], XH[:, t, k * P:(k + 1) * P], ident)
                    ins.then_inc(sem("ffn_turned"), 1)
                    pe.wait_ge(sem("tnt_ready"), N)
                    pe.wait_ge(sem("wr_loaded"), 16 * (l + 1))
                    if i >= 1:
                        pe.wait_ge(sem("router_exp"), N - 1)
                    for k in range(KT):
                        ins = mm(banks(2)[:, 0:NE], TNT[:, k, :], WR[:, k, :], k == 0, k == KT - 1)
                    ins.then_inc(sem("router_mm"), 1)
                pe.wait_ge(sem("aff_ready"), LIVE_SUM[l + 1])
                for t in LIVE[l]:
                    ins = pe.transpose(banks(2, 2)[0:NE, t * P:(t + 1) * P], AFF[:, t, :], ident)
                ins.then_inc(sem("aff_turned"), 1)
                pe.wait_ge(sem("mask_ready"), l + 1)
                for t in LIVE[l]:
                    ins = pe.transpose(banks(0)[:, NE * t:NE * t + NE], MASK[0:NE, t * P:(t + 1) * P], ident[0:NE, 0:NE])
                ins.then_inc(sem("mask_turned"), 1)
                pe.wait_ge(sem("maskt_ready"), l + 1)
                for t in LIVE[l]:
                    first = 0 if t < CT_TILES else CT_TILES
                    for u in range(first, t + 1):
                        ins = mm(banks(1)[:, NE * t:NE * t + NE], upto if u == t else ones, MASKT[:, u, :], u == first, u == t)
                ins.then_inc(sem("count_mm"), 1)
                pe.nop().then_inc(sem("onehot_used"), 1)
                meet(pe, who)

                live = LIVE[l]
                with pe.Fori(0, NE) as e:
                    k1 = e + l * NE + 1
                    pe.wait_ge(sem("onehot_ready"), k1)
                    for k in range(KT):
                        dst = psum[:, k // 4, (k % 4) * SLOTS:(k % 4 + 1) * SLOTS]
                        for t in live:
                            ins = mm(dst, XH[:, t, k * P:(k + 1) * P], OH[:, t, :], t == live[0], t == live[-1])
                    ins.then_inc(sem("gather_mm"), 1)
                    for t in live:
                        ins = pe.transpose(banks(6, 2)[0:SLOTS, t * P:(t + 1) * P], OV[:, t, :], ident)
                    ins.then_inc(sem("ovt_mm"), 1)
                    pe.drain().then_inc(sem("onehot_used"), 1)
                    pe.wait_ge(sem("xst_ready"), k1)
                    for j in range(8):
                        gj = g + j
                        piece_ready(pe, gj, loop=e)
                        w = ring[:, gj % RING, :].rearrange("p (k n) -> p k n", k=2)
                        for kk in range(2):
                            k = 2 * (j % 4) + kk
                            for h in range(2):
                                ins = mm(banks(2 + 2 * (j // 4) + h)[0:SLOTS, :], XST[:, k, :], w[:, kk, 512 * h:512 * h + 512],
                                         k == 0, k == KT - 1)
                        ins.then_inc(sem("ring_used"), 1)
                    pe.drain().then_inc(sem("gate_up_mm"), 1)
                    for h in range(2):
                        pe.wait_ge(sem("hidden_ready"), e * 2 + (2 * NE * l + h + 1))
                        for k in range(4 * h, 4 * h + 4):
                            ins = pe.transpose(psum[:, k // 4, (k % 4) * SLOTS:(k % 4 + 1) * SLOTS],
                                               HG[0:SLOTS, k * P:(k + 1) * P], ident[0:SLOTS, 0:SLOTS])
                    ins.then_inc(sem("ht_mm"), 1)
                    pe.wait_ge(sem("ht_ready"), k1)
                    for j in range(8, 12):
                        gj = g + j
                        piece_ready(pe, gj, loop=e)
                        w = ring[:, gj % RING, :].rearrange("p (k n) -> p k n", k=2)
                        for kk in range(2):
                            k = 2 * (j % 4) + kk
                            for h in range(2):
                                ins = mm(banks(2 + h)[0:SLOTS, :], HT[:, k, :], w[:, kk, 512 * h:512 * h + 512], k == 0, k == KT - 1)
                        ins.then_inc(sem("ring_used"), 1)
                    pe.drain().then_inc(sem("down_mm"), 1)
                    pe.wait_ge(sem("oe_ready"), k1)
                    pe.wait_ge(sem("ovt_ready"), k1)
                    for i, t in enumerate(live):
                        for h in range(2):
                            m = 2 * i + h
                            if m >= 2:
                                pe.wait_ge(sem("scatter_out"), e * (2 * len(live)) + (2 * NE * LIVE_SUM[l] + m - 1))
                            mm(banks(4 + m % 2), OVT[0:SLOTS, t * P:(t + 1) * P], OE[0:SLOTS, 512 * h:512 * h + 512])\
                                .then_inc(sem("scatter_mm"), 1)
                    pe.wait_ge(sem("scatter_out"), e * (2 * len(live)) + (2 * NE * LIVE_SUM[l] + 2 * len(live)))
                meet(pe, who)
                meet(pe, who)


def shape_constants(np):
    i = np.arange(P)
    same = (i[:, None] // 64) == (i[None, :] // 64)
    before = [same & (i[:, None] < i[None, :]), same & (i[:, None] > i[None, :])]
    tri = [np.stack([b | np.eye(P, dtype=bool), b, b | np.eye(P, dtype=bool)]) for b in before]
    lev = []
    for b in before:
        for j in range(LEVELS):
            m = 2 ** j
            lev.append(b & (i[:, None] // (2 * m) == i[None, :] // (2 * m)) & (i[:, None] // m != i[None, :] // m))
    cols = [np.eye(P), np.ones((P, P)), same, np.concatenate([t.transpose(1, 0, 2).reshape(P, -1) for t in tri], 1),
            i[:, None] <= i[None, :], np.tile(np.eye(64), (2, 1)), np.tile(np.arange(SLOTS), (P, 1)),
            np.stack(lev).transpose(1, 0, 2).reshape(P, -1)]
    consts = np.concatenate([np.asarray(c, np.float32) for c in cols], 1)
    assert consts.shape == (P, NCONST)

    def dft(n, scale):
        a = 2 * np.pi * (np.outer(np.arange(n), np.arange(n)) % n) / n
        return np.cos(a) * scale, np.sin(a) * scale

    def tiles(a):
        return a.reshape(-1, P, a.shape[1]).transpose(1, 0, 2).reshape(P, -1)

    c5, s5 = dft(SEQ, (SEQ * 64) ** -0.5)
    c2, s2 = dft(CTX, (CTX * 64) ** -0.5)
    c6, s6 = dft(64, 1.0)
    two = np.zeros((P, 2, P))
    for h in range(2):
        two[64 * h:64 * h + 64, 0, 64 * h:64 * h + 64] = c6
        two[64 * h:64 * h + 64, 1, 64 * h:64 * h + 64] = s6
    tables = np.concatenate([tiles(c5), tiles(-s5), tiles(c2), tiles(-s2), two.reshape(P, -1)], 1).astype(np.float32)

    inv = (np.float32(10000.0) ** (-np.arange(8, dtype=np.float32) / np.float32(8))).astype(np.float32)
    pos = np.arange(SEQ)
    rope = np.zeros((P, 2, NTOK), np.float32)
    rope[64:96, 0, :CTX] = 1.0
    for half, q in enumerate((pos // 64, pos % 64)):
        ang = (q.astype(np.float32)[None, :] * inv[:, None]).astype(np.float32)
        for part in range(2):
            r = 64 + 16 * half + 8 * part
            rope[r:r + 8, 0, CTX:] = np.cos(ang)
            rope[r:r + 8, 1, CTX:] = np.sin(ang) * (1 if part else -1)
    return consts, tables, rope.reshape(P, -1)


def kernel(**inputs):
    import numpy as np
    import concourse.bacc as bacc
    from concourse.bass_utils import run_bass_kernel_spmd as run

    a = {k: np.asarray(x) for k, x in inputs.items()}
    consts, tables, rope = shape_constants(np)

    def cols(x):
        return x.reshape(DEPTH, -1, P).transpose(0, 2, 1)

    cvec = np.stack([a["c"].reshape(KT, P).T, a["c_ctx"].reshape(KT, P).T], 2)
    vecs = np.concatenate([
        cols(a["b_mod"]), cols(a["g_pre_mix"]), cols(a["g_pre_ffn"]), cols(a["g_post_mix"]), cols(a["g_post_ffn"]),
        cols(a["conv_rkv"]), cols(a["rwkv_k_k"]), cols(a["rwkv_k_a"]), cols(a["rwkv_r_k"].reshape(DEPTH, -1)),
        cols(a["rwkv_a0"]), cols(a["mla_g_q"]), cols(a["mla_g_kv"])], 2)
    swap = np.concatenate([np.arange(8, 16), np.arange(0, 8), np.arange(24, 32), np.arange(16, 24)])
    w = a["w_in"]
    o_gd, o_q, o_kr, o_f = 3 * RW + 128, 3 * RW + 128 + GATE_LORA, 3 * RW + 128 + GATE_LORA + 384, 3 * RW + 128 + GATE_LORA + 416
    z = lambda n: np.zeros((DEPTH, D, n), np.float32)
    kr = w[:, :, o_kr:o_kr + 32]
    w_in = np.concatenate([w[:, :, 0:o_gd + GATE_LORA], z(32), kr[:, :, swap], z(32),
                           w[:, :, o_q:o_kr], z(64), kr, z(32), w[:, :, o_f:]], 2)
    assert w_in.shape[2] == NCHUNK_IN * P
    lora = np.concatenate([a["rwkv_w2"], a["rwkv_a2"]], 2).transpose(0, 2, 1, 3).reshape(DEPTH, P, 768)
    g2w0 = np.zeros((DEPTH, P, 2, RW), np.float32)
    g2w0[:, :, 0] = a["rwkv_g2"][:, :P]
    g2w0[:, 0:32, 1] = a["rwkv_g2"][:, P:]
    g2w0[:, 32, 1] = a["rwkv_w0"][:, 0]
    g2w0[:, 64, 1] = a["rwkv_w0"][:, 1]
    ln = np.stack([a["rwkv_lnx_w"], a["rwkv_lnx_b"]], 1).reshape(DEPTH, 2, PAIRS, 2, HD)
    lnx = np.repeat(ln.transpose(0, 3, 1, 2, 4).reshape(DEPTH, 2, -1), 64, axis=1)
    q6 = a["mla_w_qup"].reshape(DEPTH, 256, HEADS, 96)
    w_q = np.concatenate([a["mla_w_qup"], q6[:, :, :, 64:][:, :, :, swap].reshape(DEPTH, 256, 192)], 2)
    kv6 = a["mla_w_kvup"].reshape(DEPTH, P, HEADS, 2, HD)
    w_kv = kv6.transpose(0, 1, 3, 2, 4).reshape(DEPTH, P, 768)
    arrays = {
        "x_in": a["x"][0], "ctx_in": a["ctx"][0], "cvec": cvec, "consts": consts, "dft": tables, "rope": rope, "vecs": vecs,
        "w_mod": a["w_mod"], "w_in": w_in, "w_out": a["w_out"], "lora": lora, "g2w0": g2w0.reshape(DEPTH, P, -1),
        "lnx": lnx, "w_q": w_q, "w_kv": w_kv, "w_f": a["w_fourier"], "w_r": a["w_router"],
        "w_eg": a["w_expert_gate"].reshape(DEPTH * NE, D, FF), "w_eu": a["w_expert_up"].reshape(DEPTH * NE, D, FF),
        "w_ed": a["w_expert_down"].reshape(DEPTH * NE, FF, D),
    }
    nc = bacc.Bacc("TRN2", target_bir_lowering=False, num_devices=1)
    args, sent = [], {}
    for name, x in arrays.items():
        sent[f"{name}_dram"] = np.ascontiguousarray(x)
        args.append(nc.dram_tensor(f"{name}_dram", x.shape, F32, kind="ExternalInput").ap())
    out = nc.dram_tensor("out_dram", (SEQ, D), F32, kind="ExternalOutput").ap()
    hybrid_layers(nc, *args, out)
    r = run(nc, [sent], core_ids=[0])
    return r.results[0]["out_dram"].reshape(1, SEQ, D)
```

```python
from contextlib import ExitStack

import concourse.bass as bass
from concourse import mybir

F32 = mybir.dt.float32
BF16 = mybir.dt.bfloat16
ALU = mybir.AluOpType
ACT = mybir.ActivationFunctionType
AX_X = mybir.AxisListType.X

P = 128
D = 1024
KT = D // P
SEQ, CTX = 512, 256
NTOK = SEQ + CTX
NT = NTOK // P
CT_TILES = CTX // P
DEPTH = 2
EPS = 1e-6
HD = 64
HEADS = 6
PAIRS = HEADS // 2
RW = HEADS * HD
GN_EPS = 64e-5
GATE_LORA = 160
MLA_SCALE = 96.0 ** -0.5
NE = 16
FF = 1024
CAP_X = 2 * SEQ // NE
CAP_C = 2 * CTX // NE
SLOTS = CAP_X + CAP_C
DECAY = 0.6065306597126334
CH = 64
NCH = NTOK // CH
NCH_C = CTX // CH
LEVELS = 6

C_RKV, C_LORA, C_GD, C_GD2, C_QD, C_KVD, C_KR, C_F = 0, 9, 10, 11, 12, 14, 15, 16
NCHUNK_IN = 18
MOD_PIECES, IN_PIECES, OUT_PIECES, EX_PIECES = 24, 9, 4, 12
HEAD_PIECES = MOD_PIECES + IN_PIECES + OUT_PIECES
LAYER_PIECES = HEAD_PIECES + NE * EX_PIECES
RING = 4
GROUP = 4
GROUPS = NE // GROUP
GROUP_PIECES = GROUP * EX_PIECES

CONST = {}
_at = 0
for _name, _n in (("ident", P), ("ones", P), ("headones", P), ("tri", 2 * 3 * P), ("upto", P), ("ident2", HD),
                  ("iota", CAP_X), ("level", 2 * LEVELS * P), ("fold", 2)):
    CONST[_name] = (_at, _at + _n)
    _at += _n
NCONST = _at

VEC = {}
_at = 0
for _name, _n in (("b_mod", 48), ("g_pre_mix", 8), ("g_pre_ffn", 8), ("g_post_mix", 8), ("g_post_ffn", 8),
                  ("conv", 27), ("k_k", 3), ("k_a", 3), ("r_k", 3), ("a0", 6), ("g_q", 2), ("g_kv", 1)):
    VEC[_name] = (_at, _at + _n)
    _at += _n
NVEC = _at

SCR = 19900
PROJ = 4608
S_QD, S_KVD, S_KROPE, S_F = 0, 1536, 2304, 3072
S_TAB = SCR - 1536
TOP8 = 8


def hybrid_layers(nc, x_in, ctx_in, cvec, consts, dft, rope, vecs, w_mod, w_in, w_out, lora, g2w0, lnx, w_q, w_kv,
                  w_f, w_r, w_eg, w_eu, w_ed, out, debug=None):
    with ExitStack() as ctx:
        def sb(name, shape):
            return ctx.enter_context(nc.sbuf_tensor(name, shape, F32))

        sems = {}

        def sem(name):
            if name not in sems:
                sems[name] = ctx.enter_context(nc.semaphore(name))
            return sems[name]

        ring = sb("ring", [P, RING, 2048])
        X = sb("X", [P, NT, D])
        T = sb("T", [P, NT * D])
        U = sb("U", [P, 12, NTOK])
        cst = sb("cst", [P, NCONST])
        vec = sb("vec", [P, NVEC])
        cv = sb("cv", [P, KT, 2])
        cv_halves = ctx.enter_context(nc.sbuf_tensor("cv_halves", [P, KT, 4], BF16))
        modc = sb("modc", [P, 48, 2])
        sc_mix = sb("sc_mix", [P, KT, 2])
        sc_ffn = sb("sc_ffn", [P, KT, 2])
        gt_mix = sb("gt_mix", [P, KT, 2])
        gt_ffn = sb("gt_ffn", [P, KT, 2])
        half_a0 = sb("half_a0", [P, 6])
        ss = sb("ss", [P, 8])
        rstd = sb("rstd", [P, 8])
        scr = sb("scr", [P, SCR])
        psum = ctx.enter_context(nc.psum_tensor("psum", [P, 8, 512], F32))

        def const(name):
            return cst[:, CONST[name][0]:CONST[name][1]]

        def v(name):
            return vec[:, VEC[name][0]:VEC[name][1]]

        ident, ones, headones = const("ident"), const("ones"), const("headones")
        tri = const("tri").rearrange("p (d k n) -> p d k n", d=2, k=3)
        upto, ident2, iota, fold = const("upto"), const("ident2"), const("iota"), const("fold")
        level = const("level").rearrange("p (d j n) -> p d j n", d=2, j=LEVELS)

        def banks(b, n=1):
            return psum[:, b:b + n, :].rearrange("p b n -> p (b n)")

        def area(at, n):
            return scr[:, at:at + n]

        TT = T[:, :].rearrange("p (k n) -> p k n", k=KT)
        YA = T[:, :].rearrange("p (t n) -> p t n", t=NT)
        SEGS = ((0, 512), (512, 256))
        SEQS = ((0, CTX), (CTX, NTOK))
        LIVE = (tuple(range(NT)), tuple(range(CT_TILES, NT)))
        LIVE_SUM = (0, NT, NT + NT - CT_TILES)

        def split_high(act, g, buffer, group=0, free=False):
            piece_ready(act, g, group)
            if not free:
                act.wait_ge(sem("w_used"), group * GROUP_PIECES + (g + 1))
            act.activation(buffer, ring[:, g % RING, :], ACT.Copy).then_inc(sem("w_high"), 1)

        def split_low(dve, g, buffer, high, group=0):
            dve.wait_ge(sem("w_high"), group * GROUP_PIECES + (g + 1))
            dve.tensor_tensor(buffer, ring[:, g % RING, :], high, ALU.subtract).then_inc(sem("w_low"), 1)

        def kind(t):
            return 1 if t < CT_TILES else 0

        phase = {"pe": 0, "act": 0, "dve": 0, "pool": 0}

        def meet(eng, who):
            phase[who] += 1
            eng.drain().then_inc(sem("phase_over"), 1)
            eng.wait_ge(sem("phase_over"), 4 * phase[who])

        def piece_ready(eng, g, group=0):
            eng.wait_ge(sem(f"ring_loaded{g % RING}"), group * (16 * GROUP_PIECES // RING) + 16 * (g // RING + 1))

        MROW = area(0, 6144)
        HEAD_WH = [area(S_TAB - 8192 + 1024 * i, 1024).bitcast(BF16) for i in range(4)]
        HEAD_WL = [area(S_TAB - 4096 + 1024 * i, 1024).bitcast(BF16) for i in range(4)]
        TTH = T[:, 0:3072].bitcast(BF16).rearrange("p (k n) -> p k n", k=KT)
        TTL = T[:, 3072:6144].bitcast(BF16).rearrange("p (k n) -> p k n", k=KT)
        ZM = [area(2048 + 1024 * i, 1024).rearrange("p (k n) -> p k n", k=KT) for i in range(3)]
        TOH, TOL = [U[:, 4 * i:4 * i + 4, :].rearrange("p a n -> p (a n)").bitcast(BF16).rearrange("p (k n) -> p k n", k=KT)
                    for i in range(2)]
        QD = area(S_QD, 1536).rearrange("p (c n) -> p c n", c=2)
        KVD = area(S_KVD, 768)
        KROPE = area(S_KROPE, 768)
        F = area(S_F, 1536).rearrange("p (c n) -> p c n", c=2)
        COS, SIN = area(S_TAB, 768), area(S_TAB + 768, 768)
        C512 = area(4608, 2048).rearrange("p (t n) -> p t n", t=4)
        S512 = area(6656, 2048).rearrange("p (t n) -> p t n", t=4)
        C256 = area(8704, 512).rearrange("p (t n) -> p t n", t=2)
        S256 = area(9216, 512).rearrange("p (t n) -> p t n", t=2)
        CS64 = area(9728, 256)
        WF = area(9984, 512).rearrange("p (k n) -> p k n", k=2)
        Y1 = area(10496, 3072).rearrange("p (t n) -> p t n", t=NT)
        FO = T[:, 0:1536].rearrange("p (c n) -> p c n", c=2)
        WQ = area(3072, 1536).rearrange("p (k n) -> p k n", k=2)
        WKV = area(4608, 768)
        QT = [area(5376, 768), area(6144, 768)]
        KTH = [area(6912, 768), area(7680, 768)]
        PR = [area(8448, 768), area(9216, 768)]
        PT = [area(9984, 768).rearrange("p (k n) -> p k n", k=NT), area(10752, 768).rearrange("p (k n) -> p k n", k=NT)]
        OQ = area(11520, 2304).rearrange("p (t n) -> p t n", t=NT)
        smx = area(13824, 48)
        smn = area(13872, 48)
        ssum = area(13920, 48)
        sinv = area(13968, 48)
        VT = T[:, 0:2304].rearrange("p (t n) -> p t n", t=NT)
        R3, K3, V3 = U[:, 0:3, :], U[:, 3:6, :], U[:, 6:9, :]
        LOR = U[:, C_LORA, :]
        GD = U[:, C_GD:C_GD + 2, :]
        Y3 = T[:, 0:2304].rearrange("p (q n) -> p q n", q=PAIRS)
        at = 0

        def take(n):
            nonlocal at
            at += n
            return area(at - n, n)

        W2A2 = take(768).rearrange("p (d n) -> p d n", d=2)
        G2W0 = take(768).rearrange("p (d n) -> p d n", d=2)
        KK = take(2304).rearrange("p (q n) -> p q n", q=PAIRS)
        FMS = [[take(1536).rearrange("p (q k n) -> p q k n", q=PAIRS, k=4) for _ in range(2)] for _ in range(2)]
        MA = [take(1536).rearrange("p (q k n) -> p q k n", q=PAIRS, k=4) for _ in range(2)]
        XT = [take(384).rearrange("p (q n) -> p q n", q=PAIRS) for _ in range(2)]
        XN = [take(384).rearrange("p (q n) -> p q n", q=PAIRS) for _ in range(2)]
        BKT = [take(768).rearrange("p (k q n) -> p k q n", k=2, q=PAIRS) for _ in range(2)]
        GB = [take(192).rearrange("p (q n) -> p q n", q=PAIRS) for _ in range(2)]
        UB = [take(192).rearrange("p (q n) -> p q n", q=PAIRS) for _ in range(2)]
        ST = [take(192).rearrange("p (q n) -> p q n", q=PAIRS) for _ in range(2)]
        LC = take(64)
        LW = take(384)
        AA = take(192).rearrange("p (q n) -> p q n", q=PAIRS)
        EX = take(384).rearrange("p (q k n) -> p q k n", q=PAIRS, k=2)
        EN = take(192).rearrange("p (q n) -> p q n", q=PAIRS)
        T1 = take(192).rearrange("p (q n) -> p q n", q=PAIRS)
        T2 = take(192).rearrange("p (q n) -> p q n", q=PAIRS)
        assert at <= SCR
        wend = sb("wend", [P, 2, 2, PAIRS])
        half_ka = sb("half_ka", [P, PAIRS])
        rest_ka = sb("rest_ka", [P, PAIRS])
        bonus = sb("bonus", [P, 2, PAIRS, NCH])
        gstat = sb("gstat", [P, 2, PAIRS * NCH])
        SQ3 = scr[:, 4224:4224 + 2304].rearrange("p (q n) -> p q n", q=PAIRS)
        GT = scr[:, 6528:6528 + 2304].rearrange("p (q n) -> p q n", q=PAIRS)
        LNX = area(8832, 384).rearrange("p (w q n) -> p w q n", w=2, q=PAIRS)
        GBC = [U[:, 8:12, :].rearrange("p a n -> p (a n)")[:, 1024 * s:1024 * s + 1024] for s in range(2)]
        ZN = [area(0, 1024), area(1024, 1024)]
        DG = [area(2048, 1024), area(3072, 1024)]
        XH = U[:, 0:8, :].rearrange("p a n -> p (a n)").rearrange("p (t n) -> p t n", t=NT)
        TNT = area(0, 1024).rearrange("p (k n) -> p k n", k=KT)
        WR = area(4096, 128).rearrange("p (k n) -> p k n", k=KT)
        AFF = area(4224, 96).rearrange("p (t n) -> p t n", t=NT)
        AFT = area(4320, 768)
        WORK = area(5088, 768)
        MASK = area(5856, 768)
        MASKT = area(6624, 96).rearrange("p (t n) -> p t n", t=NT)
        SLOT = area(6720, 96).rearrange("p (t n) -> p t n", t=NT)
        TOP = area(6816, 8)
        rmx, rsm = area(6824, 8), area(6832, 8)
        SLOT_OWN = area(6840, 24).rearrange("p (t e) -> p t e", t=NT)
        AFF_OWN = area(6864, 24).rearrange("p (t e) -> p t e", t=NT)
        SLOT_NXT = area(6888, 24).rearrange("p (t e) -> p t e", t=NT)
        OHX = area(6912, 1024).rearrange("p (t e n) -> p t e n", t=4, e=GROUP)
        OHC = area(7936, 256).rearrange("p (t e n) -> p t e n", t=2, e=GROUP)
        OVX = area(8192, 1024).rearrange("p (t e n) -> p t e n", t=4, e=GROUP)
        OVC = area(9216, 256).rearrange("p (t e n) -> p t e n", t=2, e=GROUP)
        OVTX = area(9472, 1024).rearrange("p (u n) -> p u n", u=2)
        OVTC = area(10496, 256)
        XSF = [area(10752 + 384 * i, 384) for i in range(2)]
        XSH, XSL = [area(11520 + 1536 * i, 1536).bitcast(BF16).rearrange("p (k e n) -> p k e n", k=KT, e=GROUP)
                    for i in range(2)]
        HTH, HTL = [area(14592 + 384 * i, 384).bitcast(BF16).rearrange("p (k n) -> p k n", k=KT) for i in range(2)]
        OEX = area(0, 2048).rearrange("p (u n) -> p u n", u=2)
        OEC = area(2048, 1024)
        HG = U[:, 8:12, :].rearrange("p a n -> p (a n)")[:, 2048:3072]
        WH = [area(a, 1024).bitcast(BF16) for a in (15360, 16384, 3072)]
        WL = [area(a, 1024).bitcast(BF16) for a in (17408, 18432, 4320)]

        def steps(eng, before, step):
            def chunks(n, latent):
                return n, n * -1 + (NCH_C + NCH - 1 if latent else NCH_C - 1)

            before(0, chunks(0, False))
            for n in range(NCH_C):
                step(n, n % 2, chunks(n, False), chunks(n + 1, n + 1 >= NCH_C))
            with eng.Fori(NCH_C, NCH - 2, 2) as n:
                step(n, 0, chunks(n, True), chunks(n + 1, True))
                step(n + 1, 1, chunks(n + 1, True), chunks(n + 2, True))
            step(NCH - 2, 0, chunks(NCH - 2, True), chunks(NCH - 1, True))
            step(NCH - 1, 1, chunks(NCH - 1, True), None)

        def count(l, n, d):
            return n * 2 + (2 * NCH * l + d + 1)

        def level_count(l, n, d, j):
            return n * (2 * (LEVELS - 1)) + (2 * NCH * l * (LEVELS - 1) + 2 * (j - 1) + d + 1)

        block = ctx.enter_context(nc.Block())

        @block.sync
        def _(sp):
            sp.dma_start(cv[:, :, :], cvec).then_inc(sem("c_loaded"), 16)
            sp.dma_start(cst[:, :], consts).then_inc(sem("consts_loaded"), 16)
            for t in range(NT):
                src = ctx_in[t * P:(t + 1) * P, :] if t < CT_TILES else x_in[(t - CT_TILES) * P:(t - CT_TILES + 1) * P, :]
                sp.dma_start(X[:, t, :], src).then_inc(sem("x_loaded"), 16)

            def load(g, src, k, n, group=0):
                dst = ring[:, g % RING, 0:k * n].rearrange("p (k n) -> p k n", k=k)
                sp.dma_start(dst, src).then_inc(sem(f"ring_loaded{g % RING}"), 16)

            def load_expert(l, i, group):
                g = l * LAYER_PIECES + HEAD_PIECES + i
                e, j = (i % GROUP_PIECES) // EX_PIECES, i % EX_PIECES
                first = l * NE + GROUP * (i // GROUP_PIECES) + e
                at = bass.ds(group * GROUP + first, 1)
                w = (w_eg, w_eu, w_ed)[j // 4]
                src = w[at, :, :].rearrange("e (k p) n -> p (e k) n", p=P)
                if j < 8:
                    load(g, src[:, :, 256 * (j % 4):256 * (j % 4) + 256], KT, 256)
                else:
                    load(g, src[:, 2 * (j - 8):2 * (j - 8) + 2, :], 2, D)

            for l in range(DEPTH):
                for j in range(HEAD_PIECES):
                    g = l * LAYER_PIECES + j
                    if g >= RING:
                        sp.wait_ge(sem("w_low"), g - RING + 1)
                    if j < MOD_PIECES:
                        load(g, w_mod[l].rearrange("(k p) n -> p k n", p=P)[:, :, 256 * j:256 * j + 256], KT, 256)
                    elif j < MOD_PIECES + IN_PIECES:
                        i = j - MOD_PIECES
                        load(g, w_in[l].rearrange("(k p) n -> p k n", p=P)[:, :, 256 * i:256 * i + 256], KT, 256)
                    else:
                        i = j - MOD_PIECES - IN_PIECES
                        load(g, w_out[l].rearrange("(k p) n -> p k n", p=P)[:, 2 * i:2 * i + 2, :], 2, D)
                for i in range(RING):
                    sp.wait_ge(sem("w_low"), l * LAYER_PIECES + HEAD_PIECES - RING + i + 1)
                    load_expert(l, i, 0)
                with sp.Fori(0, GROUPS - 1) as group:
                    for i in range(GROUP_PIECES):
                        sp.wait_ge(sem("w_low"), group * GROUP_PIECES + (l * LAYER_PIECES + HEAD_PIECES + i + 1))
                        load_expert(l, i + RING, group)
                for i in range(GROUP_PIECES - RING):
                    sp.wait_ge(sem("w_low"), (GROUPS - 1) * GROUP_PIECES + (l * LAYER_PIECES + HEAD_PIECES + i + 1))
                    load_expert(l, i + RING, GROUPS - 1)
            for i, t in enumerate(LIVE[1]):
                sp.wait_ge(sem("ffn_out"), LIVE_SUM[1] + i + 1)
                sp.dma_start(out[(t - CT_TILES) * P:(t - CT_TILES + 1) * P, :], X[:, t, :]).then_inc(sem("stored"), 16)
            sp.wait_ge(sem("stored"), 16 * len(LIVE[1]))

        @block.gpsimd
        def _(pool):
            who = "pool"
            for l in range(DEPTH):
                pool.dma_start(vec[:, :], vecs[l]).then_inc(sem("vec_loaded"), 16)
                pool.wait_ge(sem("vec_loaded"), 16 * (l + 1))
                meet(pool, who)
                pool.dma_start(area(S_TAB, 1536), rope).then_inc(sem("rope_loaded"), 16)
                pool.wait_ge(sem("rope_loaded"), 16 * (l + 1))
                for t in range(NT):
                    pool.wait_ge(sem("mix_high"), l * NT + t + 1)
                    cols = slice(t * P, (t + 1) * P)
                    pool.tensor_tensor(TTL[:, :, cols], ZM[t % 3], TTH[:, :, cols], ALU.subtract).then_inc(sem("mix_low"), 1)
                meet(pool, who)
                meet(pool, who)
                pool.dma_start(area(4608, 5376), dft).then_inc(sem("dft_loaded"), 16)
                pool.dma_start(WF, w_f[l].rearrange("(k p) n -> p k n", p=P)).then_inc(sem("dft_loaded"), 16)
                pool.wait_ge(sem("dft_loaded"), 32 * (l + 1))
                meet(pool, who)
                pool.dma_start(WQ, w_q[l].rearrange("(k p) n -> p k n", p=P)).then_inc(sem("mlaw_loaded"), 16)
                pool.dma_start(WKV, w_kv[l]).then_inc(sem("mlaw_loaded"), 16)
                pool.wait_ge(sem("mlaw_loaded"), 32 * (l + 1))
                meet(pool, who)
                pool.dma_start(area(0, 768), lora[l]).then_inc(sem("rww_loaded"), 16)
                pool.dma_start(area(768, 768), g2w0[l]).then_inc(sem("rww_loaded"), 16)
                pool.memset(Y3, 0.0)
                pool.wait_ge(sem("rww_loaded"), 32 * (l + 1))
                meet(pool, who)

                def prepare(n, d, chunk):
                    tok = bass.ds(chunk * CH, CH)
                    pool.wait_ge(sem("gates_tanh"), count(l, n, d))
                    if not (isinstance(n, int) and n == 0 and d == 0):
                        pool.wait_ge(sem("fm_ready"), count(l, n, d) - 1)
                    pool.tensor_tensor(T2, AA, ones[:, 0:HD].unsqueeze(1).to_broadcast([P, PAIRS, HD]), ALU.add)
                    for p in range(PAIRS):
                        pool.tensor_scalar(T1[:, p, :], AA[:, p, :], half_ka[:, p:p + 1], rest_ka[:, p:p + 1], ALU.mult, ALU.add)
                    pool.drain()
                    pool.tensor_tensor(T1, T1, K3[:, :, tok], ALU.mult)
                    pool.tensor_tensor(T2, T2, KK[:, :, tok], ALU.mult)
                    pool.drain().then_inc(sem("kd_ready"), 1)

                def before(n, chunk):
                    for d in range(2):
                        prepare(n, d, chunk[d])

                def step(n, par, chunk, nxt):
                    for d in range(2):
                        pool.wait_ge(sem("fm_ready"), count(l, n, d))
                        if not (isinstance(n, int) and n == 0):
                            pool.wait_ge(sem("scan_mm"), count(l, n, d) - 2)
                        pool.tensor_tensor(BKT[d][:, 1], FMS[par][d][:, :, 1, :], FMS[par][d][:, :, 3, :], ALU.mult)\
                            .then_inc(sem("prd_ready"), 1)
                    for d in range(2):
                        pool.wait_ge(sem("a_copied"), count(l, n, d))
                        pool.tensor_tensor(MA[d][:, :, 1:4, :], MA[d][:, :, 1:4, :],
                                           tri[:, d].unsqueeze(1).to_broadcast([P, PAIRS, 3, P]), ALU.mult)\
                            .then_inc(sem("a_masked"), 1)
                    if nxt:
                        before(n + 1, nxt)

                steps(pool, before, step)
                meet(pool, who)
                pool.dma_start(area(8832, 384), lnx[l]).then_inc(sem("lnx_loaded"), 16)
                pool.wait_ge(sem("lnx_loaded"), 16 * (l + 1))
                meet(pool, who)
                meet(pool, who)
                pool.dma_start(WR, w_r[l].rearrange("(k p) n -> p k n", p=P)).then_inc(sem("wr_loaded"), 16)
                pool.memset(T[:, :], 0.0)
                pool.wait_ge(sem("wr_loaded"), 16 * (l + 1))
                meet(pool, who)

                def one_hot(t, e, slots, x, c, aff=None):
                    col = slots[:, t, e:e + 1]
                    dst = c[:, t, e, :] if t < CT_TILES else x[:, t - CT_TILES, e, :]
                    src = iota[:, 0:CAP_C] if t < CT_TILES else iota
                    if aff is None:
                        return pool.tensor_scalar(dst, src, col, None, ALU.is_equal)
                    return pool.tensor_scalar(dst, src, col, aff[:, t, e:e + 1], ALU.is_equal, ALU.mult)

                def one_hots_to_gather(group):
                    pool.wait_ge(sem("oh_used"), group + l * (GROUPS + 1) + 1)
                    pool.tensor_copy(SLOT_NXT[:, LIVE[l][0]:NT, :], SLOT[:, LIVE[l][0]:NT, bass.ds(group * GROUP, GROUP)])
                    pool.drain()
                    for t in LIVE[l]:
                        for e in range(GROUP):
                            one_hot(t, e, SLOT_NXT, OHX, OHC)
                    pool.drain().then_inc(sem("oh_ready"), 1)

                def one_hots_to_scatter(group):
                    pool.wait_ge(sem("ov_used"), group + l * (GROUPS + 1) + 1)
                    pool.tensor_copy(SLOT_OWN[:, LIVE[l][0]:NT, :], SLOT[:, LIVE[l][0]:NT, bass.ds(group * GROUP, GROUP)])
                    pool.tensor_copy(AFF_OWN[:, LIVE[l][0]:NT, :], AFF[:, LIVE[l][0]:NT, bass.ds(group * GROUP, GROUP)])
                    pool.drain()
                    for t in LIVE[l]:
                        for e in range(GROUP):
                            one_hot(t, e, SLOT_OWN, OVX, OVC, AFF_OWN)
                    pool.drain().then_inc(sem("ov_ready"), 1)

                one_hots_to_gather(0)
                with pool.Fori(0, GROUPS - 1) as group:
                    one_hots_to_scatter(group)
                    one_hots_to_gather(group + 1)
                one_hots_to_scatter(GROUPS - 1)
                meet(pool, who)
                meet(pool, who)

        @block.scalar
        def _(act):
            who = "act"
            for l in range(DEPTH):
                if l == 0:
                    act.wait_ge(sem("c_loaded"), 16)
                    act.activation(cv[:, :, :], cv[:, :, :], ACT.Silu)
                    act.drain()
                    act.activation(cv_halves[:, :, 0:2], cv[:, :, :], ACT.Copy).then_inc(sem("silu_c"), 1)
                G = l * LAYER_PIECES
                for j in range(MOD_PIECES):
                    split_high(act, G + j, HEAD_WH[j % 4])
                    if j % 2 and j >= 3:
                        act.wait_ge(sem("mod_mm"), (MOD_PIECES // 2) * l + (j - 1) // 2)
                        b = (j - 3) // 2
                        act.activation(MROW[0:4, 512 * b:512 * b + 512], banks(2 + b % 4)[0:4, :], ACT.Copy)\
                           .then_inc(sem("mod_row"), 1)
                    if j % 2 == 0 and 4 <= j < 4 + 2 * NT:
                        t = (j - 4) // 2
                        if l == 0:
                            act.wait_ge(sem("x_loaded"), 16 * NT)
                        act.activation(T[:, t * D:(t + 1) * D], X[:, t, :], ACT.Square, accum_out=ss[:, t:t + 1])\
                           .then_inc(sem("mix_ss"), 1)
                act.wait_ge(sem("mod_mm"), (MOD_PIECES // 2) * (l + 1))
                b = MOD_PIECES // 2 - 1
                act.activation(MROW[0:4, 512 * b:512 * b + 512], banks(2 + b % 4)[0:4, :], ACT.Copy).then_inc(sem("mod_row"), 1)
                act.wait_ge(sem("mix_ms"), l + 1)
                act.activation(rstd[:, 0:NT], ss[:, 0:NT], ACT.Sqrt).then_inc(sem("mix_std"), 1)
                meet(act, who)

                def mixed_high(t):
                    act.wait_ge(sem("mix_out_act"), l * NT + t + 1)
                    act.wait_ge(sem("mix_out_dve"), l * NT + t + 1)
                    act.activation(TTH[:, :, t * P:(t + 1) * P], ZM[t % 3], ACT.Copy).then_inc(sem("mix_high"), 1)

                G += MOD_PIECES
                for t in range(NT):
                    if t in (1, 3):
                        split_high(act, G + t // 2, HEAD_WH[(MOD_PIECES + t // 2) % 4])
                    act.wait_ge(sem("mix_turned"), l * NT + t + 1)
                    if t >= 3:
                        act.wait_ge(sem("mix_low"), l * NT + t - 2)
                    src = banks(2 * (t % 4), 2).rearrange("p (k n) -> p k n", k=KT)
                    for k in range(KT // 2, KT):
                        ins = act.activation(ZM[t % 3][:, k, :], src[:, k, :], ACT.Identity,
                                             bias=modc[:, k, kind(t):kind(t) + 1], scale=sc_mix[:, k, kind(t):kind(t) + 1])
                    ins.then_inc(sem("mix_out_act"), 1)
                    if t:
                        mixed_high(t - 1)
                mixed_high(NT - 1)
                meet(act, who)

                for c in range(NCHUNK_IN):
                    if c % 2 == 0 and c // 2 + 2 < IN_PIECES:
                        split_high(act, G + c // 2 + 2, HEAD_WH[(MOD_PIECES + c // 2 + 2) % 4])
                    if c < C_LORA or c == C_KR:
                        continue
                    act.wait_ge(sem("in_mm"), l * NCHUNK_IN + c + 1)
                    src = banks(2 * (c % 4), 2)[:, 0:NTOK]
                    if c == C_LORA:
                        act.activation(LOR[0:64, :], src[0:64, :], ACT.Tanh)
                        ins = act.activation(LOR[64:128, :], src[64:128, :], ACT.Copy)
                    elif c == C_GD:
                        ins = act.activation(GD[:, 0, :], src, ACT.Tanh, scale=0.5)
                    elif c == C_GD2:
                        ins = act.activation(GD[0:32, 1, :], src[0:32, :], ACT.Tanh, scale=0.5)
                    elif c < C_KVD:
                        ins = act.activation(QD[:, c - C_QD, :], src, ACT.Copy)
                    elif c == C_KVD:
                        ins = act.activation(KVD, src, ACT.Copy)
                    else:
                        ins = act.activation(F[:, c - C_F, :], src, ACT.Copy)
                    ins.then_inc(sem("in_out_act"), 1)
                meet(act, who)

                for t in range(NT):
                    act.wait_ge(sem("dft64_mm"), l * NT + t + 1)
                    act.activation(Y1[:, t, :], banks(t), ACT.Copy).then_inc(sem("dft64_out"), 1)
                for j in range(2):
                    act.wait_ge(sem("dft_mm"), 2 * l + j + 1)
                    act.activation(FO[:, j, :], banks(2 * j, 2)[:, 0:NTOK], ACT.Copy).then_inc(sem("dft_out"), 1)
                for j in range(2):
                    act.wait_ge(sem("wf_mm"), 2 * l + j + 1)
                    act.activation(TT[:, 6 + j, :], banks(4 + 2 * j, 2)[:, 0:NTOK], ACT.Copy)
                meet(act, who)

                for j in range(2):
                    act.activation(QT[j], QD[:, j, :], ACT.Square)
                act.activation(KTH[0], KVD, ACT.Square).then_inc(sem("lat_sq"), 1)
                act.wait_ge(sem("lat_ms"), l + 1)
                act.activation(PR[0], PR[0], ACT.Sqrt)
                act.activation(PR[1], PR[1], ACT.Sqrt).then_inc(sem("lat_std"), 1)
                for t in range(NT):
                    act.wait_ge(sem("v_mm"), l * NT + t + 1)
                    act.activation(VT[:, t, :], banks(4 + t % 4)[:, 0:RW], ACT.Copy).then_inc(sem("v_out"), 1)
                units = [(h, q) for h in range(HEADS) for q in LIVE[l]]
                U0 = HEADS * LIVE_SUM[l]
                for i, (h, q) in enumerate(units):
                    nk = CTX if q < CT_TILES else NTOK
                    if q == LIVE[l][0]:
                        act.wait_ge(sem("q_mm"), l * HEADS + h + 1)
                        act.activation(QT[h % 2][0:64, :], banks(6, 2)[0:64, 0:NTOK], ACT.Copy).then_inc(sem("q_out_act"), 1)
                        act.wait_ge(sem("k_mm"), l * HEADS + h + 1)
                        act.activation(KTH[h % 2][0:64, :], banks(6, 2)[0:64, 0:NTOK], ACT.Copy).then_inc(sem("k_out_act"), 1)
                    act.wait_ge(sem("smax"), U0 + i + 1)
                    if i >= 2:
                        act.wait_ge(sem("p_turned"), U0 + i - 1)
                    act.activation(PR[i % 2][:, 0:nk], banks(2 * (i % 2), 2)[:, 0:nk], ACT.Exp, bias=smn[:, i:i + 1],
                                   scale=MLA_SCALE, accum_out=ssum[:, i:i + 1]).then_inc(sem("p_ready"), 1)
                    if i >= 1:
                        act.wait_ge(sem("p_turned"), U0 + i)
                        if i >= 3:
                            act.wait_ge(sem("pv_mm"), U0 + i - 2)
                        m = CTX if units[i - 1][1] < CT_TILES else NTOK
                        act.activation(PT[(i - 1) % 2].rearrange("p k n -> p (k n)")[:, 0:m], banks(4, 2)[:, 0:m],
                                       ACT.Copy).then_inc(sem("pt_ready"), 1)
                i = len(units)
                act.wait_ge(sem("p_turned"), U0 + i)
                act.wait_ge(sem("pv_mm"), U0 + i - 2)
                act.activation(PT[(i - 1) % 2].rearrange("p k n -> p (k n)"), banks(4, 2)[:, 0:NTOK], ACT.Copy)\
                   .then_inc(sem("pt_ready"), 1)
                for i, q in enumerate(LIVE[l]):
                    act.wait_ge(sem("o_turned"), LIVE_SUM[l] + i + 1)
                    act.activation(TT[:, 3:6, q * P:(q + 1) * P], banks(i)[:, 0:RW].rearrange("p (j n) -> p j n", j=3),
                                   ACT.Copy)
                meet(act, who)

                for p in range(PAIRS):
                    act.wait_ge(sem("kk_raw"), l * PAIRS + p + 1)
                    act.activation(SQ3[:, p, :], KK[:, p, :], ACT.Square).then_inc(sem("kk_sq"), 1)
                for p in range(PAIRS):
                    act.wait_ge(sem("kk_ss"), l * PAIRS + p + 1)
                    act.activation(GT[:, p, :], banks(2 * p, 2)[:, 0:NTOK], ACT.Sqrt).then_inc(sem("kk_norm"), 1)
                meet(act, who)

                def chunk_in(n, d, chunk):
                    act.wait_ge(sem("lc_used"), count(l, n, d))
                    act.activation(LC, LOR[:, bass.ds(chunk * CH, CH)], ACT.Copy).then_inc(sem("lc_ready"), 1)

                def gates(n, d):
                    act.wait_ge(sem("gates_mm"), count(l, n, d))
                    act.activation(LW[0:64, :], psum[0:64, 3 * d + 1, 0:RW], ACT.Tanh, scale=0.5)
                    for p in range(PAIRS):
                        ins = act.activation(AA[:, p, :], psum[:, 4 - 3 * d, p * CH:(p + 1) * CH], ACT.Tanh, scale=0.5,
                                             bias=half_a0[:, 3 * d + p:3 * d + p + 1])
                    ins.then_inc(sem("gates_tanh"), 1)

                def decays(n, d):
                    act.wait_ge(sem("cum_mm"), count(l, n, d))
                    cum = psum[:, 3 * d + 1, 0:384].rearrange("p (q k n) -> p q k n", q=PAIRS, k=2)
                    act.activation(EX, cum, ACT.Exp, scale=-DECAY)
                    act.activation(EN, cum[:, :, 1, :], ACT.Exp, scale=DECAY).then_inc(sem("decays_ready"), 1)

                def before(n, chunk):
                    for d in range(2):
                        chunk_in(n, d, chunk[d])
                        gates(n, d)
                        decays(n, d)

                def step(n, par, chunk, nxt):
                    for d in range(2):
                        act.wait_ge(sem("xt_begun"), count(l, n, d))
                        act.activation(MA[d][:, :, 1:4, :], psum[:, 3 * d:3 * d + 3, 128:512].rearrange("p q (k n) -> p q k n", k=3),
                                       ACT.Copy).then_inc(sem("a_copied"), 1)
                    for d in range(2):
                        act.wait_ge(sem("bk_turned"), count(l, n, d))
                        act.activation(BKT[d].rearrange("p k q n -> p (k q n)"), banks(3 * d, 2)[:, 0:768], ACT.Copy)
                        act.activation(bonus[:, d, :, bass.ds(chunk[d], 1)], psum[:, 3 * d + 2, 0:PAIRS].unsqueeze(2), ACT.Copy)\
                           .then_inc(sem("bkt_ready"), 1)
                    for j in range(1, LEVELS):
                        if nxt and j == 4:
                            decays(n + 1, 0)
                            chunk_in(n + 1, 1, nxt[1])
                        for d in range(2):
                            act.wait_ge(sem("xt_turned"), level_count(l, n, d, j))
                            act.activation(XN[d].rearrange("p q n -> p (q n)"), psum[:, 3 * d, 0:384], ACT.Copy)\
                               .then_inc(sem("xn_ready"), 1)
                        if nxt and j == 1:
                            chunk_in(n + 1, 0, nxt[0])
                        elif nxt and j == 2:
                            gates(n + 1, 0)
                        elif nxt and j == 5:
                            gates(n + 1, 1)
                            decays(n + 1, 1)
                    for d in range(2):
                        act.wait_ge(sem("g_mm"), count(l, n, d))
                        act.activation(GB[d].rearrange("p q n -> p (q n)"), psum[:, 6 + d, 0:192], ACT.Copy)\
                           .then_inc(sem("g_ready"), 1)
                    for d in range(2):
                        act.wait_ge(sem("u_mm"), count(l, n, d))
                        act.activation(UB[d].rearrange("p q n -> p (q n)"), psum[:, 6 + d, 192:384], ACT.Copy)\
                           .then_inc(sem("u_ready"), 1)

                steps(act, before, step)
                meet(act, who)

                G += IN_PIECES
                for j in range(OUT_PIECES):
                    split_high(act, G + j, HEAD_WH[j], free=True)
                act.wait_ge(sem("y_centred"), l + 1)
                for p in range(PAIRS):
                    ins = act.activation(SQ3[:, p, :], Y3[:, p, :], ACT.Square)
                ins.then_inc(sem("y_sq"), 1)
                act.wait_ge(sem("y_var"), l + 1)
                act.activation(gstat[:, 1, :], gstat[:, 1, :], ACT.Sqrt).then_inc(sem("y_std"), 1)
                for p in range(PAIRS):
                    act.wait_ge(sem("gate_mm"), l * PAIRS + p + 1)
                    act.activation(GT[:, p, :], banks(2 * p, 2)[:, 0:NTOK], ACT.Copy).then_inc(sem("gate_out"), 1)
                meet(act, who)

                live_cols = slice(LIVE[l][0] * P, NTOK)
                for k in range(KT):
                    act.activation(TOH[:, k, live_cols], TT[:, k, live_cols], ACT.Copy).then_inc(sem("mixed_high"), 1)
                for s in range(2 - l):
                    act.wait_ge(sem("gate_bc_mm"), (0, 4)[l] + s + 1)
                    act.activation(GBC[s], banks(4 + 2 * s, 2), ACT.Copy).then_inc(sem("gate_bc"), 1)
                for i, t in enumerate(LIVE[l]):
                    N = LIVE_SUM[l] + i + 1
                    act.wait_ge(sem("out_mm"), N)
                    act.activation(DG[0], banks(2 * (i % 2), 2), ACT.Square, accum_out=ss[:, t:t + 1]).then_inc(sem("out_ss"), 1)
                    act.wait_ge(sem("out_ms"), N)
                    act.activation(rstd[:, t:t + 1], ss[:, t:t + 1], ACT.Sqrt).then_inc(sem("out_std"), 1)
                meet(act, who)

                for i, t in enumerate(LIVE[l]):
                    act.activation(XH[:, t, :], X[:, t, :], ACT.Square, accum_out=ss[:, t:t + 1]).then_inc(sem("ffn_ss"), 1)
                act.wait_ge(sem("ffn_ms"), l + 1)
                act.activation(rstd[:, 0:NT], ss[:, 0:NT], ACT.Sqrt).then_inc(sem("ffn_std"), 1)
                for i, t in enumerate(LIVE[l]):
                    N = LIVE_SUM[l] + i + 1
                    act.wait_ge(sem("ffn_turned"), N)
                    if i >= 1:
                        act.wait_ge(sem("router_mm"), N - 1)
                    src = banks(0, 2).rearrange("p (k n) -> p k n", k=KT)
                    for k in range(KT):
                        ins = act.activation(TNT[:, k, :], src[:, k, :], ACT.Identity,
                                             bias=modc[:, 24 + k, kind(t):kind(t) + 1],
                                             scale=sc_ffn[:, k, kind(t):kind(t) + 1])
                    ins.then_inc(sem("tnt_ready"), 1)
                    act.wait_ge(sem("router_max"), N)
                    act.activation(AFF[:, t, :], banks(2)[:, 0:NE], ACT.Exp, bias=rmx[:, t:t + 1],
                                   accum_out=rsm[:, t:t + 1]).then_inc(sem("router_exp"), 1)
                for s in range(2 - l):
                    act.wait_ge(sem("gate_bc_mm"), (2, 5)[l] + s + 1)
                    act.activation(GBC[s], banks(4 + 2 * s, 2), ACT.Copy).then_inc(sem("gate_bc"), 1)
                meet(act, who)

                sl = SLOTS if l == 0 else CAP_X

                def gathered(group):
                    for k in range(KT):
                        N = group * KT + (l * GROUPS * KT + k + 1)
                        act.wait_ge(sem("gather_mm"), N)
                        act.wait_ge(sem("xs_split"), N)
                        for s in range(2 - l):
                            a, b = (0, 256) if s == 0 else (256, 384)
                            ins = act.activation(XSF[k % 2][:, a:b], banks(6 + k % 2)[:, a:b], ACT.Identity,
                                                 bias=modc[:, 24 + k, s:s + 1], scale=sc_ffn[:, k, s:s + 1])
                        ins.then_inc(sem("xs_ready"), 1)

                def rows_out(group, e):
                    act.wait_ge(sem("down_mm"), group * GROUP + (l * NE + e + 1))
                    if e == 0:
                        act.wait_ge(sem("oe_used"), group + (l * (GROUPS + 1) + 1))
                    ins = act.activation(OEX[64 * (e % 2):64 * (e % 2) + 64, e // 2, :], banks(0, 2)[0:CAP_X, :], ACT.Copy)
                    if l == 0:
                        ins = act.activation(OEC[32 * e:32 * e + 32, :], banks(0, 2)[CAP_X:SLOTS, :], ACT.Copy)
                    ins.then_inc(sem("oe_ready"), 1)

                def group_body(group):
                    def high(i):
                        split_high(act, l * LAYER_PIECES + HEAD_PIECES + i, WH[i % 3], group)

                    def silu(e, h):
                        act.wait_ge(sem("expert_gate_mm"), group * (2 * GROUP) + (2 * l * NE + 2 * e + h + 1))
                        act.activation(HG[0:sl, 512 * h:512 * h + 512], banks(2 + h)[0:sl, :], ACT.Silu)\
                           .then_inc(sem("silu_ready"), 1)

                    for e in range(GROUP):
                        i = e * EX_PIECES
                        high(i)
                        high(i + 1)
                        if e:
                            rows_out(group, e - 1)
                        if e == 1:
                            act.wait_ge(sem("ovtx_mm"), group + (l * GROUPS + 1))
                            act.activation(OVTX, psum[:, 6:8, :], ACT.Copy).then_inc(sem("ovt_ready"), 1)
                        if e == 2 and l == 0:
                            act.wait_ge(sem("ovtc_mm"), group + 1)
                            act.activation(OVTC, banks(6)[:, 0:CTX], ACT.Copy).then_inc(sem("ovt_ready"), 1)
                        high(i + 2)
                        high(i + 3)
                        silu(e, 0)
                        high(i + 4)
                        high(i + 5)
                        silu(e, 1)
                        for j in range(6, EX_PIECES):
                            high(i + j)
                    rows_out(group, GROUP - 1)

                gathered(0)
                with act.Fori(0, GROUPS - 1) as group:
                    group_body(group)
                    gathered(group + 1)
                group_body(GROUPS - 1)
                meet(act, who)

                for i, t in enumerate(LIVE[l]):
                    act.activation(XH[:, t, :], YA[:, t, :], ACT.Square, accum_out=ss[:, t:t + 1]).then_inc(sem("y_ss"), 1)
                act.wait_ge(sem("y_ms"), l + 1)
                act.activation(rstd[:, 0:NT], ss[:, 0:NT], ACT.Sqrt).then_inc(sem("ys_std"), 1)
                meet(act, who)

        @block.vector
        def _(dve):
            who = "dve"

            def mean_square(width, want, got, n0=0):
                dve.tensor_scalar(ss[:, n0:NT], ss[:, n0:NT], 1.0 / width, EPS, ALU.mult, ALU.add).then_inc(sem(want), 1)

            for l in range(DEPTH):
                G = l * LAYER_PIECES
                if l == 0:
                    dve.wait_ge(sem("silu_c"), 1)
                    dve.tensor_tensor(cv_halves[:, :, 2:4], cv[:, :, :], cv_halves[:, :, 0:2], ALU.subtract)\
                       .then_inc(sem("c_split"), 1)
                for j in range(MOD_PIECES):
                    split_low(dve, G + j, HEAD_WL[j % 4], HEAD_WH[j % 4])
                dve.wait_ge(sem("mix_ss"), NT * (l + 1))
                mean_square(D, "mix_ms", None)
                dve.wait_ge(sem("mix_std"), l + 1)
                dve.reciprocal(rstd[:, 0:NT], rstd[:, 0:NT])
                dve.wait_ge(sem("vec_loaded"), 16 * (l + 1))
                dve.wait_ge(sem("mod_turned"), l + 1)
                dve.tensor_tensor(modc[:, :, :], banks(0)[:, 0:96].rearrange("p (m s) -> p m s", s=2),
                                  v("b_mod").unsqueeze(2).to_broadcast([P, 48, 2]), ALU.add)
                dve.tensor_scalar(half_a0[:, :], v("a0"), 0.5, None, ALU.mult)
                dve.tensor_scalar(half_ka[:, :], v("k_a"), 0.5, None, ALU.mult)
                dve.tensor_scalar(rest_ka[:, :], v("k_a"), -0.5, 1.0, ALU.mult, ALU.add)
                dve.drain()
                for dst, m, add, g in ((sc_mix, 1, 1.0, "g_pre_mix"), (gt_mix, 2, 0.0, "g_post_mix"),
                                       (sc_ffn, 4, 1.0, "g_pre_ffn"), (gt_ffn, 5, 0.0, "g_post_ffn")):
                    dve.scalar_tensor_tensor(out=dst[:, :, :], in0=modc[:, 8 * m:8 * m + 8, :], scalar=add,
                                             in1=v(g).unsqueeze(2).to_broadcast([P, KT, 2]), op0=ALU.add, op1=ALU.mult)
                meet(dve, who)

                def normed(t):
                    if t >= 2:
                        dve.wait_ge(sem("mix_turned"), l * NT + t - 1)
                    dve.tensor_scalar(ZN[t % 2], X[:, t, :], rstd[:, t:t + 1], None, ALU.mult).then_inc(sem("mix_normed"), 1)

                normed(0)
                G += MOD_PIECES
                for t in range(NT):
                    if t + 1 < NT:
                        normed(t + 1)
                    if t in (1, 3):
                        j = MOD_PIECES + t // 2
                        split_low(dve, G + t // 2, HEAD_WL[j % 4], HEAD_WH[j % 4])
                    dve.wait_ge(sem("mix_turned"), l * NT + t + 1)
                    if t >= 3:
                        dve.wait_ge(sem("mix_low"), l * NT + t - 2)
                    src = banks(2 * (t % 4), 2).rearrange("p (k n) -> p k n", k=KT)
                    for k in range(KT // 2):
                        ins = dve.tensor_scalar(ZM[t % 3][:, k, :], src[:, k, :], sc_mix[:, k, kind(t):kind(t) + 1],
                                                modc[:, k, kind(t):kind(t) + 1], ALU.mult, ALU.add)
                    ins.then_inc(sem("mix_out_dve"), 1)
                meet(dve, who)

                for c in range(NCHUNK_IN):
                    if c % 2 == 0 and c // 2 + 2 < IN_PIECES:
                        j = MOD_PIECES + c // 2 + 2
                        split_low(dve, G + c // 2 + 2, HEAD_WL[j % 4], HEAD_WH[j % 4])
                    src = banks(2 * (c % 4), 2)[:, 0:NTOK]
                    if c < C_LORA:
                        dve.wait_ge(sem("in_mm"), l * NCHUNK_IN + c + 1)
                        tap = [v("conv")[:, 9 * j + c:9 * j + c + 1] for j in range(3)]
                        dve.tensor_scalar(U[:, c, :], src, tap[1], None, ALU.mult)
                        dve.drain()
                        for a, b in SEQS:
                            dve.scalar_tensor_tensor(out=U[:, c, a + 1:b], in0=src[:, a:b - 1], scalar=tap[0],
                                                     in1=U[:, c, a + 1:b], op0=ALU.mult, op1=ALU.add)
                        dve.drain()
                        for a, b in SEQS:
                            ins = dve.scalar_tensor_tensor(out=U[:, c, a:b - 1], in0=src[:, a + 1:b], scalar=tap[2],
                                                           in1=U[:, c, a:b - 1], op0=ALU.mult, op1=ALU.add)
                        ins.then_inc(sem("in_out_dve"), 1)
                    elif c == C_GD2:
                        dve.wait_ge(sem("in_mm"), l * NCHUNK_IN + c + 1)
                        dve.wait_ge(sem("in_out_act"), l * 8 + 3)
                        dve.tensor_tensor(area(PROJ, 768)[64:96, :], src[64:96, :], SIN[64:96, :], ALU.mult)
                        dve.tensor_scalar(GD[:, 0, :], GD[:, 0, :], 0.5, 0.5, ALU.mult, ALU.add)
                        dve.tensor_scalar(GD[0:32, 1, :], GD[0:32, 1, :], 0.5, 0.5, ALU.mult, ALU.add)\
                           .then_inc(sem("in_out_dve"), 1)
                    elif c == C_KR:
                        dve.wait_ge(sem("in_mm"), l * NCHUNK_IN + c + 1)
                        dve.tensor_tensor(KROPE[64:96, :], src[64:96, :], COS[64:96, :], ALU.mult)
                        dve.drain()
                        dve.tensor_tensor(KROPE[64:96, :], KROPE[64:96, :], area(PROJ, 768)[64:96, :], ALU.add)\
                           .then_inc(sem("in_out_dve"), 1)
                meet(dve, who)

                meet(dve, who)

                for j, w in ((0, 256), (1, 128)):
                    dve.wait_ge(sem("lat_ss"), 2 * l + j + 1)
                    ins = dve.tensor_scalar(PR[j], banks(2 * j, 2)[:, 0:NTOK], 1.0 / w, EPS, ALU.mult, ALU.add)
                ins.then_inc(sem("lat_ms"), 1)
                dve.wait_ge(sem("lat_std"), l + 1)
                dve.reciprocal(PR[0], PR[0])
                dve.reciprocal(PR[1], PR[1])
                dve.drain()
                dve.scalar_tensor_tensor(out=KVD, in0=KVD, scalar=v("g_kv"), in1=PR[1], op0=ALU.mult, op1=ALU.mult)
                for j in range(2):
                    dve.scalar_tensor_tensor(out=QD[:, j, :], in0=QD[:, j, :], scalar=v("g_q")[:, j:j + 1], in1=PR[0],
                                             op0=ALU.mult, op1=ALU.mult)
                dve.drain().then_inc(sem("lat_normed"), 1)
                for j in range(2):
                    dve.tensor_copy(KTH[j][64:96, :], KROPE[64:96, :])
                units = [(h, q) for h in range(HEADS) for q in LIVE[l]]
                U0 = HEADS * LIVE_SUM[l]

                def finish(i):
                    h, q = units[i]
                    dve.reciprocal(sinv[:, i:i + 1], ssum[:, i:i + 1])
                    dve.drain()
                    dve.wait_ge(sem("pv_mm"), U0 + i + 1)
                    dve.tensor_scalar(OQ[:, q, h * HD:(h + 1) * HD], banks(7)[:, 256:320],
                                      sinv[:, i:i + 1], None, ALU.mult).then_inc(sem("o_ready"), 1)

                for i, (h, q) in enumerate(units):
                    nk = CTX if q < CT_TILES else NTOK
                    if q == LIVE[l][0]:
                        dve.wait_ge(sem("q_mm"), l * HEADS + h + 1)
                        dve.tensor_tensor(QT[h % 2][64:96, :], banks(6, 2)[64:96, 0:NTOK], COS[64:96, :], ALU.mult)\
                           .then_inc(sem("q_cos"), 1)
                        dve.wait_ge(sem("q_sw_mm"), l * HEADS + h + 1)
                        dve.tensor_tensor(KROPE[64:96, :], banks(6, 2)[64:96, 0:NTOK], SIN[64:96, :], ALU.mult)\
                           .then_inc(sem("q_sin"), 1)
                        dve.drain()
                        dve.tensor_tensor(QT[h % 2][64:96, :], QT[h % 2][64:96, :], KROPE[64:96, :], ALU.add)\
                           .then_inc(sem("q_out_dve"), 1)
                    dve.wait_ge(sem("s_mm"), U0 + i + 1)
                    dve.reduce_max(smx[:, i:i + 1], banks(2 * (i % 2), 2)[:, 0:nk], AX_X)
                    dve.drain()
                    dve.tensor_scalar(smn[:, i:i + 1], smx[:, i:i + 1], -MLA_SCALE, None, ALU.mult).then_inc(sem("smax"), 1)
                    if i >= 2:
                        finish(i - 2)
                dve.wait_ge(sem("p_ready"), U0 + len(units))
                finish(len(units) - 2)
                finish(len(units) - 1)
                meet(dve, who)

                for p in range(PAIRS):
                    dve.tensor_scalar(KK[:, p, :], K3[:, p, :], v("k_k")[:, p:p + 1], None, ALU.mult).then_inc(sem("kk_raw"), 1)
                for p in range(PAIRS):
                    dve.wait_ge(sem("kk_norm"), l * PAIRS + p + 1)
                    dve.tensor_scalar(GT[:, p, :], GT[:, p, :], 1e-12, None, ALU.max)
                dve.drain()
                for p in range(PAIRS):
                    dve.reciprocal(GT[:, p, :], GT[:, p, :])
                dve.drain()
                for p in range(PAIRS):
                    dve.tensor_tensor(KK[:, p, :], KK[:, p, :], GT[:, p, :], ALU.mult)
                for p in range(PAIRS):
                    dve.wait_ge(sem("vst_mm"), l * PAIRS + p + 1)
                    dve.tensor_copy(V3[:, p, :], banks(6 if p == 0 else 2 * (p - 1), 2)[:, 0:NTOK])\
                       .then_inc(sem("vst_out"), 1)
                dve.drain()
                for d in range(2):
                    dve.memset(FMS[0][d], 0.0)
                    dve.memset(FMS[1][d], 0.0)
                    dve.memset(ST[d], 0.0)
                    dve.memset(MA[d], 0.0)
                meet(dve, who)

                def low_decays(n, d):
                    dve.wait_ge(sem("gates_tanh"), count(l, n, d))
                    dve.tensor_scalar(LW[0:64, :], LW[0:64, :], 0.5, 0.5, ALU.mult, ALU.add).then_inc(sem("lw_ready"), 1)

                def factors(n, d, par, chunk, h):
                    tok, fm = bass.ds(chunk * CH, CH), FMS[par][d]
                    part, cols = slice(64 * h, 64 * h + 64), slice(64 * h, 64 * h + 64)
                    if h == 0:
                        dve.wait_ge(sem("decays_ready"), count(l, n, d))
                        dve.wait_ge(sem("kd_ready"), count(l, n, d))
                    dve.scalar_tensor_tensor(out=fm[part, :, 0, cols], in0=KK[part, :, tok], scalar=-1.0,
                                             in1=EX[part, :, 0, :], op0=ALU.mult, op1=ALU.mult)
                    dve.tensor_tensor(fm[part, :, 1, cols], EX[part, :, 1, :], R3[part, :, tok], ALU.mult)
                    dve.scalar_tensor_tensor(out=fm[part, :, 2, cols], in0=T2[part], scalar=0.5, in1=EN[part],
                                             op0=ALU.mult, op1=ALU.mult)
                    dve.tensor_tensor(fm[part, :, 3, cols], T1[part], EN[part], ALU.mult)
                    if h == 1:
                        end = (CH - 1, 0)[d]
                        dve.tensor_copy(wend[:, par, d, :], EX[:, :, 1, end:end + 1].rearrange("p q o -> p (q o)"))
                        dve.drain().then_inc(sem("fm_ready"), 1)

                def before(n, chunk):
                    for d in range(2):
                        low_decays(n, d)
                        for h in range(2):
                            factors(n, d, 0, chunk[d], h)

                def step(n, par, chunk, nxt):
                    FM = FMS[par]
                    for d in range(2):
                        dve.wait_ge(sem("a_mm"), count(l, n, d))
                        pa = psum[:, 3 * d:3 * d + 3, :]
                        pq = psum[:, 6 + d, 0:384].rearrange("p (q n) -> p q n", q=PAIRS)
                        dve.tensor_tensor(XT[d], pa[:, :, 0:128], level[:, d, 0].unsqueeze(1).to_broadcast([P, PAIRS, P]), ALU.mult)\
                           .then_inc(sem("xt_begun"), 1)
                        dve.tensor_tensor(MA[d][:, :, 0, :], pq, tri[:, 1 - d, 1].unsqueeze(1).to_broadcast([P, PAIRS, P]), ALU.mult)
                        dve.drain()
                        dve.tensor_tensor(XT[d], XT[d], ident.unsqueeze(1).to_broadcast([P, PAIRS, P]), ALU.add)\
                           .then_inc(sem("masked"), 1)
                    for j in range(1, LEVELS):
                        for d in range(2):
                            dve.wait_ge(sem("m_mm"), level_count(l, n, d, j))
                            dve.tensor_tensor(FM[d][:, :, 2, :], psum[:, 6 + d, 0:384].rearrange("p (q n) -> p q n", q=PAIRS),
                                              level[:, d, j].unsqueeze(1).to_broadcast([P, PAIRS, P]), ALU.mult)\
                               .then_inc(sem("m_ready"), 1)
                        if nxt and j == 3:
                            low_decays(n + 1, 0)
                        if nxt and j == 4:
                            factors(n + 1, 0, 1 - par, nxt[0], 0)
                        if nxt and j == 5:
                            low_decays(n + 1, 1)
                        for d in range(2):
                            dve.wait_ge(sem("x_mm"), level_count(l, n, d, j))
                            dve.tensor_tensor(XT[d], XT[d], psum[:, 3 * d + 2, 0:384].rearrange("p (q n) -> p q n", q=PAIRS), ALU.add)\
                               .then_inc(sem("x_ready"), 1)
                        if nxt and j == 4:
                            factors(n + 1, 0, 1 - par, nxt[0], 1)
                    if nxt:
                        for h in range(2):
                            factors(n + 1, 1, 1 - par, nxt[1], h)
                    for d in range(2):
                        dve.wait_ge(sem("scan_mm"), count(l, n, d))
                        dve.tensor_tensor(GB[d], ST[d], psum[:, 3 * d + 1, 192:384].rearrange("p (q n) -> p q n", q=PAIRS), ALU.add)
                        y = Y3[:, :, bass.ds(chunk[d] * CH, CH)]
                        dve.tensor_tensor(y, y, psum[:, 3 * d + 1, 0:192].rearrange("p (q n) -> p q n", q=PAIRS), ALU.add)
                        dve.drain()
                        dve.tensor_tensor(ST[d], GB[d], wend[:, par, d, :].unsqueeze(2).to_broadcast([P, PAIRS, HD]), ALU.mult)\
                           .then_inc(sem("state_ready"), 1)

                steps(dve, before, step)
                meet(dve, who)

                y4 = Y3.rearrange("p q (c n) -> p q c n", n=HD)
                s4 = SQ3.rearrange("p q (c n) -> p q c n", n=HD)
                v4 = V3.rearrange("p q (c n) -> p q c n", n=HD)
                st = [gstat[:, i, :].rearrange("p (q c) -> p q c", q=PAIRS) for i in range(2)]
                dve.tensor_reduce(st[0], y4, AX_X, ALU.add)
                dve.tensor_tensor(bonus[:, 0], bonus[:, 0], bonus[:, 1], ALU.add)
                dve.drain()
                dve.tensor_scalar(st[0], st[0], 1.0 / HD, None, ALU.mult)
                dve.drain()
                dve.tensor_tensor(y4, y4, st[0].unsqueeze(3).to_broadcast([P, PAIRS, NCH, HD]), ALU.subtract)\
                   .then_inc(sem("y_centred"), 1)
                for j in range(OUT_PIECES):
                    split_low(dve, G + IN_PIECES + j, HEAD_WL[j], HEAD_WH[j])
                dve.wait_ge(sem("y_sq"), l + 1)
                dve.tensor_reduce(st[1], s4, AX_X, ALU.add)
                dve.drain()
                dve.tensor_scalar(st[1], st[1], 1.0 / HD, GN_EPS, ALU.mult, ALU.add).then_inc(sem("y_var"), 1)
                dve.tensor_tensor(s4, v4, bonus[:, 0].unsqueeze(3).to_broadcast([P, PAIRS, NCH, HD]), ALU.mult)
                dve.wait_ge(sem("y_std"), l + 1)
                dve.reciprocal(gstat[:, 1, :], gstat[:, 1, :])
                dve.drain()
                dve.tensor_tensor(y4, y4, st[1].unsqueeze(3).to_broadcast([P, PAIRS, NCH, HD]), ALU.mult)
                dve.drain()
                dve.wait_ge(sem("lnx_loaded"), 16 * (l + 1))
                dve.tensor_tensor(y4, y4, LNX[:, 0].unsqueeze(2).to_broadcast([P, PAIRS, NCH, HD]), ALU.mult)
                dve.drain()
                dve.tensor_tensor(y4, y4, LNX[:, 1].unsqueeze(2).to_broadcast([P, PAIRS, NCH, HD]), ALU.add)
                dve.drain()
                dve.tensor_tensor(y4, y4, s4, ALU.add).then_inc(sem("y_done"), 1)
                for p in range(PAIRS):
                    dve.wait_ge(sem("gate_out"), l * PAIRS + p + 1)
                    dve.wait_ge(sem("y_turned"), l * PAIRS + p + 1)
                    b = 6 if p == 0 else 2 * (p - 1)
                    dve.tensor_tensor(Y3[:, p, :], banks(b, 2)[:, 0:NTOK], GT[:, p, :], ALU.mult)
                meet(dve, who)

                def gate_diagonals(gt):
                    for s in range(2 - l):
                        for k in range(KT):
                            ins = dve.tensor_scalar(DG[s][:, k * P:(k + 1) * P], ident, gt[:, k, s:s + 1], None, ALU.mult)
                        ins.then_inc(sem("gate_diag"), 1)

                live_cols = slice(LIVE[l][0] * P, NTOK)
                for k in range(KT):
                    dve.wait_ge(sem("mixed_high"), l * KT + k + 1)
                    dve.tensor_tensor(TOL[:, k, live_cols], TT[:, k, live_cols], TOH[:, k, live_cols], ALU.subtract)\
                       .then_inc(sem("mixed_low"), 1)
                gate_diagonals(gt_mix)
                dve.wait_ge(sem("gate_bc"), (2, 5)[l])
                for i, t in enumerate(LIVE[l]):
                    N = LIVE_SUM[l] + i + 1
                    dve.wait_ge(sem("out_ss"), N)
                    dve.tensor_scalar(ss[:, t:t + 1], ss[:, t:t + 1], 1.0 / D, EPS, ALU.mult, ALU.add).then_inc(sem("out_ms"), 1)
                    dve.wait_ge(sem("out_std"), N)
                    dve.reciprocal(rstd[:, t:t + 1], rstd[:, t:t + 1])
                    dve.drain()
                    dve.scalar_tensor_tensor(out=ZN[0], in0=banks(2 * (i % 2), 2), scalar=rstd[:, t:t + 1], in1=GBC[kind(t)],
                                             op0=ALU.mult, op1=ALU.mult).then_inc(sem("out_out"), 1)
                    dve.drain()
                    dve.tensor_tensor(X[:, t, :], X[:, t, :], ZN[0], ALU.add)
                meet(dve, who)

                dve.wait_ge(sem("ffn_ss"), LIVE_SUM[l + 1])
                dve.tensor_scalar(ss[:, 0:NT], ss[:, 0:NT], 1.0 / D, EPS, ALU.mult, ALU.add).then_inc(sem("ffn_ms"), 1)
                dve.wait_ge(sem("ffn_std"), l + 1)
                dve.reciprocal(rstd[:, 0:NT], rstd[:, 0:NT])
                dve.drain()
                gate_diagonals(gt_ffn)
                for i, t in enumerate(LIVE[l]):
                    dve.tensor_scalar(XH[:, t, :], X[:, t, :], rstd[:, t:t + 1], None, ALU.mult).then_inc(sem("xh_ready"), 1)
                dve.wait_ge(sem("wr_loaded"), 16 * (l + 1))
                for i, t in enumerate(LIVE[l]):
                    N = LIVE_SUM[l] + i + 1
                    dve.wait_ge(sem("router_mm"), N)
                    dve.reduce_max(rmx[:, t:t + 1], banks(2)[:, 0:NE], AX_X)
                    dve.drain()
                    dve.tensor_scalar(rmx[:, t:t + 1], rmx[:, t:t + 1], -1.0, None, ALU.mult).then_inc(sem("router_max"), 1)
                    dve.wait_ge(sem("router_exp"), N)
                    dve.reciprocal(rsm[:, t:t + 1], rsm[:, t:t + 1])
                    dve.drain()
                    dve.tensor_scalar(AFF[:, t, :], AFF[:, t, :], rsm[:, t:t + 1], None, ALU.mult).then_inc(sem("aff_ready"), 1)
                t0 = LIVE[l][0]
                dve.wait_ge(sem("aff_turned"), l + 1)
                dve.tensor_copy(AFT[0:NE, t0 * P:NTOK], banks(2, 2)[0:NE, t0 * P:NTOK])
                dve.drain()
                for a, b, cap in (() if l else ((0, CTX, CAP_C),)) + ((CTX, NTOK, CAP_X),):
                    src = AFT
                    for r in range(cap // TOP8):
                        dve.max(TOP[0:NE, :], src[0:NE, a:b])
                        dve.drain()
                        dve.match_replace(out=WORK[0:NE, a:b], in_to_replace=TOP[0:NE, :], in_values=src[0:NE, a:b], imm_value=-1.0)
                        dve.drain()
                        src = WORK
                dve.tensor_scalar(MASK[0:NE, t0 * P:NTOK], WORK[0:NE, t0 * P:NTOK], 0.0, None, ALU.is_lt)\
                   .then_inc(sem("mask_ready"), 1)
                dve.wait_ge(sem("mask_turned"), l + 1)
                dve.tensor_copy(MASKT[:, t0:NT, :], banks(0)[:, NE * t0:NE * NT].rearrange("p (t n) -> p t n", n=NE))\
                   .then_inc(sem("maskt_ready"), 1)
                dve.wait_ge(sem("count_mm"), l + 1)
                for t in LIVE[l]:
                    dve.scalar_tensor_tensor(out=SLOT[:, t, :], in0=banks(1)[:, NE * t:NE * t + NE],
                                             scalar=0.0, in1=MASKT[:, t, :], op0=ALU.add, op1=ALU.mult)
                dve.drain()
                dve.tensor_scalar(SLOT[:, t0:NT, :], SLOT[:, t0:NT, :], 1.0, None, ALU.subtract)
                meet(dve, who)

                live = LIVE[l]
                sl = SLOTS if l == 0 else CAP_X

                def gathered(group):
                    for k in range(KT):
                        dve.wait_ge(sem("xs_ready"), group * KT + (l * GROUPS * KT + k + 1))
                        parts = [(XSF[k % 2][:, 0:256].rearrange("p (e n) -> p e n", e=GROUP), 0, CAP_X)]
                        if l == 0:
                            parts.append((XSF[k % 2][:, 256:384].rearrange("p (e n) -> p e n", e=GROUP), CAP_X, SLOTS))
                        for src, a, b in parts:
                            dve.tensor_copy(XSH[:, k, :, a:b], src)
                        dve.drain()
                        for src, a, b in parts:
                            ins = dve.tensor_tensor(XSL[:, k, :, a:b], src, XSH[:, k, :, a:b], ALU.subtract)
                        ins.then_inc(sem("xs_split"), 1)

                def group_body(group):
                    def low(i):
                        split_low(dve, l * LAYER_PIECES + HEAD_PIECES + i, WL[i % 3], WH[i % 3], group)

                    def hidden(e, j):
                        if j % 2 == 0:
                            dve.wait_ge(sem("silu_ready"), group * (2 * GROUP) + (2 * l * NE + 2 * e + j // 2 + 1))
                        dve.wait_ge(sem("up_mm"), group * (4 * GROUP) + (4 * l * NE + 4 * e + j + 1))
                        hg = HG[0:sl, 256 * j:256 * j + 256]
                        dve.tensor_tensor(hg, hg, banks(4 + j % 2)[0:sl, 256 * (j // 2):256 * (j // 2) + 256], ALU.mult)\
                           .then_inc(sem("hidden_ready"), 1)

                    def turned(e, j):
                        dve.wait_ge(sem("ht_mm"), group * (4 * GROUP) + (4 * l * NE + 4 * e + j + 1))
                        src = banks(6 + j % 2)[:, 0:2 * SLOTS].rearrange("p (k n) -> p k n", k=2)[:, :, 0:sl]
                        dve.tensor_copy(HTH[:, 2 * j:2 * j + 2, 0:sl], src)
                        dve.drain()
                        dve.tensor_tensor(HTL[:, 2 * j:2 * j + 2, 0:sl], src, HTH[:, 2 * j:2 * j + 2, 0:sl], ALU.subtract)\
                           .then_inc(sem("ht_ready"), 1)

                    for e in range(GROUP):
                        i = e * EX_PIECES
                        for j in range(6):
                            low(i + j)
                        hidden(e, 0)
                        low(i + 6)
                        hidden(e, 1)
                        turned(e, 0)
                        low(i + 7)
                        hidden(e, 2)
                        turned(e, 1)
                        low(i + 8)
                        hidden(e, 3)
                        turned(e, 2)
                        low(i + 9)
                        low(i + 10)
                        turned(e, 3)
                        low(i + 11)

                def sums(group):
                    for i, t in enumerate(live):
                        for h in range(2):
                            m = 2 * i + h
                            dve.wait_ge(sem("scatter_mm"), group * (2 * len(live)) + (2 * GROUPS * LIVE_SUM[l] + m + 1))
                            ya = YA[:, t, 512 * h:512 * h + 512]
                            dve.tensor_tensor(ya, ya, banks(2 + m % 4), ALU.add).then_inc(sem("scatter_out"), 1)

                gathered(0)
                with dve.Fori(0, GROUPS - 1) as group:
                    group_body(group)
                    gathered(group + 1)
                    sums(group)
                group_body(GROUPS - 1)
                sums(GROUPS - 1)
                meet(dve, who)

                dve.wait_ge(sem("y_ss"), LIVE_SUM[l + 1])
                dve.tensor_scalar(ss[:, 0:NT], ss[:, 0:NT], 1.0 / D, EPS, ALU.mult, ALU.add).then_inc(sem("y_ms"), 1)
                dve.wait_ge(sem("ys_std"), l + 1)
                dve.reciprocal(rstd[:, 0:NT], rstd[:, 0:NT])
                dve.drain()
                for i, t in enumerate(live):
                    dve.scalar_tensor_tensor(out=YA[:, t, :], in0=YA[:, t, :], scalar=rstd[:, t:t + 1], in1=GBC[kind(t)],
                                             op0=ALU.mult, op1=ALU.mult)
                dve.drain()
                for i, t in enumerate(live):
                    dve.tensor_tensor(X[:, t, :], X[:, t, :], YA[:, t, :], ALU.add).then_inc(sem("ffn_out"), 1)
                meet(dve, who)

        @block.tensor
        def _(pe):
            who = "pe"

            def mm(dst, lhsT, rhs, start=True, stop=True):
                return pe.matmul(dst, lhsT, rhs, start=start, stop=stop)

            pe.wait_ge(sem("consts_loaded"), 16)
            pe.wait_ge(sem("c_split"), 1)
            for _ in range(3):
                pe.nop().then_inc(sem("w_used"), 1)

            def halves(j, k):
                return [w[j % 4].rearrange("p (k n) -> p k n", k=k) for w in (HEAD_WH, HEAD_WL)]

            for l in range(DEPTH):
                g = l * LAYER_PIECES

                def piece_split(j):
                    pe.wait_ge(sem("w_low"), g + j + 1)

                ROWS = MOD_PIECES // 2

                def turn_rows(b):
                    pe.wait_ge(sem("mod_row"), l * ROWS + b + 1)
                    for m in range(4 * b, 4 * b + 4):
                        ins = mm(banks(0)[:, 2 * m:2 * m + 2], MROW[0:4, m * P:(m + 1) * P], fold[0:4, :])
                    return ins

                for j in range(MOD_PIECES):
                    piece_split(j)
                    wh, wl = halves(j, KT)
                    b = j // 2
                    dst = banks(2 + b % 4)[0:4, 256 * (j % 2):256 * (j % 2) + 256]
                    if j % 2 == 0 and b >= 4:
                        pe.wait_ge(sem("mod_row"), l * ROWS + b - 3)
                    for k in range(KT):
                        mm(dst, cv_halves[:, k, :], wh[:, k, :], k == 0, False)
                        ins = mm(dst, cv_halves[:, k, :], wl[:, k, :], False, k == KT - 1)
                    ins.then_inc(sem("w_used"), 1)
                    if j % 2:
                        pe.drain().then_inc(sem("mod_mm"), 1)
                    elif b >= 2:
                        turn_rows(b - 2)
                turn_rows(ROWS - 2)
                turn_rows(ROWS - 1).then_inc(sem("mod_turned"), 1)
                meet(pe, who)

                for t in range(NT):
                    pe.wait_ge(sem("mix_normed"), l * NT + t + 1)
                    if t >= 4:
                        pe.wait_ge(sem("mix_out_act"), l * NT + t - 3)
                        pe.wait_ge(sem("mix_out_dve"), l * NT + t - 3)
                    dst = banks(2 * (t % 4), 2).rearrange("p (k n) -> p k n", k=KT)
                    for k in range(KT):
                        ins = pe.transpose(dst[:, k, :], ZN[t % 2][:, k * P:(k + 1) * P], ident)
                    ins.then_inc(sem("mix_turned"), 1)
                meet(pe, who)

                dve_chunks = [c for c in range(NCHUNK_IN) if c < C_LORA or c in (C_GD2, C_KR)]
                act_chunks = [c for c in range(C_LORA, NCHUNK_IN) if c != C_KR]
                for c in range(NCHUNK_IN):
                    if c % 2 == 0:
                        piece_split(MOD_PIECES + c // 2)
                    if c >= 4:
                        if c - 4 in dve_chunks:
                            pe.wait_ge(sem("in_out_dve"), l * len(dve_chunks) + dve_chunks.index(c - 4) + 1)
                        if c - 4 in act_chunks:
                            pe.wait_ge(sem("in_out_act"), l * len(act_chunks) + act_chunks.index(c - 4) + 1)
                    wh, wl = [w[:, :, (c % 2) * P:(c % 2 + 1) * P] for w in halves(MOD_PIECES + c // 2, KT)]
                    for a, n in SEGS:
                        dst = banks(2 * (c % 4), 2)[:, a:a + n]
                        for k in range(KT):
                            mm(dst, wh[:, k, :], TTH[:, k, a:a + n], k == 0, False)
                            mm(dst, wh[:, k, :], TTL[:, k, a:a + n], False, False)
                            ins = mm(dst, wl[:, k, :], TTH[:, k, a:a + n], False, k == KT - 1)
                    ins.then_inc(sem("in_mm"), 1)
                    if c % 2:
                        pe.drain().then_inc(sem("w_used"), 1)
                meet(pe, who)

                pe.wait_ge(sem("dft_loaded"), 32 * (l + 1))
                for t in range(NT):
                    dst = banks(t).rearrange("p (w q n) -> p w q n", w=2, q=2)
                    for q in range(2):
                        ins = mm(dst[:, :, q, :], F[:, q, t * P:(t + 1) * P], CS64.rearrange("p (w n) -> p w n", w=2))
                    ins.then_inc(sem("dft64_mm"), 1)
                pe.wait_ge(sem("dft64_out"), NT * (l + 1))
                for j in range(2):
                    dst = banks(2 * j, 2)
                    for a, b, c0, t_0, tabs in ((0, CTX, 0, 0, (C256, S256)), (CTX, 2 * CTX, 0, CT_TILES, (C512, S512)),
                                                (2 * CTX, 3 * CTX, CTX, CT_TILES, (C512, S512))):
                        nt = CT_TILES if t_0 == 0 else NT - CT_TILES
                        for w, tab in enumerate(tabs):
                            for t in range(nt):
                                ins = mm(dst[:, a:b], Y1[:, t_0 + t, 256 * w + j * P:256 * w + (j + 1) * P],
                                         tab[:, t, c0:c0 + CTX], w == 0 and t == 0, w == 1 and t == nt - 1)
                    ins.then_inc(sem("dft_mm"), 1)
                pe.wait_ge(sem("dft_out"), 2 * l + 2)
                for j in range(2):
                    for a, n in SEGS:
                        for k in range(2):
                            ins = mm(banks(4 + 2 * j, 2)[:, a:a + n], WF[:, k, j * P:(j + 1) * P], FO[:, k, a:a + n], k == 0, k == 1)
                    ins.then_inc(sem("wf_mm"), 1)
                meet(pe, who)

                pe.wait_ge(sem("mlaw_loaded"), 32 * (l + 1))
                pe.wait_ge(sem("lat_sq"), l + 1)
                for j, parts in ((0, QT), (1, KTH[:1])):
                    for a, n in SEGS:
                        for k, part in enumerate(parts):
                            ins = mm(banks(2 * j, 2)[:, a:a + n], ones, part[:, a:a + n], k == 0, k == len(parts) - 1)
                    ins.then_inc(sem("lat_ss"), 1)
                pe.wait_ge(sem("lat_normed"), l + 1)
                for t in range(NT):
                    if t >= 4:
                        pe.wait_ge(sem("v_out"), l * NT + t - 3)
                    mm(banks(4 + t % 4)[:, 0:RW], KVD[:, t * P:(t + 1) * P], WKV[:, RW:2 * RW]).then_inc(sem("v_mm"), 1)
                pe.wait_ge(sem("v_out"), l * NT + NT)
                units = [(h, q) for h in range(HEADS) for q in LIVE[l]]
                U0 = HEADS * LIVE_SUM[l]
                H0 = l * HEADS

                def project(h):
                    if h >= 1:
                        pe.wait_ge(sem("k_out_act"), H0 + h)
                    for a, n in SEGS:
                        for k in range(2):
                            ins = mm(banks(6, 2)[0:96, a:a + n], WQ[:, k, h * 96:(h + 1) * 96], QD[:, k, a:a + n], k == 0, k == 1)
                    ins.then_inc(sem("q_mm"), 1)
                    pe.wait_ge(sem("q_out_act"), H0 + h + 1)
                    pe.wait_ge(sem("q_cos"), H0 + h + 1)
                    for a, n in SEGS:
                        for k in range(2):
                            ins = mm(banks(6, 2)[64:96, a:a + n], WQ[:, k, 576 + h * 32:576 + (h + 1) * 32], QD[:, k, a:a + n],
                                     k == 0, k == 1)
                    ins.then_inc(sem("q_sw_mm"), 1)
                    for a, n in SEGS:
                        ins = mm(banks(6, 2)[0:64, a:a + n], WKV[:, h * HD:(h + 1) * HD], KVD[:, a:a + n])
                    ins.then_inc(sem("k_mm"), 1)
                    pe.wait_ge(sem("q_sin"), H0 + h + 1)

                def turn(i):
                    nk = (CTX if units[i][1] < CT_TILES else NTOK) // P
                    pe.wait_ge(sem("p_ready"), U0 + i + 1)
                    if i >= 1:
                        pe.wait_ge(sem("pt_ready"), U0 + i)
                    for k in range(nk):
                        ins = pe.transpose(banks(4, 2)[:, k * P:(k + 1) * P], PR[i % 2][:, k * P:(k + 1) * P], ident)
                    ins.then_inc(sem("p_turned"), 1)

                def values(i):
                    h, q = units[i]
                    nk = (CTX if q < CT_TILES else NTOK) // P
                    pe.wait_ge(sem("pt_ready"), U0 + i + 1)
                    if i >= 1:
                        pe.wait_ge(sem("o_ready"), U0 + i)
                    for k in range(nk):
                        ins = mm(banks(7)[:, 256:320], PT[i % 2][:, k, :],
                                 VT[:, k, h * HD:(h + 1) * HD], k == 0, k == nk - 1)
                    ins.then_inc(sem("pv_mm"), 1)

                for i, (h, q) in enumerate(units):
                    if q == LIVE[l][0]:
                        if i >= 3:
                            pe.wait_ge(sem("o_ready"), U0 + i - 2)
                        project(h)
                        pe.wait_ge(sem("q_out_dve"), H0 + h + 1)
                        pe.wait_ge(sem("k_out_act"), H0 + h + 1)
                    if i >= 2:
                        pe.wait_ge(sem("p_ready"), U0 + i - 1)
                    for a, n in (((0, CTX),) if q < CT_TILES else SEGS):
                        ins = mm(banks(2 * (i % 2), 2)[:, a:a + n], QT[h % 2][0:96, q * P:(q + 1) * P], KTH[h % 2][0:96, a:a + n])
                    ins.then_inc(sem("s_mm"), 1)
                    if i >= 1:
                        turn(i - 1)
                    if i >= 2:
                        values(i - 2)
                n = len(units)
                turn(n - 1)
                values(n - 2)
                values(n - 1)
                pe.wait_ge(sem("o_ready"), U0 + n)
                for i, q in enumerate(LIVE[l]):
                    for j in range(3):
                        ins = pe.transpose(banks(i)[:, j * P:(j + 1) * P], OQ[:, q, j * P:(j + 1) * P], ident)
                    ins.then_inc(sem("o_turned"), 1)
                meet(pe, who)

                for p in range(PAIRS):
                    pe.wait_ge(sem("kk_sq"), l * PAIRS + p + 1)
                    for a, n in SEGS:
                        ins = mm(banks(2 * p, 2)[:, a:a + n], headones, SQ3[:, p, a:a + n])
                    ins.then_inc(sem("kk_ss"), 1)
                for p in range(PAIRS):
                    b = 6 if p == 0 else 2 * (p - 1)
                    if p:
                        pe.wait_ge(sem("kk_norm"), l * PAIRS + p)
                    for c in range(NCH):
                        for h in range(2):
                            rows = slice(64 * h, 64 * h + 64)
                            ins = mm(banks(b, 2)[rows, c * CH:(c + 1) * CH], V3[rows, p, c * CH:(c + 1) * CH], ident2[rows, :])
                    ins.then_inc(sem("vst_mm"), 1)
                pe.nop().then_inc(sem("lc_used"), 1) if l == 0 else None
                meet(pe, who)

                def gates(n, d):
                    pe.wait_ge(sem("lc_ready"), count(l, n, d))
                    if not (isinstance(n, int) and n == 0 and d == 0):
                        pe.wait_ge(sem("kd_ready"), count(l, n, d) - 1)
                        pe.wait_ge(sem("decays_ready"), count(l, n, d) - 1)
                    for p in range(PAIRS):
                        mm(psum[:, 4 - 3 * d, p * CH:(p + 1) * CH], W2A2[64:128, d, p * P:(p + 1) * P], LC[64:128, :])
                    z = psum[0:64, 3 * d + 1, 0:RW]
                    mm(z, LC[0:64, :], W2A2[0:64, d, :], True, False)
                    row = 32 + 32 * d
                    mm(z, ones[row:row + 1, 0:64], G2W0[row:row + 1, 1, :], False, True).then_inc(sem("gates_mm"), 1)
                    pe.drain().then_inc(sem("lc_used"), 1)

                def decays(n, d):
                    pe.wait_ge(sem("lw_ready"), count(l, n, d))
                    for p in range(PAIRS):
                        ins = mm(psum[:, 3 * d + 1, 128 * p:128 * p + 128].rearrange("p (k n) -> p k n", k=2),
                                 LW[0:64, p * P:(p + 1) * P], tri[0:64, d, 1:3, 0:64])
                    ins.then_inc(sem("cum_mm"), 1)

                def before(n, chunk):
                    for d in range(2):
                        gates(n, d)
                        decays(n, d)

                def step(n, par, chunk, nxt):
                    FM = FMS[par]
                    first = isinstance(n, int) and n == 0
                    for d in range(2):
                        pe.wait_ge(sem("fm_ready"), count(l, n, d))
                        if not first:
                            pe.wait_ge(sem("state_ready"), count(l, n, d) - 2)
                        for p in range(PAIRS):
                            ar = FM[d][:, p, 0:2, :].rearrange("p k n -> p (k n)")
                            mm(psum[:, 3 * d + p, 0:256], FM[d][:, p, 2, :], ar)
                            mm(psum[:, 3 * d + p, 256:512], FM[d][:, p, 3, :], ar)
                            ins = mm(psum[:, 6 + d, p * P:(p + 1) * P], FM[d][:, p, 0, :], FM[d][:, p, 2, :])
                        ins.then_inc(sem("a_mm"), 1)
                    for d in range(2):
                        pe.wait_ge(sem("masked"), count(l, n, d))
                        pe.wait_ge(sem("a_copied"), count(l, n, d))
                        pe.wait_ge(sem("prd_ready"), count(l, n, d))
                        for w in range(2):
                            for p in range(PAIRS):
                                i = 3 * w + p
                                pe.transpose(psum[:, 3 * d + i // 4, (i % 4) * P:(i % 4 + 1) * P], FM[d][:, p, 2 + w, :], ident)
                        for p in range(PAIRS):
                            ins = mm(psum[:, 3 * d + 2, p:p + 1], BKT[d][:, 1, p, :], v("r_k")[:, p:p + 1])
                        ins.then_inc(sem("bk_turned"), 1)
                    for j in range(1, LEVELS):
                        for d in range(2):
                            if j > 1:
                                pe.wait_ge(sem("x_ready"), level_count(l, n, d, j - 1))
                            for p in range(PAIRS):
                                ins = mm(psum[:, 6 + d, p * P:(p + 1) * P], MA[d][:, p, 0, :], XT[d][:, p, :])
                            ins.then_inc(sem("m_mm"), 1)
                            if j == 1:
                                pe.wait_ge(sem("bkt_ready"), count(l, n, d))
                            for p in range(PAIRS):
                                ins = pe.transpose(psum[:, 3 * d, p * P:(p + 1) * P], XT[d][:, p, :], ident)
                            ins.then_inc(sem("xt_turned"), 1)
                        for d in range(2):
                            pe.wait_ge(sem("m_ready"), level_count(l, n, d, j))
                            pe.wait_ge(sem("xn_ready"), level_count(l, n, d, j))
                            for p in range(PAIRS):
                                ins = mm(psum[:, 3 * d + 2, p * P:(p + 1) * P], XN[d][:, p, :], FM[d][:, p, 2, :])
                            ins.then_inc(sem("x_mm"), 1)
                        if nxt:
                            if j == 1:
                                gates(n + 1, 0)
                            elif j == 3:
                                decays(n + 1, 0)
                            elif j == 4:
                                gates(n + 1, 1)
                            elif j == 5:
                                decays(n + 1, 1)
                    for d in range(2):
                        tok = bass.ds(chunk[d] * CH, CH)
                        pe.wait_ge(sem("x_ready"), level_count(l, n, d, LEVELS - 1))
                        pe.wait_ge(sem("a_masked"), count(l, n, d))
                        for p in range(PAIRS):
                            mm(psum[:, 6 + d, p * HD:(p + 1) * HD], FM[d][:, p, 0, :], ST[d][:, p, :], True, False)
                            ins = mm(psum[:, 6 + d, p * HD:(p + 1) * HD], MA[d][:, p, 2, :], V3[:, p, tok], False, True)
                        ins.then_inc(sem("g_mm"), 1)
                    for d in range(2):
                        pe.wait_ge(sem("g_ready"), count(l, n, d))
                        for p in range(PAIRS):
                            ins = mm(psum[:, 6 + d, 192 + p * HD:192 + (p + 1) * HD], XT[d][:, p, :], GB[d][:, p, :])
                        ins.then_inc(sem("u_mm"), 1)
                    if nxt:
                        pe.wait_ge(sem("decays_ready"), count(l, n + 1, 1))
                    for d in range(2):
                        tok = bass.ds(chunk[d] * CH, CH)
                        pe.wait_ge(sem("u_ready"), count(l, n, d))
                        for p in range(PAIRS):
                            y = psum[:, 3 * d + 1, p * HD:(p + 1) * HD]
                            mm(y, FM[d][:, p, 1, :], ST[d][:, p, :], True, False)
                            mm(y, MA[d][:, p, 1, :], UB[d][:, p, :], False, False)
                            mm(y, MA[d][:, p, 3, :], V3[:, p, tok], False, True)
                            s = psum[:, 3 * d + 1, 192 + p * HD:192 + (p + 1) * HD]
                            mm(s, BKT[d][:, 0, p, :], UB[d][:, p, :], True, False)
                            ins = mm(s, BKT[d][:, 1, p, :], V3[:, p, tok], False, True)
                        ins.then_inc(sem("scan_mm"), 1)

                steps(pe, before, step)
                meet(pe, who)

                for p in range(PAIRS):
                    for a, n in SEGS:
                        mm(banks(2 * p, 2)[:, a:a + n], G2W0[:, 0, p * P:(p + 1) * P], GD[:, 0, a:a + n], True, False)
                        ins = mm(banks(2 * p, 2)[:, a:a + n], G2W0[0:32, 1, p * P:(p + 1) * P], GD[0:32, 1, a:a + n], False, True)
                    ins.then_inc(sem("gate_mm"), 1)
                pe.wait_ge(sem("y_done"), l + 1)
                for p in range(PAIRS):
                    b = 6 if p == 0 else 2 * (p - 1)
                    if p:
                        pe.wait_ge(sem("gate_out"), l * PAIRS + p)
                    for c in range(NCH):
                        for h in range(2):
                            rows = slice(64 * h, 64 * h + 64)
                            ins = mm(banks(b, 2)[rows, c * CH:(c + 1) * CH], Y3[rows, p, c * CH:(c + 1) * CH], ident2[rows, :])
                    ins.then_inc(sem("y_turned"), 1)
                meet(pe, who)

                def gate_on_all(base):
                    for s in range(2 - l):
                        pe.wait_ge(sem("gate_diag"), base + s + 1)
                        for k in range(KT):
                            ins = mm(banks(4 + 2 * s, 2)[:, k * P:(k + 1) * P], ones, DG[s][:, k * P:(k + 1) * P])
                        ins.then_inc(sem("gate_bc_mm"), 1)

                for i, t in enumerate(LIVE[l]):
                    if i >= 2:
                        pe.wait_ge(sem("out_out"), LIVE_SUM[l] + i - 1)
                    for k in range(KT):
                        if i == 0:
                            pe.wait_ge(sem("mixed_low"), l * KT + k + 1)
                        wh, wl = [w[:, k % 2, :] for w in halves(k // 2, 2)]
                        for h in range(2):
                            dst, cols = banks(2 * (i % 2) + h), slice(512 * h, 512 * h + 512)
                            mm(dst, TOH[:, k, t * P:(t + 1) * P], wh[:, cols], k == 0, False)
                            mm(dst, TOH[:, k, t * P:(t + 1) * P], wl[:, cols], False, False)
                            ins = mm(dst, TOL[:, k, t * P:(t + 1) * P], wh[:, cols], False, k == KT - 1)
                    ins.then_inc(sem("out_mm"), 1)
                    if i == 0:
                        gate_on_all((0, 4)[l])
                for j in range(OUT_PIECES):
                    pe.drain().then_inc(sem("w_used"), 1)
                meet(pe, who)

                gate_on_all((2, 5)[l])
                for i, t in enumerate(LIVE[l]):
                    N = LIVE_SUM[l] + i + 1
                    pe.wait_ge(sem("xh_ready"), N)
                    if i >= 1:
                        pe.wait_ge(sem("tnt_ready"), N - 1)
                    for k in range(KT):
                        ins = pe.transpose(banks(0, 2)[:, k * P:(k + 1) * P], XH[:, t, k * P:(k + 1) * P], ident)
                    ins.then_inc(sem("ffn_turned"), 1)
                    pe.wait_ge(sem("tnt_ready"), N)
                    pe.wait_ge(sem("wr_loaded"), 16 * (l + 1))
                    if i >= 1:
                        pe.wait_ge(sem("router_exp"), N - 1)
                    for k in range(KT):
                        ins = mm(banks(2)[:, 0:NE], TNT[:, k, :], WR[:, k, :], k == 0, k == KT - 1)
                    ins.then_inc(sem("router_mm"), 1)
                pe.wait_ge(sem("aff_ready"), LIVE_SUM[l + 1])
                for t in LIVE[l]:
                    ins = pe.transpose(banks(2, 2)[0:NE, t * P:(t + 1) * P], AFF[:, t, :], ident)
                ins.then_inc(sem("aff_turned"), 1)
                pe.wait_ge(sem("mask_ready"), l + 1)
                for t in LIVE[l]:
                    ins = pe.transpose(banks(0)[:, NE * t:NE * t + NE], MASK[0:NE, t * P:(t + 1) * P], ident[0:NE, 0:NE])
                ins.then_inc(sem("mask_turned"), 1)
                pe.wait_ge(sem("maskt_ready"), l + 1)
                for t in LIVE[l]:
                    first = 0 if t < CT_TILES else CT_TILES
                    for u in range(first, t + 1):
                        ins = mm(banks(1)[:, NE * t:NE * t + NE], upto if u == t else ones, MASKT[:, u, :], u == first, u == t)
                ins.then_inc(sem("count_mm"), 1)
                for name, n in (("oh_used", 1), ("ov_used", 1), ("oe_used", 1), ("xs_split", 2 - 2 * l)):
                    for _ in range(n):
                        pe.nop().then_inc(sem(name), 1)
                meet(pe, who)

                live = LIVE[l]
                sl = SLOTS if l == 0 else CAP_X

                def gather(group):
                    pe.wait_ge(sem("oh_ready"), group + (l * GROUPS + 1))
                    for k in range(KT):
                        N = group * KT + (l * GROUPS * KT + k + 1)
                        if k >= 2:
                            pe.wait_ge(sem("xs_ready"), N - 2)
                        for t in range(CT_TILES, NT):
                            ins = mm(banks(6 + k % 2)[:, 0:256], XH[:, t, k * P:(k + 1) * P],
                                     OHX[:, t - CT_TILES].rearrange("p e n -> p (e n)"), t == CT_TILES, t == NT - 1)
                        if l == 0:
                            for t in range(CT_TILES):
                                ins = mm(banks(6 + k % 2)[:, 256:384], XH[:, t, k * P:(k + 1) * P],
                                         OHC[:, t].rearrange("p e n -> p (e n)"), t == 0, t == CT_TILES - 1)
                        ins.then_inc(sem("gather_mm"), 1)
                    pe.drain().then_inc(sem("oh_used"), 1)

                def group_body(group):
                    def piece(i):
                        pe.wait_ge(sem("w_low"), group * GROUP_PIECES + (l * LAYER_PIECES + HEAD_PIECES + i + 1))

                    def into(dst, i, j, e):
                        piece(i)
                        wh, wl = [w[i % 3].rearrange("p (k n) -> p k n", k=KT) for w in (WH, WL)]
                        for k in range(KT):
                            mm(dst, XSH[:, k, e, 0:sl], wh[:, k, :], k == 0, False)
                            mm(dst, XSH[:, k, e, 0:sl], wl[:, k, :], False, False)
                            ins = mm(dst, XSL[:, k, e, 0:sl], wh[:, k, :], False, k == KT - 1)
                        ins.then_inc(sem("w_used"), 1)

                    def turn(e, j):
                        pe.wait_ge(sem("hidden_ready"), group * (4 * GROUP) + (4 * l * NE + 4 * e + j + 1))
                        if j >= 2:
                            pe.wait_ge(sem("ht_ready"), group * (4 * GROUP) + (4 * l * NE + 4 * e + j - 1))
                        for c in range(2):
                            ins = pe.transpose(banks(6 + j % 2)[:, c * SLOTS:(c + 1) * SLOTS],
                                               HG[0:SLOTS, (2 * j + c) * P:(2 * j + c + 1) * P], ident[0:SLOTS, 0:SLOTS])
                        ins.then_inc(sem("ht_mm"), 1)

                    def down(i, j, e):
                        piece(i)
                        pe.wait_ge(sem("ht_ready"), group * (4 * GROUP) + (4 * l * NE + 4 * e + j + 1))
                        wh, wl = [w[i % 3].rearrange("p (k n) -> p k n", k=2) for w in (WH, WL)]
                        for c in range(2):
                            k = 2 * j + c
                            for h in range(2):
                                dst, cols = banks(h)[0:sl, :], slice(512 * h, 512 * h + 512)
                                mm(dst, HTH[:, k, 0:sl], wh[:, c, cols], k == 0, False)
                                mm(dst, HTH[:, k, 0:sl], wl[:, c, cols], False, False)
                                ins = mm(dst, HTL[:, k, 0:sl], wh[:, c, cols], False, k == KT - 1)
                        ins.then_inc(sem("w_used"), 1)

                    for e in range(GROUP):
                        i = e * EX_PIECES
                        if e == 1:
                            pe.wait_ge(sem("ov_ready"), group + (l * GROUPS + 1))
                            for u in range(2):
                                for t in range(4):
                                    ins = pe.transpose(banks(6 + u)[:, t * P:(t + 1) * P],
                                                       OVX[:, t, 2 * u:2 * u + 2, :].rearrange("p e n -> p (e n)"), ident)
                            ins.then_inc(sem("ovtx_mm"), 1)
                            pe.wait_ge(sem("ovt_ready"), group * (2 - l) + (l * 2 * GROUPS + 1))
                        if e == 2 and l == 0:
                            for t in range(CT_TILES):
                                ins = pe.transpose(banks(6)[:, t * P:(t + 1) * P], OVC[:, t].rearrange("p e n -> p (e n)"), ident)
                            ins.then_inc(sem("ovtc_mm"), 1)
                        if e == 2:
                            pe.drain().then_inc(sem("ov_used"), 1)
                            if l == 0:
                                pe.wait_ge(sem("ovt_ready"), group * 2 + 2)
                        for j in range(4):
                            into(banks(2 + j // 2)[0:sl, 256 * (j % 2):256 * (j % 2) + 256], i + j, j, e)
                            if j % 2:
                                pe.drain().then_inc(sem("expert_gate_mm"), 1)
                        for j in range(4):
                            if j >= 2:
                                pe.wait_ge(sem("hidden_ready"), group * (4 * GROUP) + (4 * l * NE + 4 * e + j - 1))
                            into(banks(4 + j % 2)[0:sl, 256 * (j // 2):256 * (j // 2) + 256], i + 4 + j, j, e)
                            pe.drain().then_inc(sem("up_mm"), 1)
                            if j:
                                turn(e, j - 1)
                        if e:
                            pe.wait_ge(sem("oe_ready"), group * GROUP + (l * NE + e))
                        down(i + 8, 0, e)
                        down(i + 9, 1, e)
                        turn(e, 3)
                        down(i + 10, 2, e)
                        down(i + 11, 3, e)
                        pe.drain().then_inc(sem("down_mm"), 1)

                def scatter(group):
                    pe.wait_ge(sem("oe_ready"), group * GROUP + (l * NE + GROUP))
                    for i, t in enumerate(live):
                        for h in range(2):
                            m = 2 * i + h
                            if m >= 4:
                                pe.wait_ge(sem("scatter_out"), group * (2 * len(live)) + (2 * GROUPS * LIVE_SUM[l] + m - 3))
                            cols = slice(512 * h, 512 * h + 512)
                            if t < CT_TILES:
                                ins = mm(banks(2 + m % 4), OVTC[:, t * P:(t + 1) * P], OEC[:, cols])
                            else:
                                for u in range(2):
                                    ins = mm(banks(2 + m % 4), OVTX[:, u, (t - CT_TILES) * P:(t - CT_TILES + 1) * P],
                                             OEX[:, u, cols], u == 0, u == 1)
                            ins.then_inc(sem("scatter_mm"), 1)
                    pe.drain().then_inc(sem("oe_used"), 1)
                    pe.wait_ge(sem("scatter_out"), group * (2 * len(live)) + (2 * GROUPS * LIVE_SUM[l] + 2 * len(live)))

                gather(0)
                with pe.Fori(0, GROUPS - 1) as group:
                    group_body(group)
                    gather(group + 1)
                    scatter(group)
                group_body(GROUPS - 1)
                scatter(GROUPS - 1)
                meet(pe, who)
                meet(pe, who)


def shape_constants(np):
    i = np.arange(P)
    same = (i[:, None] // 64) == (i[None, :] // 64)
    before = [same & (i[:, None] < i[None, :]), same & (i[:, None] > i[None, :])]
    tri = [np.stack([b | np.eye(P, dtype=bool), b, b | np.eye(P, dtype=bool)]) for b in before]
    lev = []
    for b in before:
        for j in range(LEVELS):
            m = 2 ** j
            lev.append(b & (i[:, None] // (2 * m) == i[None, :] // (2 * m)) & (i[:, None] // m != i[None, :] // m))
    cols = [np.eye(P), np.ones((P, P)), same, np.concatenate([t.transpose(1, 0, 2).reshape(P, -1) for t in tri], 1),
            i[:, None] <= i[None, :], np.tile(np.eye(64), (2, 1)), np.tile(np.arange(CAP_X), (P, 1)),
            np.stack(lev).transpose(1, 0, 2).reshape(P, -1), np.tile(np.eye(2), (P // 2, 1))]
    consts = np.concatenate([np.asarray(c, np.float32) for c in cols], 1)
    assert consts.shape == (P, NCONST)

    def dft(n, scale):
        a = 2 * np.pi * (np.outer(np.arange(n), np.arange(n)) % n) / n
        return np.cos(a) * scale, np.sin(a) * scale

    def tiles(a):
        return a.reshape(-1, P, a.shape[1]).transpose(1, 0, 2).reshape(P, -1)

    c5, s5 = dft(SEQ, (SEQ * 64) ** -0.5)
    c2, s2 = dft(CTX, (CTX * 64) ** -0.5)
    c6, s6 = dft(64, 1.0)
    two = np.zeros((P, 2, P))
    for h in range(2):
        two[64 * h:64 * h + 64, 0, 64 * h:64 * h + 64] = c6
        two[64 * h:64 * h + 64, 1, 64 * h:64 * h + 64] = s6
    tables = np.concatenate([tiles(c5), tiles(-s5), tiles(c2), tiles(-s2), two.reshape(P, -1)], 1).astype(np.float32)

    inv = (np.float32(10000.0) ** (-np.arange(8, dtype=np.float32) / np.float32(8))).astype(np.float32)
    pos = np.arange(SEQ)
    rope = np.zeros((P, 2, NTOK), np.float32)
    rope[64:96, 0, :CTX] = 1.0
    for half, q in enumerate((pos // 64, pos % 64)):
        ang = (q.astype(np.float32)[None, :] * inv[:, None]).astype(np.float32)
        for part in range(2):
            r = 64 + 16 * half + 8 * part
            rope[r:r + 8, 0, CTX:] = np.cos(ang)
            rope[r:r + 8, 1, CTX:] = np.sin(ang) * (1 if part else -1)
    return consts, tables, rope.reshape(P, -1)


def kernel(**inputs):
    import numpy as np
    import concourse.bacc as bacc
    from concourse.bass_utils import run_bass_kernel_spmd as run

    a = {k: np.asarray(x) for k, x in inputs.items()}
    consts, tables, rope = shape_constants(np)

    def cols(x):
        return x.reshape(DEPTH, -1, P).transpose(0, 2, 1)

    cvec = np.stack([a["c"].reshape(KT, P).T, a["c_ctx"].reshape(KT, P).T], 2)
    vecs = np.concatenate([
        cols(a["b_mod"]), cols(a["g_pre_mix"]), cols(a["g_pre_ffn"]), cols(a["g_post_mix"]), cols(a["g_post_ffn"]),
        cols(a["conv_rkv"]), cols(a["rwkv_k_k"]), cols(a["rwkv_k_a"]), cols(a["rwkv_r_k"].reshape(DEPTH, -1)),
        cols(a["rwkv_a0"]), cols(a["mla_g_q"]), cols(a["mla_g_kv"])], 2)
    swap = np.concatenate([np.arange(8, 16), np.arange(0, 8), np.arange(24, 32), np.arange(16, 24)])
    w = a["w_in"]
    o_gd, o_q, o_kr, o_f = 3 * RW + 128, 3 * RW + 128 + GATE_LORA, 3 * RW + 128 + GATE_LORA + 384, 3 * RW + 128 + GATE_LORA + 416
    z = lambda n: np.zeros((DEPTH, D, n), np.float32)
    kr = w[:, :, o_kr:o_kr + 32]
    w_in = np.concatenate([w[:, :, 0:o_gd + GATE_LORA], z(32), kr[:, :, swap], z(32),
                           w[:, :, o_q:o_kr], z(64), kr, z(32), w[:, :, o_f:]], 2)
    assert w_in.shape[2] == NCHUNK_IN * P
    lora = np.concatenate([a["rwkv_w2"], a["rwkv_a2"]], 2).transpose(0, 2, 1, 3).reshape(DEPTH, P, 768)
    g2w0 = np.zeros((DEPTH, P, 2, RW), np.float32)
    g2w0[:, :, 0] = a["rwkv_g2"][:, :P]
    g2w0[:, 0:32, 1] = a["rwkv_g2"][:, P:]
    g2w0[:, 32, 1] = a["rwkv_w0"][:, 0]
    g2w0[:, 64, 1] = a["rwkv_w0"][:, 1]
    ln = np.stack([a["rwkv_lnx_w"], a["rwkv_lnx_b"]], 1).reshape(DEPTH, 2, PAIRS, 2, HD)
    lnx = np.repeat(ln.transpose(0, 3, 1, 2, 4).reshape(DEPTH, 2, -1), 64, axis=1)
    q6 = a["mla_w_qup"].reshape(DEPTH, 256, HEADS, 96)
    w_q = np.concatenate([a["mla_w_qup"], q6[:, :, :, 64:][:, :, :, swap].reshape(DEPTH, 256, 192)], 2)
    kv6 = a["mla_w_kvup"].reshape(DEPTH, P, HEADS, 2, HD)
    w_kv = kv6.transpose(0, 1, 3, 2, 4).reshape(DEPTH, P, 768)
    arrays = {
        "x_in": a["x"][0], "ctx_in": a["ctx"][0], "cvec": cvec, "consts": consts, "dft": tables, "rope": rope, "vecs": vecs,
        "w_mod": a["w_mod"], "w_in": w_in, "w_out": a["w_out"], "lora": lora, "g2w0": g2w0.reshape(DEPTH, P, -1),
        "lnx": lnx, "w_q": w_q, "w_kv": w_kv, "w_f": a["w_fourier"], "w_r": a["w_router"],
        "w_eg": a["w_expert_gate"].reshape(DEPTH * NE, D, FF), "w_eu": a["w_expert_up"].reshape(DEPTH * NE, D, FF),
        "w_ed": a["w_expert_down"].reshape(DEPTH * NE, FF, D),
    }
    nc = bacc.Bacc("TRN2", target_bir_lowering=False, num_devices=1)
    args, sent = [], {}
    for name, x in arrays.items():
        sent[f"{name}_dram"] = np.ascontiguousarray(x)
        args.append(nc.dram_tensor(f"{name}_dram", x.shape, F32, kind="ExternalInput").ap())
    out = nc.dram_tensor("out_dram", (SEQ, D), F32, kind="ExternalOutput").ap()
    hybrid_layers(nc, *args, out)
    r = run(nc, [sent], core_ids=[0])
    return r.results[0]["out_dram"].reshape(1, SEQ, D)
```

```python
from contextlib import ExitStack

import concourse.bass as bass
from concourse import mybir

F32 = mybir.dt.float32
BF16 = mybir.dt.bfloat16
ALU = mybir.AluOpType
ACT = mybir.ActivationFunctionType
AX_X = mybir.AxisListType.X

P = 128
D = 1024
KT = D // P
SEQ, CTX = 512, 256
NTOK = SEQ + CTX
NT = NTOK // P
CT_TILES = CTX // P
DEPTH = 2
EPS = 1e-6
HD = 64
HEADS = 6
PAIRS = HEADS // 2
RW = HEADS * HD
GN_EPS = 64e-5
GATE_LORA = 160
MLA_SCALE = 96.0 ** -0.5
NE = 16
FF = 1024
CAP_X = 2 * SEQ // NE
CAP_C = 2 * CTX // NE
SLOTS = CAP_X + CAP_C
DECAY = 0.6065306597126334
CH = 64
NCH = NTOK // CH
NCH_C = CTX // CH
LEVELS = 6

C_LORA, C_GD, C_GD2, C_QD, C_KVD, C_KR, C_F = 9, 10, 11, 12, 14, 15, 16
NCHUNK_IN = 18
MOD_PIECES, IN_PIECES, OUT_PIECES, EX_PIECES = 24, 9, 4, 12
HEAD_PIECES = MOD_PIECES + IN_PIECES + OUT_PIECES
LAYER_PIECES = HEAD_PIECES + NE * EX_PIECES
RING = 4
MOD_EARLY = 4
GROUP = 4
GROUPS = NE // GROUP
GROUP_PIECES = GROUP * EX_PIECES

CONST = {}
_at = 0
for _name, _n in (("ident", P), ("ones", P), ("headones", P), ("tri", 2 * 3 * P), ("upto", P), ("ident2", HD),
                  ("iota", CAP_X), ("level", 2 * LEVELS * P), ("fold", 2), ("zero", 1)):
    CONST[_name] = (_at, _at + _n)
    _at += _n
NCONST = _at

VEC = {}
_at = 0
for _name, _n in (("b_mod", 48), ("g_pre_mix", 8), ("g_pre_ffn", 8), ("g_post_mix", 8), ("g_post_ffn", 8),
                  ("conv", 27), ("k_k", 3), ("k_a", 3), ("r_k", 3), ("a0", 6), ("g_q", 2), ("g_kv", 1)):
    VEC[_name] = (_at, _at + _n)
    _at += _n
NVEC = _at

SCR = 19900
PROJ = 3840
S_QD, S_KVD, S_KROPE, S_F = 0, 1536, 2304, 3072
S_TAB = SCR - 1536
TOP8 = 8


def hybrid_layers(nc, x_in, ctx_in, cvec, consts, dft, rope, vecs, w_mod, w_in, w_out, lora, g2w0, lnx, w_q, w_kv,
                  w_f, w_r, w_eg, w_eu, w_ed, out):
    with ExitStack() as ctx:
        def sb(name, shape):
            return ctx.enter_context(nc.sbuf_tensor(name, shape, F32))

        sems = {}

        def sem(name):
            if name not in sems:
                sems[name] = ctx.enter_context(nc.semaphore(name))
            return sems[name]

        ring = sb("ring", [P, RING, 2048])
        X = sb("X", [P, NT, D])
        T = sb("T", [P, NT * D])
        U = sb("U", [P, 12, NTOK])
        cst = sb("cst", [P, NCONST])
        vec = sb("vec", [P, NVEC])
        cv = sb("cv", [P, KT, 2])
        cv_halves = ctx.enter_context(nc.sbuf_tensor("cv_halves", [P, KT, 4], BF16))
        modc = sb("modc", [P, 48, 2])
        sc_mix = sb("sc_mix", [P, KT, 2])
        sc_ffn = sb("sc_ffn", [P, KT, 2])
        gt_mix = sb("gt_mix", [P, KT, 2])
        gt_ffn = sb("gt_ffn", [P, KT, 2])
        half_a0 = sb("half_a0", [P, 6])
        ss = sb("ss", [P, 8])
        rstd = sb("rstd", [P, 8])
        scr = sb("scr", [P, SCR])
        psum = ctx.enter_context(nc.psum_tensor("psum", [P, 8, 512], F32))

        def const(name):
            return cst[:, CONST[name][0]:CONST[name][1]]

        def v(name):
            return vec[:, VEC[name][0]:VEC[name][1]]

        ident, ones, headones = const("ident"), const("ones"), const("headones")
        tri = const("tri").rearrange("p (d k n) -> p d k n", d=2, k=3)
        upto, ident2, iota = const("upto"), const("ident2"), const("iota")
        fold, zero = const("fold"), const("zero")
        level = const("level").rearrange("p (d j n) -> p d j n", d=2, j=LEVELS)

        def banks(b, n=1):
            return psum[:, b:b + n, :].rearrange("p b n -> p (b n)")

        def area(at, n):
            return scr[:, at:at + n]

        TT = T[:, :].rearrange("p (k n) -> p k n", k=KT)
        YA = T[:, :].rearrange("p (t n) -> p t n", t=NT)
        SEGS = ((0, 512), (512, 256))
        SEQS = ((0, CTX), (CTX, NTOK))
        LIVE = (tuple(range(NT)), tuple(range(CT_TILES, NT)))
        LIVE_SUM = (0, NT, NT + NT - CT_TILES)
        SHARES = [[range(m, min(m + 2 * len(live) // 3 + (len(live) % 3 > 0), 2 * len(live)))
                   for m in range(0, 2 * len(live), 2 * len(live) // 3 + (len(live) % 3 > 0))] for live in LIVE]

        def split_high(act, g, buffer, group=0, free=False):
            piece_ready(act, g, group)
            if not free:
                act.wait_ge(sem("w_used"), group * GROUP_PIECES + (g + 1))
            act.activation(buffer, ring[:, g % RING, :], ACT.Copy).then_inc(sem("w_high"), 1)

        def split_low(dve, g, buffer, high, group=0):
            dve.wait_ge(sem("w_high"), group * GROUP_PIECES + (g + 1))
            dve.tensor_tensor(buffer, ring[:, g % RING, :], high, ALU.subtract).then_inc(sem("w_low"), 1)

        def in_columns(l, c):
            return CTX if l == DEPTH - 1 and c in (C_GD, C_QD, C_QD + 1, C_F, C_F + 1) else 0

        def kind(t):
            return 1 if t < CT_TILES else 0

        phase = {"pe": 0, "act": 0, "dve": 0, "pool": 0}

        def meet(eng, who):
            phase[who] += 1
            eng.drain().then_inc(sem("phase_over"), 1)
            eng.wait_ge(sem("phase_over"), 4 * phase[who])

        def small_loads(l, upto):
            return 16 * (10 * l + {"vec": 1, "rope": 2, "dft": 3, "w_f": 4, "mlaw": 6, "rww": 8, "lnx": 9, "wr": 10}[upto])

        def piece_ready(eng, g, group=0):
            eng.wait_ge(sem(f"ring_loaded{g % RING}"), group * (16 * GROUP_PIECES // RING) + 16 * (g // RING + 1))

        MROW = area(0, 6144)
        HEAD_WH = [area(S_TAB - 8192 + 1024 * i, 1024).bitcast(BF16) for i in range(4)]
        HEAD_WL = [area(S_TAB - 4096 + 1024 * i, 1024).bitcast(BF16) for i in range(4)]
        TTH = T[:, 0:3072].bitcast(BF16).rearrange("p (k n) -> p k n", k=KT)
        TTL = T[:, 3072:6144].bitcast(BF16).rearrange("p (k n) -> p k n", k=KT)
        ZM = [area(2048 + 1024 * i, 1024).rearrange("p (k n) -> p k n", k=KT) for i in range(3)]
        TOH, TOL = [U[:, 4 * i:4 * i + 4, :].rearrange("p a n -> p (a n)").bitcast(BF16).rearrange("p (k n) -> p k n", k=KT)
                    for i in range(2)]
        QD = area(S_QD, 1536).rearrange("p (c n) -> p c n", c=2)
        KVD = area(S_KVD, 768)
        KROPE = area(S_KROPE, 768)
        F = area(S_F, 1536).rearrange("p (c n) -> p c n", c=2)
        COS, SIN = area(S_TAB, 768), area(S_TAB + 768, 768)
        C512 = area(4608, 2048).rearrange("p (t n) -> p t n", t=4)
        S512 = area(6656, 2048).rearrange("p (t n) -> p t n", t=4)
        C256 = area(8704, 512).rearrange("p (t n) -> p t n", t=2)
        S256 = area(9216, 512).rearrange("p (t n) -> p t n", t=2)
        CS64 = area(9728, 256)
        WF = area(9984, 512).rearrange("p (k n) -> p k n", k=2)
        Y1 = area(10496, 3072).rearrange("p (t n) -> p t n", t=NT)
        FO = T[:, 0:1536].rearrange("p (c n) -> p c n", c=2)
        WQ = area(3072, 1536).rearrange("p (k n) -> p k n", k=2)
        WKV = area(4608, 768)
        QT = [area(5376, 768), area(6144, 768)]
        KTH = [area(6912, 768), area(7680, 768)]
        PR = [area(8448, 768), area(9216, 768)]
        PT = [area(9984, 768).rearrange("p (k n) -> p k n", k=NT), area(10752, 768).rearrange("p (k n) -> p k n", k=NT)]
        OQ = area(11520, 2304).rearrange("p (t n) -> p t n", t=NT)
        smx = area(13824, 48)
        smn = area(13872, 48)
        ssum = area(13920, 48)
        sinv = area(13968, 48)
        VT = T[:, 0:2304].rearrange("p (t n) -> p t n", t=NT)
        R3, K3, V3 = U[:, 0:3, :], U[:, 3:6, :], U[:, 6:9, :]
        LOR = U[:, C_LORA, :]
        GD = U[:, C_GD:C_GD + 2, :]
        Y3 = T[:, 0:2304].rearrange("p (q n) -> p q n", q=PAIRS)
        at = 0

        def take(n):
            nonlocal at
            at += n
            return area(at - n, n)

        W2A2 = take(768).rearrange("p (d n) -> p d n", d=2)
        G2W0 = take(768).rearrange("p (d n) -> p d n", d=2)
        KK = take(2304).rearrange("p (q n) -> p q n", q=PAIRS)
        FMS = [[take(1536).rearrange("p (q k n) -> p q k n", q=PAIRS, k=4) for _ in range(2)] for _ in range(2)]
        MA = [take(1536).rearrange("p (q k n) -> p q k n", q=PAIRS, k=4) for _ in range(2)]
        XT = [take(384).rearrange("p (q n) -> p q n", q=PAIRS) for _ in range(2)]
        XN = [take(384).rearrange("p (q n) -> p q n", q=PAIRS) for _ in range(2)]
        BKT = [take(768).rearrange("p (k q n) -> p k q n", k=2, q=PAIRS) for _ in range(2)]
        GB = [take(192).rearrange("p (q n) -> p q n", q=PAIRS) for _ in range(2)]
        UB = [take(192).rearrange("p (q n) -> p q n", q=PAIRS) for _ in range(2)]
        ST = [take(192).rearrange("p (q n) -> p q n", q=PAIRS) for _ in range(2)]
        LC = take(64)
        LW = take(384)
        AA = take(192).rearrange("p (q n) -> p q n", q=PAIRS)
        EX = take(384).rearrange("p (q k n) -> p q k n", q=PAIRS, k=2)
        EN = take(192).rearrange("p (q n) -> p q n", q=PAIRS)
        T1 = take(192).rearrange("p (q n) -> p q n", q=PAIRS)
        T2 = take(192).rearrange("p (q n) -> p q n", q=PAIRS)
        assert at <= SCR
        wend = sb("wend", [P, 2, 2, PAIRS])
        half_ka = sb("half_ka", [P, PAIRS])
        rest_ka = sb("rest_ka", [P, PAIRS])
        bonus = sb("bonus", [P, 2, PAIRS, NCH])
        gstat = sb("gstat", [P, 2, PAIRS * NCH])
        SQ3 = scr[:, 4224:4224 + 2304].rearrange("p (q n) -> p q n", q=PAIRS)
        GT = scr[:, 6528:6528 + 2304].rearrange("p (q n) -> p q n", q=PAIRS)
        VB = scr[:, 1536:1536 + 2304].rearrange("p (q n) -> p q n", q=PAIRS)
        LNX = area(8832, 384).rearrange("p (w q n) -> p w q n", w=2, q=PAIRS)
        GBC = [U[:, 8:12, :].rearrange("p a n -> p (a n)")[:, 1024 * s:1024 * s + 1024] for s in range(2)]
        ZN = [area(0, 1024), area(1024, 1024)]
        DG = [area(2048, 1024), area(3072, 1024)]
        BIN = U[:, 0:8, :].rearrange("p a n -> p (a n)").rearrange("p (t n) -> p t n", t=NT)
        XT_N = [area(6912 + 1024 * i, 1024) for i in range(3)]
        XHH, XHL = [U[:, 4 * i:4 * i + 4, :].rearrange("p a n -> p (a n)").bitcast(BF16)
                    .rearrange("p (t n) -> p t n", t=NT) for i in range(2)]
        TNT = [area(1024 * i, 1024).rearrange("p (k n) -> p k n", k=KT) for i in range(2)]
        WR = area(4096, 128).rearrange("p (k n) -> p k n", k=KT)
        AFF = area(4224, 96).rearrange("p (t n) -> p t n", t=NT)
        AFT = area(4320, 768)
        WORK = area(5088, 768)
        MASK = area(5856, 768)
        MASKT = area(6624, 96).rearrange("p (t n) -> p t n", t=NT)
        SLOT = area(6720, 96).rearrange("p (t n) -> p t n", t=NT)
        TOP = area(6816, 8)
        rmx, rsm = area(6824, 8), area(6832, 8)
        SLOT_OWN = area(6840, 24).rearrange("p (t e) -> p t e", t=NT)
        AFF_OWN = area(6864, 24).rearrange("p (t e) -> p t e", t=NT)
        SLOT_NXT = area(6888, 24).rearrange("p (t e) -> p t e", t=NT)
        OHX = area(6912, 512).bitcast(BF16).rearrange("p (t e n) -> p t e n", t=4, e=GROUP)
        OHC = area(7424, 128).bitcast(BF16).rearrange("p (t e n) -> p t e n", t=2, e=GROUP)
        OVX = area(8192, 1024).rearrange("p (t e n) -> p t e n", t=4, e=GROUP)
        OVC = area(9216, 256).rearrange("p (t e n) -> p t e n", t=2, e=GROUP)
        OVTFX = area(9472, 1024).rearrange("p (u n) -> p u n", u=2)
        OVTFC = area(10496, 256)
        OVTX = area(7552, 512).bitcast(BF16).rearrange("p (u n) -> p u n", u=2)
        OVTC = area(8064, 128).bitcast(BF16)
        slot_aff = area(19456, 3)
        XSF = [area(a, 384).rearrange("p (e n) -> p e n", e=GROUP) for a in (10752, 11136, 19460)]
        XSH, XSL = [area(11520 + 1536 * i, 1536).bitcast(BF16).rearrange("p (k e n) -> p k e n", k=KT, e=GROUP)
                    for i in range(2)]
        HTH, HTL = [area(14592 + 384 * i, 384).bitcast(BF16).rearrange("p (k n) -> p k n", k=KT) for i in range(2)]
        OE = [area(0, 1024), area(9472, 1024), area(2048, 1024)]
        OEH = [area(a, 512).bitcast(BF16) for a in (1024, 0, 5344)]
        OEL = [area(a, 512).bitcast(BF16) for a in (1536, 512, 5856)]
        HG = U[:, 8:12, :].rearrange("p a n -> p (a n)")[:, 2048:3072]
        WH = [area(a, 1024).bitcast(BF16) for a in (15360, 16384, 3072)]
        WL = [area(a, 1024).bitcast(BF16) for a in (17408, 18432, 4320)]

        def steps(eng, before, step):
            def chunks(n, latent):
                return n, n * -1 + (NCH_C + NCH - 1 if latent else NCH_C - 1)

            before(0, chunks(0, False))
            for n in range(NCH_C):
                step(n, n % 2, chunks(n, False), chunks(n + 1, n + 1 >= NCH_C))
            with eng.Fori(NCH_C, NCH - 2, 2) as n:
                step(n, 0, chunks(n, True), chunks(n + 1, True))
                step(n + 1, 1, chunks(n + 1, True), chunks(n + 2, True))
            step(NCH - 2, 0, chunks(NCH - 2, True), chunks(NCH - 1, True))
            step(NCH - 1, 1, chunks(NCH - 1, True), None)

        def output_needed(l, n):
            return l < DEPTH - 1 or not isinstance(n, int) or n >= NCH_C

        def count(l, n, d):
            return n * 2 + (2 * NCH * l + d + 1)

        def level_count(l, n, d, j):
            return n * (2 * (LEVELS - 1)) + (2 * NCH * l * (LEVELS - 1) + 2 * (j - 1) + d + 1)

        block = ctx.enter_context(nc.Block())

        @block.sync
        def _(sp):
            sp.dma_start(cv[:, :, :], cvec).then_inc(sem("c_loaded"), 16)
            sp.dma_start(cst[:, :], consts).then_inc(sem("consts_loaded"), 16)
            for t in range(NT):
                src = ctx_in[t * P:(t + 1) * P, :] if t < CT_TILES else x_in[(t - CT_TILES) * P:(t - CT_TILES + 1) * P, :]
                sp.dma_start(X[:, t, :], src).then_inc(sem("x_loaded"), 16)

            def load(g, src, k, n, group=0):
                dst = ring[:, g % RING, 0:k * n].rearrange("p (k n) -> p k n", k=k)
                sp.dma_start(dst, src).then_inc(sem(f"ring_loaded{g % RING}"), 16)

            def load_expert(l, i, group):
                g = l * LAYER_PIECES + HEAD_PIECES + i
                e, j = (i % GROUP_PIECES) // EX_PIECES, i % EX_PIECES
                first = l * NE + GROUP * (i // GROUP_PIECES) + e
                at = bass.ds(group * GROUP + first, 1)
                w = (w_eg, w_eu, w_ed)[j // 4]
                src = w[at, :, :].rearrange("e (k p) n -> p (e k) n", p=P)
                if j < 8:
                    load(g, src[:, :, 256 * (j % 4):256 * (j % 4) + 256], KT, 256)
                else:
                    load(g, src[:, 2 * (j - 8):2 * (j - 8) + 2, :], 2, D)

            for l in range(DEPTH):
                for j in range(HEAD_PIECES):
                    g = l * LAYER_PIECES + j
                    if g >= RING:
                        sp.wait_ge(sem("w_low"), g - RING + 1)
                    if j < MOD_PIECES:
                        load(g, w_mod[l].rearrange("(k p) n -> p k n", p=P)[:, :, 256 * j:256 * j + 256], KT, 256)
                    elif j < MOD_PIECES + IN_PIECES:
                        i = j - MOD_PIECES
                        load(g, w_in[l].rearrange("(k p) n -> p k n", p=P)[:, :, 256 * i:256 * i + 256], KT, 256)
                    else:
                        i = j - MOD_PIECES - IN_PIECES
                        load(g, w_out[l].rearrange("(k p) n -> p k n", p=P)[:, 2 * i:2 * i + 2, :], 2, D)
                for i in range(RING):
                    sp.wait_ge(sem("w_low"), l * LAYER_PIECES + HEAD_PIECES - RING + i + 1)
                    load_expert(l, i, 0)
                with sp.Fori(0, GROUPS - 1) as group:
                    for i in range(GROUP_PIECES):
                        sp.wait_ge(sem("w_low"), group * GROUP_PIECES + (l * LAYER_PIECES + HEAD_PIECES + i + 1))
                        load_expert(l, i + RING, group)
                for i in range(GROUP_PIECES - RING):
                    sp.wait_ge(sem("w_low"), (GROUPS - 1) * GROUP_PIECES + (l * LAYER_PIECES + HEAD_PIECES + i + 1))
                    load_expert(l, i + RING, GROUPS - 1)
            for i, t in enumerate(LIVE[1]):
                sp.wait_ge(sem("ffn_out"), LIVE_SUM[1] + i + 1)
                sp.dma_start(out[(t - CT_TILES) * P:(t - CT_TILES + 1) * P, :], X[:, t, :]).then_inc(sem("stored"), 16)
            sp.wait_ge(sem("stored"), 16 * len(LIVE[1]))

        @block.gpsimd
        def _(pool):
            who = "pool"
            for l in range(DEPTH):
                pool.dma_start(vec[:, :], vecs[l]).then_inc(sem("small_loaded"), 16)
                pool.wait_ge(sem("small_loaded"), small_loads(l, "vec"))
                meet(pool, who)
                pool.dma_start(area(S_TAB, 1536), rope).then_inc(sem("small_loaded"), 16)
                pool.wait_ge(sem("small_loaded"), small_loads(l, "rope"))
                for t in range(NT):
                    pool.wait_ge(sem("mix_high"), l * NT + t + 1)
                    cols = slice(t * P, (t + 1) * P)
                    pool.tensor_tensor(TTL[:, :, cols], ZM[t % 3], TTH[:, :, cols], ALU.subtract).then_inc(sem("mix_low"), 1)
                meet(pool, who)
                pool.dma_start(area(4608, 5376), dft).then_inc(sem("small_loaded"), 16)
                pool.wait_ge(sem("small_loaded"), small_loads(l, "dft"))
                meet(pool, who)
                pool.dma_start(WF, w_f[l].rearrange("(k p) n -> p k n", p=P)).then_inc(sem("small_loaded"), 16)
                pool.wait_ge(sem("small_loaded"), small_loads(l, "w_f"))
                meet(pool, who)
                pool.dma_start(WQ, w_q[l].rearrange("(k p) n -> p k n", p=P)).then_inc(sem("small_loaded"), 16)
                pool.dma_start(WKV, w_kv[l]).then_inc(sem("small_loaded"), 16)
                pool.wait_ge(sem("small_loaded"), small_loads(l, "mlaw"))
                meet(pool, who)
                pool.dma_start(area(0, 768), lora[l]).then_inc(sem("small_loaded"), 16)
                pool.dma_start(area(768, 768), g2w0[l]).then_inc(sem("small_loaded"), 16)
                pool.memset(Y3, 0.0)
                for d in range(2):
                    pool.memset(ST[d], 0.0)
                    pool.memset(MA[d], 0.0)
                pool.wait_ge(sem("small_loaded"), small_loads(l, "rww"))
                meet(pool, who)

                def prepare(n, d, chunk):
                    tok = bass.ds(chunk * CH, CH)
                    pool.wait_ge(sem("gates_tanh"), count(l, n, d))
                    if not (isinstance(n, int) and n == 0 and d == 0):
                        pool.wait_ge(sem("fm_ready"), count(l, n, d) - 1)
                    pool.tensor_tensor(T2, AA, ones[:, 0:HD].unsqueeze(1).to_broadcast([P, PAIRS, HD]), ALU.add)
                    for p in range(PAIRS):
                        pool.tensor_scalar(T1[:, p, :], AA[:, p, :], half_ka[:, p:p + 1], rest_ka[:, p:p + 1], ALU.mult, ALU.add)
                    pool.drain()
                    pool.tensor_tensor(T1, T1, K3[:, :, tok], ALU.mult)
                    pool.tensor_tensor(T2, T2, KK[:, :, tok], ALU.mult)
                    pool.drain().then_inc(sem("kd_ready"), 1)

                def before(n, chunk):
                    for d in range(2):
                        prepare(n, d, chunk[d])

                def step(n, par, chunk, nxt):
                    for d in range(2):
                        pool.wait_ge(sem("fm_ready"), count(l, n, d))
                        if not (isinstance(n, int) and n == 0):
                            pool.wait_ge(sem("scan_mm"), count(l, n, d) - 2)
                        pool.tensor_tensor(BKT[d][:, 1], FMS[par][d][:, :, 1, :], FMS[par][d][:, :, 3, :], ALU.mult)\
                            .then_inc(sem("prd_ready"), 1)
                    for d in range(2):
                        pool.wait_ge(sem("a_copied"), count(l, n, d))
                        pool.tensor_tensor(MA[d][:, :, 1:4, :], MA[d][:, :, 1:4, :],
                                           tri[:, d].unsqueeze(1).to_broadcast([P, PAIRS, 3, P]), ALU.mult)\
                            .then_inc(sem("a_masked"), 1)
                    if nxt:
                        before(n + 1, nxt)

                steps(pool, before, step)
                meet(pool, who)
                pool.dma_start(area(8832, 384), lnx[l]).then_inc(sem("small_loaded"), 16)
                pool.tensor_tensor(bonus[:, 0], bonus[:, 0], bonus[:, 1], ALU.add)
                pool.drain()
                vb = VB.rearrange("p q (c n) -> p q c n", n=HD)
                pool.tensor_tensor(vb, V3.rearrange("p q (c n) -> p q c n", n=HD),
                                   bonus[:, 0].unsqueeze(3).to_broadcast([P, PAIRS, NCH, HD]), ALU.mult)
                pool.wait_ge(sem("small_loaded"), small_loads(l, "lnx"))
                pool.drain()
                pool.tensor_tensor(vb, vb, LNX[:, 1].unsqueeze(2).to_broadcast([P, PAIRS, NCH, HD]), ALU.add)\
                    .then_inc(sem("vb_ready"), 1)
                meet(pool, who)
                meet(pool, who)
                pool.dma_start(WR, w_r[l].rearrange("(k p) n -> p k n", p=P)).then_inc(sem("small_loaded"), 16)
                for i, t in enumerate(LIVE[l]):
                    pool.wait_ge(sem("xh_high"), LIVE_SUM[l] + i + 1)
                    pool.tensor_tensor(XHL[:, t, :], XT_N[i % 3], XHH[:, t, :], ALU.subtract).then_inc(sem("xh_low"), 1)
                pool.memset(T[:, :], 0.0)
                pool.wait_ge(sem("small_loaded"), small_loads(l, "wr"))
                meet(pool, who)

                def one_hot(t, e, slots, x, c, aff=None):
                    col = slots[:, t, e:e + 1]
                    dst = c[:, t, e, :] if t < CT_TILES else x[:, t - CT_TILES, e, :]
                    src = iota[:, 0:CAP_C] if t < CT_TILES else iota
                    if aff is None:
                        return pool.tensor_scalar(dst, src, col, None, ALU.is_equal)
                    return pool.tensor_scalar(dst, src, col, aff[:, t, e:e + 1], ALU.is_equal, ALU.mult)

                def one_hots_to_gather(group):
                    pool.wait_ge(sem("oh_used"), group + l * (GROUPS + 1) + 1)
                    pool.tensor_copy(SLOT_NXT[:, LIVE[l][0]:NT, :], SLOT[:, LIVE[l][0]:NT, bass.ds(group * GROUP, GROUP)])
                    pool.drain()
                    for t in LIVE[l]:
                        for e in range(GROUP):
                            one_hot(t, e, SLOT_NXT, OHX, OHC)
                    pool.drain().then_inc(sem("oh_ready"), 1)

                def one_hots_to_scatter(group):
                    pool.wait_ge(sem("ov_used"), group + l * (GROUPS + 1) + 1)
                    pool.tensor_copy(SLOT_OWN[:, LIVE[l][0]:NT, :], SLOT[:, LIVE[l][0]:NT, bass.ds(group * GROUP, GROUP)])
                    pool.tensor_copy(AFF_OWN[:, LIVE[l][0]:NT, :], AFF[:, LIVE[l][0]:NT, bass.ds(group * GROUP, GROUP)])
                    pool.drain()
                    for t in LIVE[l]:
                        for e in range(GROUP):
                            one_hot(t, e, SLOT_OWN, OVX, OVC, AFF_OWN)
                    pool.drain().then_inc(sem("ov_ready"), 1)

                def ones_of_transposed(group):
                    pool.wait_ge(sem("ovt_ready"), group + (l * GROUPS + 1))
                    pool.tensor_tensor(OVTX, OVTFX, zero.unsqueeze(1).to_broadcast([P, 2, SEQ]), ALU.add)
                    if l == 0:
                        pool.tensor_scalar(OVTC, OVTFC, 0.0, None, ALU.is_gt)
                    pool.drain()
                    pool.tensor_scalar(OVTX, OVTX, 0.0, None, ALU.is_gt)
                    pool.drain().then_inc(sem("ovt_ones"), 1)

                def gathered(group):
                    n = SLOTS if l == 0 else CAP_X
                    for k in range(KT):
                        pool.wait_ge(sem("xs_ready"), group * KT + (l * GROUPS * KT + k + 1))
                        pool.tensor_tensor(XSH[:, k, :, 0:n], XSF[k % 3][:, :, 0:n],
                                           zero.unsqueeze(1).to_broadcast([P, GROUP, n]), ALU.add)\
                            .then_inc(sem("xs_high"), 1)

                one_hots_to_gather(0)
                gathered(0)
                with pool.Fori(0, GROUPS - 1) as group:
                    one_hots_to_scatter(group)
                    ones_of_transposed(group)
                    one_hots_to_gather(group + 1)
                    gathered(group + 1)
                one_hots_to_scatter(GROUPS - 1)
                ones_of_transposed(GROUPS - 1)
                meet(pool, who)

        @block.scalar
        def _(act):
            who = "act"

            def modulate(l, j):
                split_high(act, l * LAYER_PIECES + j, HEAD_WH[j % 4])
                if j % 2 and j >= 3:
                    act.wait_ge(sem("mod_mm"), (MOD_PIECES // 2) * l + (j - 1) // 2)
                    b = (j - 3) // 2
                    act.activation(MROW[0:4, 512 * b:512 * b + 512], banks(2 + b % 4)[0:4, :], ACT.Copy)\
                       .then_inc(sem("mod_row"), 1)

            for l in range(DEPTH):
                if l == 0:
                    act.wait_ge(sem("c_loaded"), 16)
                    act.activation(cv[:, :, :], cv[:, :, :], ACT.Silu)
                    act.drain()
                    act.activation(cv_halves[:, :, 0:2], cv[:, :, :], ACT.Copy).then_inc(sem("silu_c"), 1)
                G = l * LAYER_PIECES
                for j in range(MOD_PIECES):
                    if l == 0 or j >= MOD_EARLY:
                        modulate(l, j)
                    if j % 2 == 0 and 4 <= j < 4 + 2 * NT:
                        t = (j - 4) // 2
                        if l == 0:
                            act.wait_ge(sem("x_loaded"), 16 * NT)
                        else:
                            act.wait_ge(sem("ffn_out"), t + 1)
                        act.activation(T[:, t * D:(t + 1) * D], X[:, t, :], ACT.Square, accum_out=ss[:, t:t + 1])\
                           .then_inc(sem("mix_ss"), 1)
                act.wait_ge(sem("mod_mm"), (MOD_PIECES // 2) * (l + 1))
                b = MOD_PIECES // 2 - 1
                act.activation(MROW[0:4, 512 * b:512 * b + 512], banks(2 + b % 4)[0:4, :], ACT.Copy).then_inc(sem("mod_row"), 1)
                act.wait_ge(sem("mix_ms"), l + 1)
                act.activation(rstd[:, 0:NT], ss[:, 0:NT], ACT.Sqrt).then_inc(sem("mix_std"), 1)
                meet(act, who)

                def mixed_high(t):
                    act.wait_ge(sem("mix_out_act"), l * NT + t + 1)
                    act.wait_ge(sem("mix_out_dve"), l * NT + t + 1)
                    act.activation(TTH[:, :, t * P:(t + 1) * P], ZM[t % 3], ACT.Copy).then_inc(sem("mix_high"), 1)

                G += MOD_PIECES
                for t in range(NT):
                    if t in (1, 3):
                        split_high(act, G + t // 2, HEAD_WH[(MOD_PIECES + t // 2) % 4])
                    act.wait_ge(sem("mix_turned"), l * NT + t + 1)
                    if t >= 3:
                        act.wait_ge(sem("mix_low"), l * NT + t - 2)
                    src = banks(2 * (t % 4), 2).rearrange("p (k n) -> p k n", k=KT)
                    for k in range(KT // 2, KT):
                        ins = act.activation(ZM[t % 3][:, k, :], src[:, k, :], ACT.Identity,
                                             bias=modc[:, k, kind(t):kind(t) + 1], scale=sc_mix[:, k, kind(t):kind(t) + 1])
                    ins.then_inc(sem("mix_out_act"), 1)
                    if t:
                        mixed_high(t - 1)
                mixed_high(NT - 1)
                meet(act, who)

                for c in range(NCHUNK_IN):
                    if c % 2 == 0 and c // 2 + 2 < IN_PIECES:
                        split_high(act, G + c // 2 + 2, HEAD_WH[(MOD_PIECES + c // 2 + 2) % 4])
                    if c < C_LORA or c == C_KR:
                        continue
                    act.wait_ge(sem("in_mm"), l * NCHUNK_IN + c + 1)
                    if c == NCHUNK_IN - 1:
                        act.wait_ge(sem("in_out_dve"), 11 * (l + 1))
                    src = banks(2 * (c % 4), 2)[:, 0:NTOK]
                    if c == C_LORA:
                        act.activation(LOR[0:64, :], src[0:64, :], ACT.Tanh)
                        ins = act.activation(LOR[64:128, :], src[64:128, :], ACT.Copy)
                    elif c == C_GD:
                        ins = act.activation(GD[:, 0, :], src, ACT.Tanh, scale=0.5)
                    elif c == C_GD2:
                        ins = act.activation(GD[0:32, 1, :], src[0:32, :], ACT.Tanh, scale=0.5)
                    elif c < C_KVD:
                        ins = act.activation(QD[:, c - C_QD, :], src, ACT.Copy)
                    elif c == C_KVD:
                        ins = act.activation(KVD, src, ACT.Copy)
                    else:
                        ins = act.activation(F[:, c - C_F, :], src, ACT.Copy)
                    ins.then_inc(sem("in_out_act"), 1)
                meet(act, who)

                for t in range(NT):
                    act.wait_ge(sem("dft64_mm"), l * NT + t + 1)
                    act.activation(Y1[:, t, :], banks(t), ACT.Copy).then_inc(sem("dft64_out"), 1)
                for j in range(2):
                    act.wait_ge(sem("dft_mm"), 2 * l + j + 1)
                    act.activation(FO[:, j, :], banks(2 * j, 2)[:, 0:NTOK], ACT.Copy).then_inc(sem("dft_out"), 1)
                for j in range(2):
                    act.wait_ge(sem("wf_mm"), 2 * l + j + 1)
                    act.activation(TT[:, 6 + j, :], banks(4 + 2 * j, 2)[:, 0:NTOK], ACT.Copy)
                meet(act, who)

                for j in range(2):
                    act.activation(QT[j], QD[:, j, :], ACT.Square)
                act.activation(KTH[0], KVD, ACT.Square).then_inc(sem("lat_sq"), 1)
                act.wait_ge(sem("lat_ms"), l + 1)
                act.activation(PR[0], PR[0], ACT.Sqrt)
                act.activation(PR[1], PR[1], ACT.Sqrt).then_inc(sem("lat_std"), 1)

                def projected(h, r):
                    act.wait_ge(sem("proj_mm"), 4 * (l * HEADS + h) + r + 1)
                    (a, n), dst = SEGS[r % 2], (QT, KTH)[r // 2][h % 2]
                    act.activation(dst[0:64, a:a + n], banks(6)[0:64, 0:n], ACT.Copy).then_inc(sem("proj_out_act"), 1)

                for t in range(NT):
                    act.wait_ge(sem("v_mm"), l * NT + t + 1)
                    act.activation(VT[:, t, :], banks(t % 4)[:, 0:RW], ACT.Copy).then_inc(sem("v_out"), 1)
                    if t >= 3:
                        projected(0, t - 3)
                projected(0, 3)
                units = [(h, q) for h in range(HEADS) for q in LIVE[l]]
                U0 = HEADS * LIVE_SUM[l]
                for i, (h, q) in enumerate(units):
                    nk = CTX if q < CT_TILES else NTOK
                    if i % len(LIVE[l]) < 4 and h + 1 < HEADS:
                        projected(h + 1, i % len(LIVE[l]))
                    act.wait_ge(sem("smax"), U0 + i + 1)
                    if i >= 2:
                        act.wait_ge(sem("p_turned"), U0 + i - 1)
                    act.activation(PR[i % 2][:, 0:nk], banks(2 * (i % 2), 2)[:, 0:nk], ACT.Exp, bias=smn[:, i:i + 1],
                                   scale=MLA_SCALE, accum_out=ssum[:, i:i + 1]).then_inc(sem("p_ready"), 1)
                    if i >= 1:
                        act.wait_ge(sem("p_turned"), U0 + i)
                        if i >= 3:
                            act.wait_ge(sem("pv_mm"), U0 + i - 2)
                        m = CTX if units[i - 1][1] < CT_TILES else NTOK
                        act.activation(PT[(i - 1) % 2].rearrange("p k n -> p (k n)")[:, 0:m], banks(4, 2)[:, 0:m],
                                       ACT.Copy).then_inc(sem("pt_ready"), 1)
                i = len(units)
                act.wait_ge(sem("p_turned"), U0 + i)
                act.wait_ge(sem("pv_mm"), U0 + i - 2)
                act.activation(PT[(i - 1) % 2].rearrange("p k n -> p (k n)"), banks(4, 2)[:, 0:NTOK], ACT.Copy)\
                   .then_inc(sem("pt_ready"), 1)
                for i, q in enumerate(LIVE[l]):
                    act.wait_ge(sem("o_turned"), LIVE_SUM[l] + i + 1)
                    act.activation(TT[:, 3:6, q * P:(q + 1) * P], banks(i)[:, 0:RW].rearrange("p (j n) -> p j n", j=3),
                                   ACT.Copy)
                meet(act, who)

                for p in range(PAIRS):
                    act.wait_ge(sem("kk_raw"), l * PAIRS + p + 1)
                    act.activation(SQ3[:, p, :], KK[:, p, :], ACT.Square).then_inc(sem("kk_sq"), 1)
                for p in range(PAIRS):
                    act.wait_ge(sem("kk_ss"), l * PAIRS + p + 1)
                    act.activation(GT[:, p, :], banks(2 * p, 2)[:, 0:NTOK], ACT.Sqrt).then_inc(sem("kk_norm"), 1)
                meet(act, who)

                def chunk_in(n, d, chunk):
                    act.wait_ge(sem("lc_used"), count(l, n, d))
                    act.activation(LC, LOR[:, bass.ds(chunk * CH, CH)], ACT.Copy).then_inc(sem("lc_ready"), 1)

                def gates(n, d):
                    act.wait_ge(sem("gates_mm"), count(l, n, d))
                    act.activation(LW[0:64, :], psum[0:64, 3 * d + 1, 0:RW], ACT.Tanh, scale=0.5)
                    for p in range(PAIRS):
                        ins = act.activation(AA[:, p, :], psum[:, 4 - 3 * d, p * CH:(p + 1) * CH], ACT.Tanh, scale=0.5,
                                             bias=half_a0[:, 3 * d + p:3 * d + p + 1])
                    ins.then_inc(sem("gates_tanh"), 1)

                def decays(n, d):
                    act.wait_ge(sem("cum_mm"), count(l, n, d))
                    cum = psum[:, 3 * d + 1, 0:384].rearrange("p (q k n) -> p q k n", q=PAIRS, k=2)
                    act.activation(EX, cum, ACT.Exp, scale=-DECAY)
                    act.activation(EN, cum[:, :, 1, :], ACT.Exp, scale=DECAY).then_inc(sem("decays_ready"), 1)

                def before(n, chunk):
                    for d in range(2):
                        chunk_in(n, d, chunk[d])
                        gates(n, d)
                        decays(n, d)

                def step(n, par, chunk, nxt):
                    for d in range(2):
                        act.wait_ge(sem("xt_begun"), count(l, n, d))
                        act.activation(MA[d][:, :, 1:4, :], psum[:, 3 * d:3 * d + 3, 128:512].rearrange("p q (k n) -> p q k n", k=3),
                                       ACT.Copy).then_inc(sem("a_copied"), 1)
                    for d in range(2):
                        act.wait_ge(sem("bk_turned"), count(l, n, d))
                        act.activation(BKT[d].rearrange("p k q n -> p (k q n)"), banks(3 * d, 2)[:, 0:768], ACT.Copy)
                        act.activation(bonus[:, d, :, bass.ds(chunk[d], 1)], psum[:, 3 * d + 2, 0:PAIRS].unsqueeze(2), ACT.Copy)\
                           .then_inc(sem("bkt_ready"), 1)
                    for j in range(1, LEVELS):
                        if nxt and j == 4:
                            decays(n + 1, 0)
                            chunk_in(n + 1, 1, nxt[1])
                        for d in range(2):
                            act.wait_ge(sem("xt_turned"), level_count(l, n, d, j))
                            act.activation(XN[d].rearrange("p q n -> p (q n)"), psum[:, 3 * d, 0:384], ACT.Copy)\
                               .then_inc(sem("xn_ready"), 1)
                        if nxt and j == 1:
                            chunk_in(n + 1, 0, nxt[0])
                        elif nxt and j == 2:
                            gates(n + 1, 0)
                        elif nxt and j == 5:
                            gates(n + 1, 1)
                            decays(n + 1, 1)
                    for d in range(2):
                        act.wait_ge(sem("g_mm"), count(l, n, d))
                        act.activation(GB[d].rearrange("p q n -> p (q n)"), psum[:, 6 + d, 0:192], ACT.Copy)\
                           .then_inc(sem("g_ready"), 1)
                    for d in range(2):
                        act.wait_ge(sem("u_mm"), count(l, n, d))
                        act.activation(UB[d].rearrange("p q n -> p (q n)"), psum[:, 6 + d, 192:384], ACT.Copy)\
                           .then_inc(sem("u_ready"), 1)

                steps(act, before, step)
                meet(act, who)

                G += IN_PIECES
                split_high(act, G, HEAD_WH[0], free=True)
                for p in range(PAIRS):
                    act.wait_ge(sem("y_centred"), l * PAIRS + p + 1)
                    act.activation(SQ3[:, p, :], Y3[:, p, :], ACT.Square).then_inc(sem("y_sq"), 1)
                split_high(act, G + 1, HEAD_WH[1], free=True)
                act.wait_ge(sem("y_var"), l + 1)
                act.activation(gstat[:, 1, :], gstat[:, 1, :], ACT.Sqrt).then_inc(sem("y_std"), 1)
                for j in range(2, OUT_PIECES):
                    split_high(act, G + j, HEAD_WH[j], free=True)
                for p in range(PAIRS):
                    act.wait_ge(sem("gate_mm"), l * PAIRS + p + 1)
                    act.activation(GT[:, p, :], banks(2 * p, 2)[:, 0:NTOK], ACT.Copy).then_inc(sem("gate_out"), 1)
                meet(act, who)

                live_cols = slice(LIVE[l][0] * P, NTOK)
                for k in range(KT):
                    act.activation(TOH[:, k, live_cols], TT[:, k, live_cols], ACT.Copy).then_inc(sem("mixed_high"), 1)
                for s in range(2 - l):
                    act.wait_ge(sem("gate_bc_mm"), (0, 4)[l] + s + 1)
                    act.activation(GBC[s], banks(4 + 2 * s, 2), ACT.Copy).then_inc(sem("gate_bc"), 1)
                for i, t in enumerate(LIVE[l]):
                    N = LIVE_SUM[l] + i + 1
                    act.wait_ge(sem("out_mm"), N)
                    act.activation(DG[0], banks(2 * (i % 2), 2), ACT.Square, accum_out=ss[:, t:t + 1]).then_inc(sem("out_ss"), 1)
                    act.wait_ge(sem("out_ms"), N)
                    act.activation(rstd[:, t:t + 1], ss[:, t:t + 1], ACT.Sqrt).then_inc(sem("out_std"), 1)
                meet(act, who)

                for i, t in enumerate(LIVE[l]):
                    act.activation(BIN[:, t, :], X[:, t, :], ACT.Square, accum_out=ss[:, t:t + 1]).then_inc(sem("ffn_ss"), 1)
                act.wait_ge(sem("ffn_ms"), l + 1)
                act.activation(rstd[:, 0:NT], ss[:, 0:NT], ACT.Sqrt).then_inc(sem("ffn_std"), 1)

                def router_exp(i):
                    t = LIVE[l][i]
                    act.wait_ge(sem("router_max"), LIVE_SUM[l] + i + 1)
                    act.activation(AFF[:, t, :], banks(2 + i % 2)[:, 0:NE], ACT.Exp, bias=rmx[:, t:t + 1],
                                   accum_out=rsm[:, t:t + 1]).then_inc(sem("router_exp"), 1)

                for i, t in enumerate(LIVE[l]):
                    N = LIVE_SUM[l] + i + 1
                    act.wait_ge(sem("xh_ready"), N)
                    act.activation(XHH[:, t, :], XT_N[i % 3], ACT.Copy).then_inc(sem("xh_high"), 1)
                    act.wait_ge(sem("ffn_turned"), N)
                    if i >= 2:
                        act.wait_ge(sem("router_mm"), N - 2)
                    src = banks((0, 6)[i % 2], 2).rearrange("p (k n) -> p k n", k=KT)
                    for k in range(KT):
                        ins = act.activation(TNT[i % 2][:, k, :], src[:, k, :], ACT.Identity,
                                             bias=modc[:, 24 + k, kind(t):kind(t) + 1],
                                             scale=sc_ffn[:, k, kind(t):kind(t) + 1])
                    ins.then_inc(sem("tnt_ready"), 1)
                    if i:
                        router_exp(i - 1)
                router_exp(len(LIVE[l]) - 1)
                for s in range(2 - l):
                    act.wait_ge(sem("gate_bc_mm"), (2, 5)[l] + s + 1)
                    act.activation(GBC[s], banks(4 + 2 * s, 2), ACT.Copy).then_inc(sem("gate_bc"), 1)
                meet(act, who)

                sl = SLOTS if l == 0 else CAP_X

                def high(group, i):
                    split_high(act, l * LAYER_PIECES + HEAD_PIECES + i, WH[i % 3], group)

                def gathered(group):
                    for k in range(KT):
                        N = group * KT + (l * GROUPS * KT + k + 1)
                        act.wait_ge(sem("gather_mm"), N)
                        act.wait_ge(sem("xs_split"), N)
                        for s in range(2 - l):
                            a, b = (0, 256) if s == 0 else (256, 384)
                            ins = act.activation(XSF[k % 3][:, :, (0, CAP_X)[s]:(CAP_X, SLOTS)[s]],
                                                 banks(2 + k % 6)[:, a:b].rearrange("p (e n) -> p e n", e=GROUP),
                                                 ACT.Identity, bias=modc[:, 24 + k, s:s + 1],
                                                 scale=sc_ffn[:, k, s:s + 1])
                        ins.then_inc(sem("xs_ready"), 1)

                def rows_out(group, e):
                    act.wait_ge(sem("down_mm"), group * GROUP + (l * NE + e + 1))
                    if e == 0:
                        act.wait_ge(sem("oe_used"), group + (l * (GROUPS + 1) + 1))
                    if e == 2:
                        act.wait_ge(sem("ovt_ones"), group + (l * GROUPS + 1))
                    ins = act.activation(OE[e // 2][64 * (e % 2):64 * (e % 2) + 64, :], banks(0, 2)[0:CAP_X, :], ACT.Copy)
                    if l == 0:
                        ins = act.activation(OE[2][32 * e:32 * e + 32, :], banks(0, 2)[CAP_X:SLOTS, :], ACT.Copy)
                    ins.then_inc(sem("oe_ready"), 1)

                def weighted(group, u):
                    act.wait_ge(sem("oe_ready"), group * GROUP + (l * NE + (2 if u == 0 else GROUP)))
                    if u:
                        act.wait_ge(sem("oe_low"), group * (3 - l) + (3 * GROUPS * l + 1))
                    act.activation(OEH[u], OE[u], ACT.Identity, scale=slot_aff[:, u:u + 1]).then_inc(sem("oe_high"), 1)

                def group_body(group, another):

                    def silu(e, h):
                        act.wait_ge(sem("expert_gate_mm"), group * (2 * GROUP) + (2 * l * NE + 2 * e + h + 1))
                        act.activation(HG[0:sl, 512 * h:512 * h + 512], banks(2 + h)[0:sl, :], ACT.Silu)\
                           .then_inc(sem("silu_ready"), 1)

                    for e in range(GROUP):
                        i = e * EX_PIECES
                        if e:
                            high(group, i)
                            high(group, i + 1)
                        if e == 1:
                            act.wait_ge(sem("ovt_mm"), group + (l * GROUPS + 1))
                            if l == 0:
                                act.activation(OVTFC, banks(4)[:, 0:CTX], ACT.Copy, accum_out=slot_aff[:, 2:3])
                            for u in range(2):
                                ins = act.activation(OVTFX[:, u, :], banks(6 + u), ACT.Copy, accum_out=slot_aff[:, u:u + 1])
                            ins.then_inc(sem("ovt_ready"), 1)
                        if e:
                            rows_out(group, e - 1)
                            high(group, i + 2)
                        if e == 2:
                            weighted(group, 0)
                        high(group, i + 3)
                        silu(e, 0)
                        high(group, i + 4)
                        high(group, i + 5)
                        silu(e, 1)
                        for j in range(6, EX_PIECES):
                            high(group, i + j)
                    if another:
                        high(group + 1, 0)
                        high(group + 1, 1)

                def last_rows(group):
                    rows_out(group, GROUP - 1)
                    for u in range(1, 3 - l):
                        weighted(group, u)

                high(0, 0)
                high(0, 1)
                gathered(0)
                high(0, 2)
                with act.Fori(0, GROUPS - 1) as group:
                    group_body(group, True)
                    gathered(group + 1)
                    last_rows(group)
                    high(group + 1, 2)
                group_body(GROUPS - 1, False)
                last_rows(GROUPS - 1)
                meet(act, who)

                for i, t in enumerate(LIVE[l]):
                    act.activation(BIN[:, t, :], YA[:, t, :], ACT.Square, accum_out=ss[:, t:t + 1]).then_inc(sem("y_ss"), 1)
                for j in range(MOD_EARLY if l + 1 < DEPTH else 0):
                    modulate(l + 1, j)
                    if j == 0:
                        act.wait_ge(sem("y_ms"), l + 1)
                        act.activation(rstd[:, 0:NT], ss[:, 0:NT], ACT.Sqrt).then_inc(sem("ys_std"), 1)
                if l + 1 == DEPTH:
                    act.wait_ge(sem("y_ms"), l + 1)
                    act.activation(rstd[:, 0:NT], ss[:, 0:NT], ACT.Sqrt).then_inc(sem("ys_std"), 1)

        @block.vector
        def _(dve):
            who = "dve"

            for l in range(DEPTH):
                G = l * LAYER_PIECES
                if l == 0:
                    dve.wait_ge(sem("silu_c"), 1)
                    dve.tensor_tensor(cv_halves[:, :, 2:4], cv[:, :, :], cv_halves[:, :, 0:2], ALU.subtract)\
                       .then_inc(sem("c_split"), 1)
                for j in range(MOD_EARLY if l else 0, MOD_PIECES):
                    split_low(dve, G + j, HEAD_WL[j % 4], HEAD_WH[j % 4])
                dve.wait_ge(sem("mix_ss"), NT * (l + 1))
                dve.tensor_scalar(ss[:, 0:NT], ss[:, 0:NT], 1.0 / D, EPS, ALU.mult, ALU.add).then_inc(sem("mix_ms"), 1)
                dve.wait_ge(sem("mix_std"), l + 1)
                dve.reciprocal(rstd[:, 0:NT], rstd[:, 0:NT])
                dve.wait_ge(sem("small_loaded"), small_loads(l, "vec"))
                dve.wait_ge(sem("mod_turned"), l + 1)
                dve.tensor_tensor(modc[:, :, :], banks(0)[:, 0:96].rearrange("p (m s) -> p m s", s=2),
                                  v("b_mod").unsqueeze(2).to_broadcast([P, 48, 2]), ALU.add)
                dve.tensor_scalar(half_a0[:, :], v("a0"), 0.5, None, ALU.mult)
                dve.tensor_scalar(half_ka[:, :], v("k_a"), 0.5, None, ALU.mult)
                dve.tensor_scalar(rest_ka[:, :], v("k_a"), -0.5, 1.0, ALU.mult, ALU.add)
                dve.drain()
                for dst, m, add, g in ((sc_mix, 1, 1.0, "g_pre_mix"), (gt_mix, 2, 0.0, "g_post_mix"),
                                       (sc_ffn, 4, 1.0, "g_pre_ffn"), (gt_ffn, 5, 0.0, "g_post_ffn")):
                    dve.scalar_tensor_tensor(out=dst[:, :, :], in0=modc[:, 8 * m:8 * m + 8, :], scalar=add,
                                             in1=v(g).unsqueeze(2).to_broadcast([P, KT, 2]), op0=ALU.add, op1=ALU.mult)
                meet(dve, who)

                def normed(t):
                    if t >= 2:
                        dve.wait_ge(sem("mix_turned"), l * NT + t - 1)
                    dve.tensor_scalar(ZN[t % 2], X[:, t, :], rstd[:, t:t + 1], None, ALU.mult).then_inc(sem("mix_normed"), 1)

                normed(0)
                G += MOD_PIECES
                for t in range(NT):
                    if t + 1 < NT:
                        normed(t + 1)
                    if t in (1, 3):
                        j = MOD_PIECES + t // 2
                        split_low(dve, G + t // 2, HEAD_WL[j % 4], HEAD_WH[j % 4])
                    dve.wait_ge(sem("mix_turned"), l * NT + t + 1)
                    if t >= 3:
                        dve.wait_ge(sem("mix_low"), l * NT + t - 2)
                    src = banks(2 * (t % 4), 2).rearrange("p (k n) -> p k n", k=KT)
                    for k in range(KT // 2):
                        ins = dve.tensor_scalar(ZM[t % 3][:, k, :], src[:, k, :], sc_mix[:, k, kind(t):kind(t) + 1],
                                                modc[:, k, kind(t):kind(t) + 1], ALU.mult, ALU.add)
                    ins.then_inc(sem("mix_out_dve"), 1)
                meet(dve, who)

                for c in range(NCHUNK_IN):
                    if c % 2 == 0 and c // 2 + 2 < IN_PIECES:
                        j = MOD_PIECES + c // 2 + 2
                        split_low(dve, G + c // 2 + 2, HEAD_WL[j % 4], HEAD_WH[j % 4])
                    src = banks(2 * (c % 4), 2)[:, 0:NTOK]
                    if c < C_LORA:
                        dve.wait_ge(sem("in_mm"), l * NCHUNK_IN + c + 1)
                        tap = [v("conv")[:, 9 * j + c:9 * j + c + 1] for j in range(3)]
                        dve.tensor_scalar(U[:, c, :], src, tap[1], None, ALU.mult)
                        dve.drain()
                        for a, b in SEQS:
                            dve.scalar_tensor_tensor(out=U[:, c, a + 1:b], in0=src[:, a:b - 1], scalar=tap[0],
                                                     in1=U[:, c, a + 1:b], op0=ALU.mult, op1=ALU.add)
                        dve.drain()
                        for a, b in SEQS:
                            ins = dve.scalar_tensor_tensor(out=U[:, c, a:b - 1], in0=src[:, a + 1:b], scalar=tap[2],
                                                           in1=U[:, c, a:b - 1], op0=ALU.mult, op1=ALU.add)
                        ins.then_inc(sem("in_out_dve"), 1)
                    elif c == C_GD2:
                        dve.wait_ge(sem("in_mm"), l * NCHUNK_IN + c + 1)
                        dve.wait_ge(sem("in_out_act"), l * 8 + 3)
                        dve.tensor_tensor(area(PROJ, 768)[64:96, :], src[64:96, :], SIN[64:96, :], ALU.mult)
                        dve.tensor_scalar(GD[:, 0, :], GD[:, 0, :], 0.5, 0.5, ALU.mult, ALU.add)
                        dve.tensor_scalar(GD[0:32, 1, :], GD[0:32, 1, :], 0.5, 0.5, ALU.mult, ALU.add)\
                           .then_inc(sem("in_out_dve"), 1)
                    elif c == C_KR:
                        dve.wait_ge(sem("in_mm"), l * NCHUNK_IN + c + 1)
                        dve.tensor_tensor(KROPE[64:96, :], src[64:96, :], COS[64:96, :], ALU.mult)
                        dve.drain()
                        dve.tensor_tensor(KROPE[64:96, :], KROPE[64:96, :], area(PROJ, 768)[64:96, :], ALU.add)\
                           .then_inc(sem("in_out_dve"), 1)
                meet(dve, who)

                meet(dve, who)

                for i, (j, w) in enumerate(((1, 128), (0, 256))):
                    dve.wait_ge(sem("lat_ss"), 2 * l + i + 1)
                    ins = dve.tensor_scalar(PR[j], banks(2 * j, 2)[:, 0:NTOK], 1.0 / w, EPS, ALU.mult, ALU.add)
                ins.then_inc(sem("lat_ms"), 1)
                dve.wait_ge(sem("lat_std"), l + 1)
                dve.reciprocal(PR[1], PR[1])
                dve.drain()
                dve.scalar_tensor_tensor(out=KVD, in0=KVD, scalar=v("g_kv"), in1=PR[1], op0=ALU.mult, op1=ALU.mult)\
                   .then_inc(sem("lat_normed"), 1)
                dve.reciprocal(PR[0], PR[0])
                dve.drain()
                for j in range(2):
                    dve.scalar_tensor_tensor(out=QD[:, j, :], in0=QD[:, j, :], scalar=v("g_q")[:, j:j + 1], in1=PR[0],
                                             op0=ALU.mult, op1=ALU.mult)
                dve.drain().then_inc(sem("lat_normed"), 1)
                for j in range(2):
                    dve.tensor_copy(KTH[j][64:96, :], KROPE[64:96, :])
                dve.drain()
                units = [(h, q) for h in range(HEADS) for q in LIVE[l]]
                U0 = HEADS * LIVE_SUM[l]

                def finish(i):
                    h, q = units[i]
                    dve.reciprocal(sinv[:, i:i + 1], ssum[:, i:i + 1])
                    dve.drain()
                    dve.wait_ge(sem("pv_mm"), U0 + i + 1)
                    dve.tensor_scalar(OQ[:, q, h * HD:(h + 1) * HD], banks(7)[:, 256:320],
                                      sinv[:, i:i + 1], None, ALU.mult).then_inc(sem("o_ready"), 1)

                def projected(h, r):
                    (a, n), qt = SEGS[r], QT[h % 2]
                    dve.wait_ge(sem("proj_mm"), 4 * (l * HEADS + h) + r + 1)
                    dve.tensor_tensor(qt[64:96, a:a + n], banks(6)[64:96, 0:n], COS[64:96, a:a + n], ALU.mult)
                    dve.tensor_tensor(KROPE[64:96, a:a + n], banks(6)[96:128, 0:n], SIN[96:128, a:a + n], ALU.mult)
                    dve.drain()
                    dve.tensor_tensor(qt[64:96, a:a + n], qt[64:96, a:a + n], KROPE[64:96, a:a + n], ALU.add)\
                       .then_inc(sem("proj_out_dve"), 1)

                projected(0, 0)
                projected(0, 1)
                for i, (h, q) in enumerate(units):
                    nk = CTX if q < CT_TILES else NTOK
                    dve.wait_ge(sem("s_mm"), U0 + i + 1)
                    dve.reduce_max(smx[:, i:i + 1], banks(2 * (i % 2), 2)[:, 0:nk], AX_X)
                    dve.drain()
                    dve.tensor_scalar(smn[:, i:i + 1], smx[:, i:i + 1], -MLA_SCALE, None, ALU.mult).then_inc(sem("smax"), 1)
                    if i % len(LIVE[l]) < 2 and h + 1 < HEADS:
                        projected(h + 1, i % len(LIVE[l]))
                    if i >= 2:
                        finish(i - 2)
                dve.wait_ge(sem("p_ready"), U0 + len(units))
                finish(len(units) - 2)
                finish(len(units) - 1)
                meet(dve, who)

                for p in range(PAIRS):
                    dve.tensor_scalar(KK[:, p, :], K3[:, p, :], v("k_k")[:, p:p + 1], None, ALU.mult).then_inc(sem("kk_raw"), 1)
                for p in range(PAIRS):
                    dve.wait_ge(sem("kk_norm"), l * PAIRS + p + 1)
                    dve.tensor_scalar(GT[:, p, :], GT[:, p, :], 1e-12, None, ALU.max)
                dve.drain()
                for p in range(PAIRS):
                    dve.reciprocal(GT[:, p, :], GT[:, p, :])
                dve.drain()
                for p in range(PAIRS):
                    dve.tensor_tensor(KK[:, p, :], KK[:, p, :], GT[:, p, :], ALU.mult)
                for p in range(PAIRS):
                    dve.wait_ge(sem("vst_mm"), l * PAIRS + p + 1)
                    dve.tensor_copy(V3[:, p, :], banks(6 if p == 0 else 2 * (p - 1), 2)[:, 0:NTOK])\
                       .then_inc(sem("vst_out"), 1)
                dve.drain()
                for d in range(2):
                    dve.memset(FMS[0][d], 0.0)
                    dve.memset(FMS[1][d], 0.0)
                meet(dve, who)

                def low_decays(n, d):
                    dve.wait_ge(sem("gates_tanh"), count(l, n, d))
                    dve.tensor_scalar(LW[0:64, :], LW[0:64, :], 0.5, 0.5, ALU.mult, ALU.add).then_inc(sem("lw_ready"), 1)

                def factors(n, d, par, chunk, h):
                    tok, fm = bass.ds(chunk * CH, CH), FMS[par][d]
                    part, cols = slice(64 * h, 64 * h + 64), slice(64 * h, 64 * h + 64)
                    if h == 0:
                        dve.wait_ge(sem("decays_ready"), count(l, n, d))
                        dve.wait_ge(sem("kd_ready"), count(l, n, d))
                    dve.scalar_tensor_tensor(out=fm[part, :, 0, cols], in0=KK[part, :, tok], scalar=-1.0,
                                             in1=EX[part, :, 0, :], op0=ALU.mult, op1=ALU.mult)
                    dve.tensor_tensor(fm[part, :, 1, cols], EX[part, :, 1, :], R3[part, :, tok], ALU.mult)
                    dve.scalar_tensor_tensor(out=fm[part, :, 2, cols], in0=T2[part], scalar=0.5, in1=EN[part],
                                             op0=ALU.mult, op1=ALU.mult)
                    dve.tensor_tensor(fm[part, :, 3, cols], T1[part], EN[part], ALU.mult)
                    if h == 1:
                        end = (CH - 1, 0)[d]
                        dve.tensor_copy(wend[:, par, d, :], EX[:, :, 1, end:end + 1].rearrange("p q o -> p (q o)"))
                        dve.drain().then_inc(sem("fm_ready"), 1)

                def before(n, chunk):
                    for d in range(2):
                        low_decays(n, d)
                        for h in range(2):
                            factors(n, d, 0, chunk[d], h)

                def step(n, par, chunk, nxt):
                    FM = FMS[par]
                    for d in range(2):
                        dve.wait_ge(sem("a_mm"), count(l, n, d))
                        pa = psum[:, 3 * d:3 * d + 3, :]
                        pq = psum[:, 6 + d, 0:384].rearrange("p (q n) -> p q n", q=PAIRS)
                        dve.tensor_tensor(XT[d], pa[:, :, 0:128], level[:, d, 0].unsqueeze(1).to_broadcast([P, PAIRS, P]), ALU.mult)\
                           .then_inc(sem("xt_begun"), 1)
                        dve.tensor_tensor(MA[d][:, :, 0, :], pq, tri[:, 1 - d, 1].unsqueeze(1).to_broadcast([P, PAIRS, P]), ALU.mult)
                        dve.drain()
                        dve.tensor_tensor(XT[d], XT[d], ident.unsqueeze(1).to_broadcast([P, PAIRS, P]), ALU.add)\
                           .then_inc(sem("masked"), 1)
                    for j in range(1, LEVELS):
                        for d in range(2):
                            dve.wait_ge(sem("m_mm"), level_count(l, n, d, j))
                            dve.tensor_tensor(FM[d][:, :, 2, :], psum[:, 6 + d, 0:384].rearrange("p (q n) -> p q n", q=PAIRS),
                                              level[:, d, j].unsqueeze(1).to_broadcast([P, PAIRS, P]), ALU.mult)\
                               .then_inc(sem("m_ready"), 1)
                        if nxt and j == 3:
                            low_decays(n + 1, 0)
                        if nxt and j == 4:
                            factors(n + 1, 0, 1 - par, nxt[0], 0)
                        if nxt and j == 5:
                            low_decays(n + 1, 1)
                        for d in range(2):
                            dve.wait_ge(sem("x_mm"), level_count(l, n, d, j))
                            dve.tensor_tensor(XT[d], XT[d], psum[:, 3 * d + 2, 0:384].rearrange("p (q n) -> p q n", q=PAIRS), ALU.add)\
                               .then_inc(sem("x_ready"), 1)
                        if nxt and j == 4:
                            factors(n + 1, 0, 1 - par, nxt[0], 1)
                    if nxt:
                        for h in range(2):
                            factors(n + 1, 1, 1 - par, nxt[1], h)
                    for d in range(2):
                        dve.wait_ge(sem("scan_mm"), count(l, n, d))
                        dve.tensor_tensor(GB[d], ST[d], psum[:, 3 * d + 1, 192:384].rearrange("p (q n) -> p q n", q=PAIRS), ALU.add)
                        if output_needed(l, n):
                            y = Y3[:, :, bass.ds(chunk[d] * CH, CH)]
                            dve.tensor_tensor(y, y, psum[:, 3 * d + 1, 0:192].rearrange("p (q n) -> p q n", q=PAIRS), ALU.add)
                        dve.drain()
                        dve.tensor_tensor(ST[d], GB[d], wend[:, par, d, :].unsqueeze(2).to_broadcast([P, PAIRS, HD]), ALU.mult)\
                           .then_inc(sem("state_ready"), 1)

                steps(dve, before, step)
                meet(dve, who)

                y4, s4, v4 = [y.rearrange("p q (c n) -> p q c n", n=HD) for y in (Y3, SQ3, VB)]
                st = [gstat[:, i, :].rearrange("p (q c) -> p q c", q=PAIRS) for i in range(2)]

                def of_head(x, p):
                    return x[:, p, :].unsqueeze(2).to_broadcast([P, NCH, HD])

                for p in range(PAIRS):
                    dve.tensor_reduce(st[0][:, p, :], y4[:, p], AX_X, ALU.add)
                    dve.drain()
                    dve.tensor_scalar(st[0][:, p, :], st[0][:, p, :], 1.0 / HD, None, ALU.mult)
                    dve.drain()
                    dve.tensor_tensor(y4[:, p], y4[:, p], of_head(st[0], p), ALU.subtract).then_inc(sem("y_centred"), 1)
                for p in range(PAIRS):
                    dve.wait_ge(sem("y_sq"), l * PAIRS + p + 1)
                    dve.tensor_reduce(st[1][:, p, :], s4[:, p], AX_X, ALU.add)
                dve.drain()
                dve.tensor_scalar(st[1], st[1], 1.0 / HD, GN_EPS, ALU.mult, ALU.add).then_inc(sem("y_var"), 1)
                dve.wait_ge(sem("y_std"), l + 1)
                dve.reciprocal(gstat[:, 1, :], gstat[:, 1, :])
                dve.drain()
                dve.wait_ge(sem("vb_ready"), l + 1)
                for p in range(PAIRS):
                    dve.tensor_tensor(y4[:, p], y4[:, p], of_head(st[1], p), ALU.mult)
                    dve.drain()
                    dve.tensor_tensor(y4[:, p], y4[:, p], LNX[:, 0, p].unsqueeze(1).to_broadcast([P, NCH, HD]), ALU.mult)
                    dve.drain()
                    dve.tensor_tensor(y4[:, p], y4[:, p], v4[:, p], ALU.add).then_inc(sem("y_done"), 1)
                for p in range(PAIRS):
                    split_low(dve, G + IN_PIECES + p, HEAD_WL[p], HEAD_WH[p])
                    dve.wait_ge(sem("gate_out"), l * PAIRS + p + 1)
                    dve.wait_ge(sem("y_turned"), l * PAIRS + p + 1)
                    b = 6 if p == 0 else 2 * (p - 1)
                    dve.tensor_tensor(Y3[:, p, :], banks(b, 2)[:, 0:NTOK], GT[:, p, :], ALU.mult)
                meet(dve, who)

                def gate_diagonals(gt):
                    for s in range(2 - l):
                        for k in range(KT):
                            ins = dve.tensor_scalar(DG[s][:, k * P:(k + 1) * P], ident, gt[:, k, s:s + 1], None, ALU.mult)
                        ins.then_inc(sem("gate_diag"), 1)

                live_cols = slice(LIVE[l][0] * P, NTOK)
                for k in range(KT):
                    if k == 3:
                        split_low(dve, G + IN_PIECES + 3, HEAD_WL[3], HEAD_WH[3])
                    dve.wait_ge(sem("mixed_high"), l * KT + k + 1)
                    dve.tensor_tensor(TOL[:, k, live_cols], TT[:, k, live_cols], TOH[:, k, live_cols], ALU.subtract)\
                       .then_inc(sem("mixed_low"), 1)
                gate_diagonals(gt_mix)
                dve.wait_ge(sem("gate_bc"), (2, 5)[l])
                for i, t in enumerate(LIVE[l]):
                    N = LIVE_SUM[l] + i + 1
                    dve.wait_ge(sem("out_ss"), N)
                    dve.tensor_scalar(ss[:, t:t + 1], ss[:, t:t + 1], 1.0 / D, EPS, ALU.mult, ALU.add).then_inc(sem("out_ms"), 1)
                    dve.wait_ge(sem("out_std"), N)
                    dve.reciprocal(rstd[:, t:t + 1], rstd[:, t:t + 1])
                    dve.drain()
                    dve.scalar_tensor_tensor(out=ZN[0], in0=banks(2 * (i % 2), 2), scalar=rstd[:, t:t + 1], in1=GBC[kind(t)],
                                             op0=ALU.mult, op1=ALU.mult).then_inc(sem("out_out"), 1)
                    dve.drain()
                    dve.tensor_tensor(X[:, t, :], X[:, t, :], ZN[0], ALU.add)
                meet(dve, who)

                dve.wait_ge(sem("ffn_ss"), LIVE_SUM[l + 1])
                dve.tensor_scalar(ss[:, 0:NT], ss[:, 0:NT], 1.0 / D, EPS, ALU.mult, ALU.add).then_inc(sem("ffn_ms"), 1)
                dve.wait_ge(sem("ffn_std"), l + 1)
                dve.reciprocal(rstd[:, 0:NT], rstd[:, 0:NT])
                dve.drain()

                def normed_ffn(i):
                    t, N = LIVE[l][i], LIVE_SUM[l] + i + 1
                    if i >= 3:
                        dve.wait_ge(sem("ffn_turned"), N - 3)
                        dve.wait_ge(sem("xh_low"), N - 3)
                    dve.tensor_scalar(XT_N[i % 3], X[:, t, :], rstd[:, t:t + 1], None, ALU.mult).then_inc(sem("xh_ready"), 1)

                def affinities(i):
                    t = LIVE[l][i]
                    dve.wait_ge(sem("router_exp"), LIVE_SUM[l] + i + 1)
                    dve.reciprocal(rsm[:, t:t + 1], rsm[:, t:t + 1])
                    dve.drain()
                    dve.tensor_scalar(AFF[:, t, :], AFF[:, t, :], rsm[:, t:t + 1], None, ALU.mult).then_inc(sem("aff_ready"), 1)

                for i in range(3):
                    normed_ffn(i)
                gate_diagonals(gt_ffn)
                for i, t in enumerate(LIVE[l]):
                    dve.wait_ge(sem("router_mm"), LIVE_SUM[l] + i + 1)
                    dve.reduce_max(rmx[:, t:t + 1], banks(2 + i % 2)[:, 0:NE], AX_X)
                    dve.drain()
                    dve.tensor_scalar(rmx[:, t:t + 1], rmx[:, t:t + 1], -1.0, None, ALU.mult).then_inc(sem("router_max"), 1)
                    if i + 3 < len(LIVE[l]):
                        normed_ffn(i + 3)
                    if i:
                        affinities(i - 1)
                affinities(len(LIVE[l]) - 1)
                t0 = LIVE[l][0]
                dve.wait_ge(sem("aff_turned"), l + 1)
                dve.tensor_copy(AFT[0:NE, t0 * P:NTOK], banks(2, 2)[0:NE, t0 * P:NTOK])
                dve.drain()
                for a, b, cap in (() if l else ((0, CTX, CAP_C),)) + ((CTX, NTOK, CAP_X),):
                    src = AFT
                    for r in range(cap // TOP8):
                        dve.max(TOP[0:NE, :], src[0:NE, a:b])
                        dve.drain()
                        dve.match_replace(out=WORK[0:NE, a:b], in_to_replace=TOP[0:NE, :], in_values=src[0:NE, a:b], imm_value=-1.0)
                        dve.drain()
                        src = WORK
                dve.tensor_scalar(MASK[0:NE, t0 * P:NTOK], WORK[0:NE, t0 * P:NTOK], 0.0, None, ALU.is_lt)\
                   .then_inc(sem("mask_ready"), 1)
                dve.wait_ge(sem("mask_turned"), l + 1)
                dve.tensor_copy(MASKT[:, t0:NT, :], banks(0)[:, NE * t0:NE * NT].rearrange("p (t n) -> p t n", n=NE))\
                   .then_inc(sem("maskt_ready"), 1)
                dve.wait_ge(sem("count_mm"), l + 1)
                for t in LIVE[l]:
                    dve.scalar_tensor_tensor(out=SLOT[:, t, :], in0=banks(1)[:, NE * t:NE * t + NE],
                                             scalar=0.0, in1=MASKT[:, t, :], op0=ALU.add, op1=ALU.mult)
                dve.drain()
                dve.tensor_scalar(SLOT[:, t0:NT, :], SLOT[:, t0:NT, :], 1.0, None, ALU.subtract)
                meet(dve, who)

                live = LIVE[l]
                sl = SLOTS if l == 0 else CAP_X

                def low(group, i):
                    split_low(dve, l * LAYER_PIECES + HEAD_PIECES + i, WL[i % 3], WH[i % 3], group)

                def gathered(group):
                    for k in range(KT):
                        dve.wait_ge(sem("xs_high"), group * KT + (l * GROUPS * KT + k + 1))
                        dve.tensor_tensor(XSL[:, k, :, 0:sl], XSF[k % 3][:, :, 0:sl], XSH[:, k, :, 0:sl], ALU.subtract)\
                           .then_inc(sem("xs_split"), 1)

                def weighted(group, u):
                    dve.wait_ge(sem("oe_high"), group * (3 - l) + (3 * GROUPS * l + u + 1))
                    dve.scalar_tensor_tensor(out=OEL[u], in0=OE[u], scalar=slot_aff[:, u:u + 1], in1=OEH[u],
                                             op0=ALU.mult, op1=ALU.subtract).then_inc(sem("oe_low"), 1)

                def group_body(group, another):

                    def hidden(e, j):
                        if j % 2 == 0:
                            dve.wait_ge(sem("silu_ready"), group * (2 * GROUP) + (2 * l * NE + 2 * e + j // 2 + 1))
                        dve.wait_ge(sem("up_mm"), group * (4 * GROUP) + (4 * l * NE + 4 * e + j + 1))
                        hg = HG[0:sl, 256 * j:256 * j + 256]
                        dve.tensor_tensor(hg, hg, banks(4 + j % 2)[0:sl, 256 * (j // 2):256 * (j // 2) + 256], ALU.mult)\
                           .then_inc(sem("hidden_ready"), 1)

                    def turned(e, j):
                        dve.wait_ge(sem("ht_mm"), group * (4 * GROUP) + (4 * l * NE + 4 * e + j + 1))
                        src = banks(6 + j % 2)[:, 0:2 * SLOTS].rearrange("p (k n) -> p k n", k=2)[:, :, 0:sl]
                        dve.tensor_copy(HTH[:, 2 * j:2 * j + 2, 0:sl], src)
                        dve.drain()
                        dve.tensor_tensor(HTL[:, 2 * j:2 * j + 2, 0:sl], src, HTH[:, 2 * j:2 * j + 2, 0:sl], ALU.subtract)\
                           .then_inc(sem("ht_ready"), 1)

                    for e in range(GROUP):
                        i = e * EX_PIECES
                        for j in range(0 if e else 5, 6):
                            low(group, i + j)
                            if e == 2 and j == 3:
                                weighted(group, 0)
                        hidden(e, 0)
                        low(group, i + 6)
                        hidden(e, 1)
                        turned(e, 0)
                        low(group, i + 7)
                        hidden(e, 2)
                        turned(e, 1)
                        low(group, i + 8)
                        hidden(e, 3)
                        turned(e, 2)
                        low(group, i + 9)
                        low(group, i + 10)
                        turned(e, 3)
                        low(group, i + 11)
                    if another:
                        low(group + 1, 0)
                        low(group + 1, 1)

                def sums(group, units):
                    for m in units:
                        t, h = live[m // 2], m % 2
                        dve.wait_ge(sem("scatter_mm"), group * (2 * len(live)) + (2 * GROUPS * LIVE_SUM[l] + m + 1))
                        ya = YA[:, t, 512 * h:512 * h + 512]
                        dve.tensor_tensor(ya, ya, banks((0, 1, 4, 5)[m % 4]), ALU.add).then_inc(sem("scatter_out"), 1)

                low(0, 0)
                low(0, 1)
                gathered(0)
                for i in range(2, 5):
                    low(0, i)
                with dve.Fori(0, GROUPS - 1) as group:
                    group_body(group, True)
                    gathered(group + 1)
                    for u in range(1, 3 - l):
                        weighted(group, u)
                    for j in range(3):
                        low(group + 1, 2 + j)
                        sums(group, SHARES[l][j])
                group_body(GROUPS - 1, False)
                for u in range(1, 3 - l):
                    weighted(GROUPS - 1, u)
                sums(GROUPS - 1, range(2 * len(live)))
                meet(dve, who)

                dve.wait_ge(sem("y_ss"), LIVE_SUM[l + 1])
                dve.tensor_scalar(ss[:, 0:NT], ss[:, 0:NT], 1.0 / D, EPS, ALU.mult, ALU.add).then_inc(sem("y_ms"), 1)

                def early(j):
                    if l + 1 < DEPTH:
                        split_low(dve, (l + 1) * LAYER_PIECES + j, HEAD_WL[j % 4], HEAD_WH[j % 4])

                early(0)
                dve.wait_ge(sem("ys_std"), l + 1)
                dve.reciprocal(rstd[:, 0:NT], rstd[:, 0:NT])
                dve.drain()
                for i, t in enumerate(live):
                    if i == 3:
                        early(1)
                    dve.scalar_tensor_tensor(out=YA[:, t, :], in0=YA[:, t, :], scalar=rstd[:, t:t + 1], in1=GBC[kind(t)],
                                             op0=ALU.mult, op1=ALU.mult)
                early(2)
                dve.drain()
                for i, t in enumerate(live):
                    if i == 3:
                        early(3)
                    dve.tensor_tensor(X[:, t, :], X[:, t, :], YA[:, t, :], ALU.add).then_inc(sem("ffn_out"), 1)

        @block.tensor
        def _(pe):
            who = "pe"

            def mm(dst, lhsT, rhs, start=True, stop=True):
                return pe.matmul(dst, lhsT, rhs, start=start, stop=stop)

            pe.wait_ge(sem("consts_loaded"), 16)
            pe.wait_ge(sem("c_split"), 1)
            for _ in range(3):
                pe.nop().then_inc(sem("w_used"), 1)

            def halves(j, k):
                return [w[j % 4].rearrange("p (k n) -> p k n", k=k) for w in (HEAD_WH, HEAD_WL)]

            for l in range(DEPTH):
                g = l * LAYER_PIECES

                def piece_split(j):
                    pe.wait_ge(sem("w_low"), g + j + 1)

                ROWS = MOD_PIECES // 2

                def turn_rows(b):
                    pe.wait_ge(sem("mod_row"), l * ROWS + b + 1)
                    for m in range(4 * b, 4 * b + 4):
                        ins = mm(banks(0)[:, 2 * m:2 * m + 2], MROW[0:4, m * P:(m + 1) * P], fold[0:4, :])
                    return ins

                for j in range(MOD_PIECES):
                    piece_split(j)
                    wh, wl = halves(j, KT)
                    b = j // 2
                    dst = banks(2 + b % 4)[0:4, 256 * (j % 2):256 * (j % 2) + 256]
                    if j % 2 == 0 and b >= 4:
                        pe.wait_ge(sem("mod_row"), l * ROWS + b - 3)
                    for k in range(KT):
                        mm(dst, cv_halves[:, k, :], wh[:, k, :], k == 0, False)
                        ins = mm(dst, cv_halves[:, k, :], wl[:, k, :], False, k == KT - 1)
                    ins.then_inc(sem("w_used"), 1)
                    if j % 2:
                        pe.drain().then_inc(sem("mod_mm"), 1)
                    elif b >= 2:
                        turn_rows(b - 2)
                turn_rows(ROWS - 2)
                turn_rows(ROWS - 1).then_inc(sem("mod_turned"), 1)
                meet(pe, who)

                for t in range(NT):
                    pe.wait_ge(sem("mix_normed"), l * NT + t + 1)
                    if t >= 4:
                        pe.wait_ge(sem("mix_out_act"), l * NT + t - 3)
                        pe.wait_ge(sem("mix_out_dve"), l * NT + t - 3)
                    dst = banks(2 * (t % 4), 2).rearrange("p (k n) -> p k n", k=KT)
                    for k in range(KT):
                        ins = pe.transpose(dst[:, k, :], ZN[t % 2][:, k * P:(k + 1) * P], ident)
                    ins.then_inc(sem("mix_turned"), 1)
                meet(pe, who)

                dve_chunks = [c for c in range(NCHUNK_IN) if c < C_LORA or c in (C_GD2, C_KR)]
                act_chunks = [c for c in range(C_LORA, NCHUNK_IN) if c != C_KR]
                for c in range(NCHUNK_IN):
                    if c % 2 == 0:
                        piece_split(MOD_PIECES + c // 2)
                    if c >= 4:
                        if c - 4 in dve_chunks:
                            pe.wait_ge(sem("in_out_dve"), l * len(dve_chunks) + dve_chunks.index(c - 4) + 1)
                        if c - 4 in act_chunks:
                            pe.wait_ge(sem("in_out_act"), l * len(act_chunks) + act_chunks.index(c - 4) + 1)
                    wh, wl = [w[:, :, (c % 2) * P:(c % 2 + 1) * P] for w in halves(MOD_PIECES + c // 2, KT)]
                    for a, n in (((CTX, CTX), (2 * CTX, CTX)) if in_columns(l, c) else SEGS):
                        dst = banks(2 * (c % 4), 2)[:, a:a + n]
                        for k in range(KT):
                            mm(dst, wh[:, k, :], TTH[:, k, a:a + n], k == 0, False)
                            mm(dst, wh[:, k, :], TTL[:, k, a:a + n], False, False)
                            ins = mm(dst, wl[:, k, :], TTH[:, k, a:a + n], False, k == KT - 1)
                    ins.then_inc(sem("in_mm"), 1)
                    if c % 2:
                        pe.drain().then_inc(sem("w_used"), 1)
                meet(pe, who)

                pe.wait_ge(sem("small_loaded"), small_loads(l, "dft"))
                for t in range(NT):
                    dst = banks(t).rearrange("p (w q n) -> p w q n", w=2, q=2)
                    for q in range(2):
                        ins = mm(dst[:, :, q, :], F[:, q, t * P:(t + 1) * P], CS64.rearrange("p (w n) -> p w n", w=2))
                    ins.then_inc(sem("dft64_mm"), 1)
                pe.wait_ge(sem("dft64_out"), NT * (l + 1))
                for j in range(2):
                    dst = banks(2 * j, 2)
                    for a, b, c0, t_0, tabs in ((0, CTX, 0, 0, (C256, S256)), (CTX, 2 * CTX, 0, CT_TILES, (C512, S512)),
                                                (2 * CTX, 3 * CTX, CTX, CT_TILES, (C512, S512))):
                        nt = CT_TILES if t_0 == 0 else NT - CT_TILES
                        for w, tab in enumerate(tabs):
                            for t in range(nt):
                                ins = mm(dst[:, a:b], Y1[:, t_0 + t, 256 * w + j * P:256 * w + (j + 1) * P],
                                         tab[:, t, c0:c0 + CTX], w == 0 and t == 0, w == 1 and t == nt - 1)
                    ins.then_inc(sem("dft_mm"), 1)
                pe.wait_ge(sem("dft_out"), 2 * l + 2)
                pe.wait_ge(sem("small_loaded"), small_loads(l, "w_f"))
                for j in range(2):
                    for a, n in SEGS:
                        for k in range(2):
                            ins = mm(banks(4 + 2 * j, 2)[:, a:a + n], WF[:, k, j * P:(j + 1) * P], FO[:, k, a:a + n], k == 0, k == 1)
                    ins.then_inc(sem("wf_mm"), 1)
                meet(pe, who)

                pe.wait_ge(sem("small_loaded"), small_loads(l, "mlaw"))
                pe.wait_ge(sem("lat_sq"), l + 1)
                for j, parts in ((1, KTH[:1]), (0, QT)):
                    for a, n in SEGS:
                        for k, part in enumerate(parts):
                            ins = mm(banks(2 * j, 2)[:, a:a + n], ones, part[:, a:a + n], k == 0, k == len(parts) - 1)
                    ins.then_inc(sem("lat_ss"), 1)
                units = [(h, q) for h in range(HEADS) for q in LIVE[l]]
                U0 = HEADS * LIVE_SUM[l]

                def project(h, r):
                    if r:
                        pe.wait_ge(sem("proj_out_act"), 4 * (l * HEADS + h) + r)
                        pe.wait_ge(sem("proj_out_dve"), 2 * (l * HEADS + h) + min(r, 2))
                    a, n = SEGS[r % 2]
                    if r < 2:
                        for k in range(2):
                            ins = mm(banks(6)[:, 0:n], WQ[:, k, h * P:(h + 1) * P], QD[:, k, a:a + n], k == 0, k == 1)
                    else:
                        ins = mm(banks(6)[0:64, 0:n], WKV[:, h * HD:(h + 1) * HD], KVD[:, a:a + n])
                    ins.then_inc(sem("proj_mm"), 1)

                pe.wait_ge(sem("lat_normed"), 2 * l + 1)
                for t in range(NT):
                    if t >= 4:
                        pe.wait_ge(sem("v_out"), l * NT + t - 3)
                    mm(banks(t % 4)[:, 0:RW], KVD[:, t * P:(t + 1) * P], WKV[:, RW:2 * RW]).then_inc(sem("v_mm"), 1)
                    if t == 3:
                        pe.wait_ge(sem("lat_normed"), 2 * l + 2)
                    if t >= 3:
                        project(0, t - 3)
                project(0, 3)
                pe.wait_ge(sem("v_out"), l * NT + NT)

                def turn(i):
                    nk = (CTX if units[i][1] < CT_TILES else NTOK) // P
                    pe.wait_ge(sem("p_ready"), U0 + i + 1)
                    if i >= 1:
                        pe.wait_ge(sem("pt_ready"), U0 + i)
                    for k in range(nk):
                        ins = pe.transpose(banks(4, 2)[:, k * P:(k + 1) * P], PR[i % 2][:, k * P:(k + 1) * P], ident)
                    ins.then_inc(sem("p_turned"), 1)

                def values(i):
                    h, q = units[i]
                    nk = (CTX if q < CT_TILES else NTOK) // P
                    pe.wait_ge(sem("pt_ready"), U0 + i + 1)
                    if i >= 1:
                        pe.wait_ge(sem("o_ready"), U0 + i)
                    for k in range(nk):
                        ins = mm(banks(7)[:, 256:320], PT[i % 2][:, k, :],
                                 VT[:, k, h * HD:(h + 1) * HD], k == 0, k == nk - 1)
                    ins.then_inc(sem("pv_mm"), 1)

                for i, (h, q) in enumerate(units):
                    if q == LIVE[l][0]:
                        pe.wait_ge(sem("proj_out_act"), 4 * (l * HEADS + h + 1))
                        pe.wait_ge(sem("proj_out_dve"), 2 * (l * HEADS + h + 1))
                    if i >= 2:
                        pe.wait_ge(sem("p_ready"), U0 + i - 1)
                    for a, n in (((0, CTX),) if q < CT_TILES else SEGS):
                        ins = mm(banks(2 * (i % 2), 2)[:, a:a + n], QT[h % 2][0:96, q * P:(q + 1) * P], KTH[h % 2][0:96, a:a + n])
                    ins.then_inc(sem("s_mm"), 1)
                    if i % len(LIVE[l]) < 4 and h + 1 < HEADS:
                        project(h + 1, i % len(LIVE[l]))
                    if i >= 1:
                        turn(i - 1)
                    if i >= 2:
                        values(i - 2)
                n = len(units)
                turn(n - 1)
                values(n - 2)
                values(n - 1)
                pe.wait_ge(sem("o_ready"), U0 + n)
                for i, q in enumerate(LIVE[l]):
                    for j in range(3):
                        ins = pe.transpose(banks(i)[:, j * P:(j + 1) * P], OQ[:, q, j * P:(j + 1) * P], ident)
                    ins.then_inc(sem("o_turned"), 1)
                meet(pe, who)

                for p in range(PAIRS):
                    pe.wait_ge(sem("kk_sq"), l * PAIRS + p + 1)
                    for a, n in SEGS:
                        ins = mm(banks(2 * p, 2)[:, a:a + n], headones, SQ3[:, p, a:a + n])
                    ins.then_inc(sem("kk_ss"), 1)
                for p in range(PAIRS):
                    b = 6 if p == 0 else 2 * (p - 1)
                    if p:
                        pe.wait_ge(sem("kk_norm"), l * PAIRS + p)
                    for c in range(NCH):
                        for h in range(2):
                            rows = slice(64 * h, 64 * h + 64)
                            ins = mm(banks(b, 2)[rows, c * CH:(c + 1) * CH], V3[rows, p, c * CH:(c + 1) * CH], ident2[rows, :])
                    ins.then_inc(sem("vst_mm"), 1)
                pe.nop().then_inc(sem("lc_used"), 1) if l == 0 else None
                meet(pe, who)

                def gates(n, d):
                    pe.wait_ge(sem("lc_ready"), count(l, n, d))
                    if not (isinstance(n, int) and n == 0 and d == 0):
                        pe.wait_ge(sem("kd_ready"), count(l, n, d) - 1)
                        pe.wait_ge(sem("decays_ready"), count(l, n, d) - 1)
                    for p in range(PAIRS):
                        mm(psum[:, 4 - 3 * d, p * CH:(p + 1) * CH], W2A2[64:128, d, p * P:(p + 1) * P], LC[64:128, :])
                    z = psum[0:64, 3 * d + 1, 0:RW]
                    mm(z, LC[0:64, :], W2A2[0:64, d, :], True, False)
                    row = 32 + 32 * d
                    mm(z, ones[row:row + 1, 0:64], G2W0[row:row + 1, 1, :], False, True).then_inc(sem("gates_mm"), 1)
                    pe.drain().then_inc(sem("lc_used"), 1)

                def decays(n, d):
                    pe.wait_ge(sem("lw_ready"), count(l, n, d))
                    for p in range(PAIRS):
                        ins = mm(psum[:, 3 * d + 1, 128 * p:128 * p + 128].rearrange("p (k n) -> p k n", k=2),
                                 LW[0:64, p * P:(p + 1) * P], tri[0:64, d, 1:3, 0:64])
                    ins.then_inc(sem("cum_mm"), 1)

                def before(n, chunk):
                    for d in range(2):
                        gates(n, d)
                        decays(n, d)

                def step(n, par, chunk, nxt):
                    FM = FMS[par]
                    first = isinstance(n, int) and n == 0
                    for d in range(2):
                        pe.wait_ge(sem("fm_ready"), count(l, n, d))
                        if not first:
                            pe.wait_ge(sem("state_ready"), count(l, n, d) - 2)
                        for p in range(PAIRS):
                            ar = FM[d][:, p, 0:2, :].rearrange("p k n -> p (k n)")
                            mm(psum[:, 3 * d + p, 0:256], FM[d][:, p, 2, :], ar)
                            mm(psum[:, 3 * d + p, 256:512], FM[d][:, p, 3, :], ar)
                            ins = mm(psum[:, 6 + d, p * P:(p + 1) * P], FM[d][:, p, 0, :], FM[d][:, p, 2, :])
                        ins.then_inc(sem("a_mm"), 1)
                    for d in range(2):
                        pe.wait_ge(sem("masked"), count(l, n, d))
                        pe.wait_ge(sem("a_copied"), count(l, n, d))
                        pe.wait_ge(sem("prd_ready"), count(l, n, d))
                        for w in range(2):
                            for p in range(PAIRS):
                                i = 3 * w + p
                                pe.transpose(psum[:, 3 * d + i // 4, (i % 4) * P:(i % 4 + 1) * P], FM[d][:, p, 2 + w, :], ident)
                        for p in range(PAIRS):
                            ins = mm(psum[:, 3 * d + 2, p:p + 1], BKT[d][:, 1, p, :], v("r_k")[:, p:p + 1])
                        ins.then_inc(sem("bk_turned"), 1)
                    for j in range(1, LEVELS):
                        for d in range(2):
                            if j > 1:
                                pe.wait_ge(sem("x_ready"), level_count(l, n, d, j - 1))
                            for p in range(PAIRS):
                                ins = mm(psum[:, 6 + d, p * P:(p + 1) * P], MA[d][:, p, 0, :], XT[d][:, p, :])
                            ins.then_inc(sem("m_mm"), 1)
                            if j == 1:
                                pe.wait_ge(sem("bkt_ready"), count(l, n, d))
                            for p in range(PAIRS):
                                ins = pe.transpose(psum[:, 3 * d, p * P:(p + 1) * P], XT[d][:, p, :], ident)
                            ins.then_inc(sem("xt_turned"), 1)
                        for d in range(2):
                            pe.wait_ge(sem("m_ready"), level_count(l, n, d, j))
                            pe.wait_ge(sem("xn_ready"), level_count(l, n, d, j))
                            for p in range(PAIRS):
                                ins = mm(psum[:, 3 * d + 2, p * P:(p + 1) * P], XN[d][:, p, :], FM[d][:, p, 2, :])
                            ins.then_inc(sem("x_mm"), 1)
                        if nxt:
                            if j == 1:
                                gates(n + 1, 0)
                            elif j == 3:
                                decays(n + 1, 0)
                            elif j == 4:
                                gates(n + 1, 1)
                            elif j == 5:
                                decays(n + 1, 1)
                    for d in range(2):
                        tok = bass.ds(chunk[d] * CH, CH)
                        pe.wait_ge(sem("x_ready"), level_count(l, n, d, LEVELS - 1))
                        pe.wait_ge(sem("a_masked"), count(l, n, d))
                        for p in range(PAIRS):
                            mm(psum[:, 6 + d, p * HD:(p + 1) * HD], FM[d][:, p, 0, :], ST[d][:, p, :], True, False)
                            ins = mm(psum[:, 6 + d, p * HD:(p + 1) * HD], MA[d][:, p, 2, :], V3[:, p, tok], False, True)
                        ins.then_inc(sem("g_mm"), 1)
                    for d in range(2):
                        pe.wait_ge(sem("g_ready"), count(l, n, d))
                        for p in range(PAIRS):
                            ins = mm(psum[:, 6 + d, 192 + p * HD:192 + (p + 1) * HD], XT[d][:, p, :], GB[d][:, p, :])
                        ins.then_inc(sem("u_mm"), 1)
                    if nxt:
                        pe.wait_ge(sem("decays_ready"), count(l, n + 1, 1))
                    for d in range(2):
                        tok = bass.ds(chunk[d] * CH, CH)
                        pe.wait_ge(sem("u_ready"), count(l, n, d))
                        for p in range(PAIRS):
                            if output_needed(l, n):
                                y = psum[:, 3 * d + 1, p * HD:(p + 1) * HD]
                                mm(y, FM[d][:, p, 1, :], ST[d][:, p, :], True, False)
                                mm(y, MA[d][:, p, 1, :], UB[d][:, p, :], False, False)
                                mm(y, MA[d][:, p, 3, :], V3[:, p, tok], False, True)
                            s = psum[:, 3 * d + 1, 192 + p * HD:192 + (p + 1) * HD]
                            mm(s, BKT[d][:, 0, p, :], UB[d][:, p, :], True, False)
                            ins = mm(s, BKT[d][:, 1, p, :], V3[:, p, tok], False, True)
                        ins.then_inc(sem("scan_mm"), 1)

                steps(pe, before, step)
                meet(pe, who)

                for p in range(PAIRS):
                    for a, n in SEGS:
                        mm(banks(2 * p, 2)[:, a:a + n], G2W0[:, 0, p * P:(p + 1) * P], GD[:, 0, a:a + n], True, False)
                        ins = mm(banks(2 * p, 2)[:, a:a + n], G2W0[0:32, 1, p * P:(p + 1) * P], GD[0:32, 1, a:a + n], False, True)
                    ins.then_inc(sem("gate_mm"), 1)
                for p in range(PAIRS):
                    pe.wait_ge(sem("y_done"), l * PAIRS + p + 1)
                    b = 6 if p == 0 else 2 * (p - 1)
                    if p:
                        pe.wait_ge(sem("gate_out"), l * PAIRS + p)
                    for c in range(NCH):
                        for h in range(2):
                            rows = slice(64 * h, 64 * h + 64)
                            ins = mm(banks(b, 2)[rows, c * CH:(c + 1) * CH], Y3[rows, p, c * CH:(c + 1) * CH], ident2[rows, :])
                    ins.then_inc(sem("y_turned"), 1)
                meet(pe, who)

                def gate_on_all(base):
                    for s in range(2 - l):
                        pe.wait_ge(sem("gate_diag"), base + s + 1)
                        for k in range(KT):
                            ins = mm(banks(4 + 2 * s, 2)[:, k * P:(k + 1) * P], ones, DG[s][:, k * P:(k + 1) * P])
                        ins.then_inc(sem("gate_bc_mm"), 1)

                for i, t in enumerate(LIVE[l]):
                    if i >= 2:
                        pe.wait_ge(sem("out_out"), LIVE_SUM[l] + i - 1)
                    for k in range(KT):
                        if i == 0:
                            pe.wait_ge(sem("mixed_low"), l * KT + k + 1)
                            piece_split(MOD_PIECES + IN_PIECES + k // 2)
                        wh, wl = [w[:, k % 2, :] for w in halves(k // 2, 2)]
                        for h in range(2):
                            dst, cols = banks(2 * (i % 2) + h), slice(512 * h, 512 * h + 512)
                            mm(dst, TOH[:, k, t * P:(t + 1) * P], wh[:, cols], k == 0, False)
                            mm(dst, TOH[:, k, t * P:(t + 1) * P], wl[:, cols], False, False)
                            ins = mm(dst, TOL[:, k, t * P:(t + 1) * P], wh[:, cols], False, k == KT - 1)
                    ins.then_inc(sem("out_mm"), 1)
                    if i == 0:
                        gate_on_all((0, 4)[l])
                for j in range(OUT_PIECES):
                    pe.drain().then_inc(sem("w_used"), 1)
                meet(pe, who)

                def turn_tile(i):
                    N = LIVE_SUM[l] + i + 1
                    pe.wait_ge(sem("xh_ready"), N)
                    if i >= 2:
                        pe.wait_ge(sem("tnt_ready"), N - 2)
                    for k in range(KT):
                        ins = pe.transpose(banks((0, 6)[i % 2], 2)[:, k * P:(k + 1) * P],
                                           XT_N[i % 3][:, k * P:(k + 1) * P], ident)
                    ins.then_inc(sem("ffn_turned"), 1)

                turn_tile(0)
                pe.wait_ge(sem("small_loaded"), small_loads(l, "wr"))
                for i, t in enumerate(LIVE[l]):
                    N = LIVE_SUM[l] + i + 1
                    if i + 1 < len(LIVE[l]):
                        turn_tile(i + 1)
                    pe.wait_ge(sem("tnt_ready"), N)
                    if i >= 2:
                        pe.wait_ge(sem("router_exp"), N - 2)
                    for k in range(KT):
                        ins = mm(banks(2 + i % 2)[:, 0:NE], TNT[i % 2][:, k, :], WR[:, k, :], k == 0, k == KT - 1)
                    ins.then_inc(sem("router_mm"), 1)
                gate_on_all((2, 5)[l])
                pe.wait_ge(sem("aff_ready"), LIVE_SUM[l + 1])
                for t in LIVE[l]:
                    ins = pe.transpose(banks(2, 2)[0:NE, t * P:(t + 1) * P], AFF[:, t, :], ident)
                ins.then_inc(sem("aff_turned"), 1)
                pe.wait_ge(sem("mask_ready"), l + 1)
                for t in LIVE[l]:
                    ins = pe.transpose(banks(0)[:, NE * t:NE * t + NE], MASK[0:NE, t * P:(t + 1) * P], ident[0:NE, 0:NE])
                ins.then_inc(sem("mask_turned"), 1)
                pe.wait_ge(sem("maskt_ready"), l + 1)
                for t in LIVE[l]:
                    first = 0 if t < CT_TILES else CT_TILES
                    for u in range(first, t + 1):
                        ins = mm(banks(1)[:, NE * t:NE * t + NE], upto if u == t else ones, MASKT[:, u, :], u == first, u == t)
                ins.then_inc(sem("count_mm"), 1)
                for name, n in (("oh_used", 1), ("ov_used", 1), ("oe_used", 1), ("xs_split", 3 - 3 * l)):
                    for _ in range(n):
                        pe.nop().then_inc(sem(name), 1)
                meet(pe, who)

                live = LIVE[l]
                sl = SLOTS if l == 0 else CAP_X

                def gather(group):
                    pe.wait_ge(sem("oh_ready"), group + (l * GROUPS + 1))
                    for k in range(KT):
                        N = group * KT + (l * GROUPS * KT + k + 1)
                        if k >= 6:
                            pe.wait_ge(sem("xs_ready"), N - 6)
                        for half in (XHH, XHL):
                            for t in range(CT_TILES, NT):
                                ins = mm(banks(2 + k % 6)[:, 0:256], half[:, t, k * P:(k + 1) * P],
                                         OHX[:, t - CT_TILES].rearrange("p e n -> p (e n)"), half is XHH and t == CT_TILES,
                                         half is XHL and t == NT - 1)
                        if l == 0:
                            for half in (XHH, XHL):
                                for t in range(CT_TILES):
                                    ins = mm(banks(2 + k % 6)[:, 256:384], half[:, t, k * P:(k + 1) * P],
                                             OHC[:, t].rearrange("p e n -> p (e n)"), half is XHH and t == 0,
                                             half is XHL and t == CT_TILES - 1)
                        ins.then_inc(sem("gather_mm"), 1)
                    pe.drain().then_inc(sem("oh_used"), 1)

                def piece(group, i):
                    pe.wait_ge(sem("w_low"), group * GROUP_PIECES + (l * LAYER_PIECES + HEAD_PIECES + i + 1))

                def into(group, dst, i, e):
                    piece(group, i)
                    wh, wl = [w[i % 3].rearrange("p (k n) -> p k n", k=KT) for w in (WH, WL)]
                    for k in range(KT):
                        mm(dst, XSH[:, k, e, 0:sl], wh[:, k, :], k == 0, False)
                        mm(dst, XSH[:, k, e, 0:sl], wl[:, k, :], False, False)
                        ins = mm(dst, XSL[:, k, e, 0:sl], wh[:, k, :], False, k == KT - 1)
                    ins.then_inc(sem("w_used"), 1)

                def gate(group, e, j):
                    into(group, banks(2 + j // 2)[0:sl, 256 * (j % 2):256 * (j % 2) + 256], e * EX_PIECES + j, e)
                    if j % 2:
                        pe.drain().then_inc(sem("expert_gate_mm"), 1)

                def group_body(group):
                    def turn(e, j):
                        pe.wait_ge(sem("hidden_ready"), group * (4 * GROUP) + (4 * l * NE + 4 * e + j + 1))
                        if j >= 2:
                            pe.wait_ge(sem("ht_ready"), group * (4 * GROUP) + (4 * l * NE + 4 * e + j - 1))
                        for c in range(2):
                            ins = pe.transpose(banks(6 + j % 2)[:, c * SLOTS:(c + 1) * SLOTS],
                                               HG[0:SLOTS, (2 * j + c) * P:(2 * j + c + 1) * P], ident[0:SLOTS, 0:SLOTS])
                        ins.then_inc(sem("ht_mm"), 1)

                    def down(i, j, e):
                        piece(group, i)
                        pe.wait_ge(sem("ht_ready"), group * (4 * GROUP) + (4 * l * NE + 4 * e + j + 1))
                        wh, wl = [w[i % 3].rearrange("p (k n) -> p k n", k=2) for w in (WH, WL)]
                        for c in range(2):
                            k = 2 * j + c
                            for h in range(2):
                                dst, cols = banks(h)[0:sl, :], slice(512 * h, 512 * h + 512)
                                mm(dst, HTH[:, k, 0:sl], wh[:, c, cols], k == 0, False)
                                mm(dst, HTH[:, k, 0:sl], wl[:, c, cols], False, False)
                                ins = mm(dst, HTL[:, k, 0:sl], wh[:, c, cols], False, k == KT - 1)
                        ins.then_inc(sem("w_used"), 1)

                    for e in range(GROUP):
                        i = e * EX_PIECES
                        if e == 1:
                            pe.wait_ge(sem("ov_ready"), group + (l * GROUPS + 1))
                            if l == 0:
                                for t in range(CT_TILES):
                                    pe.transpose(banks(4)[:, t * P:(t + 1) * P], OVC[:, t].rearrange("p e n -> p (e n)"), ident)
                            for u in range(2):
                                for t in range(4):
                                    ins = pe.transpose(banks(6 + u)[:, t * P:(t + 1) * P],
                                                       OVX[:, t, 2 * u:2 * u + 2, :].rearrange("p e n -> p (e n)"), ident)
                            ins.then_inc(sem("ovt_mm"), 1)
                            pe.drain().then_inc(sem("ov_used"), 1)
                        for j in range(4 if e else 0):
                            gate(group, e, j)
                        if e == 1:
                            pe.wait_ge(sem("ovt_ready"), group + (l * GROUPS + 1))
                        for j in range(4):
                            if j >= 2:
                                pe.wait_ge(sem("hidden_ready"), group * (4 * GROUP) + (4 * l * NE + 4 * e + j - 1))
                            into(group, banks(4 + j % 2)[0:sl, 256 * (j // 2):256 * (j // 2) + 256], i + 4 + j, e)
                            pe.drain().then_inc(sem("up_mm"), 1)
                            if j:
                                turn(e, j - 1)
                        if e:
                            pe.wait_ge(sem("oe_ready"), group * GROUP + (l * NE + e))
                        down(i + 8, 0, e)
                        down(i + 9, 1, e)
                        turn(e, 3)
                        down(i + 10, 2, e)
                        down(i + 11, 3, e)
                        pe.drain().then_inc(sem("down_mm"), 1)

                def scatter(group, units):
                    pe.wait_ge(sem("oe_low"), group * (3 - l) + (3 * GROUPS * l + 3 - l))
                    pe.wait_ge(sem("ovt_ones"), group + (l * GROUPS + 1))
                    for m in units:
                        t, h = live[m // 2], m % 2
                        if m >= 4:
                            pe.wait_ge(sem("scatter_out"), group * (2 * len(live)) + (2 * GROUPS * LIVE_SUM[l] + m - 3))
                        dst, cols = banks((0, 1, 4, 5)[m % 4]), slice(512 * h, 512 * h + 512)
                        if t < CT_TILES:
                            mm(dst, OVTC[:, t * P:(t + 1) * P], OEH[2][:, cols], True, False)
                            ins = mm(dst, OVTC[:, t * P:(t + 1) * P], OEL[2][:, cols], False, True)
                        else:
                            for u in range(2):
                                ones_u = OVTX[:, u, (t - CT_TILES) * P:(t - CT_TILES + 1) * P]
                                mm(dst, ones_u, OEH[u][:, cols], u == 0, False)
                                ins = mm(dst, ones_u, OEL[u][:, cols], False, u == 1)
                        ins.then_inc(sem("scatter_mm"), 1)

                def scattered(group):
                    pe.drain().then_inc(sem("oe_used"), 1)
                    pe.wait_ge(sem("scatter_out"), group * (2 * len(live)) + (2 * GROUPS * LIVE_SUM[l] + 2 * len(live)))

                def opening(group, former=None):
                    pe.wait_ge(sem("xs_split"), group * KT + (l * GROUPS * KT + KT + 3))
                    for j in range(4):
                        gate(group, 0, j)
                        if former is not None and j > 0:
                            scatter(former, SHARES[l][j - 1])
                    if former is not None:
                        scattered(former)

                gather(0)
                opening(0)
                with pe.Fori(0, GROUPS - 1) as group:
                    group_body(group)
                    gather(group + 1)
                    opening(group + 1, group)
                group_body(GROUPS - 1)
                scatter(GROUPS - 1, range(2 * len(live)))
                scattered(GROUPS - 1)
                meet(pe, who)


def shape_constants(np):
    i = np.arange(P)
    same = (i[:, None] // 64) == (i[None, :] // 64)
    before = [same & (i[:, None] < i[None, :]), same & (i[:, None] > i[None, :])]
    tri = [np.stack([b | np.eye(P, dtype=bool), b, b | np.eye(P, dtype=bool)]) for b in before]
    lev = []
    for b in before:
        for j in range(LEVELS):
            m = 2 ** j
            lev.append(b & (i[:, None] // (2 * m) == i[None, :] // (2 * m)) & (i[:, None] // m != i[None, :] // m))
    cols = [np.eye(P), np.ones((P, P)), same, np.concatenate([t.transpose(1, 0, 2).reshape(P, -1) for t in tri], 1),
            i[:, None] <= i[None, :], np.tile(np.eye(64), (2, 1)), np.tile(np.arange(CAP_X), (P, 1)),
            np.stack(lev).transpose(1, 0, 2).reshape(P, -1), np.tile(np.eye(2), (P // 2, 1)), np.zeros((P, 1))]
    consts = np.concatenate([np.asarray(c, np.float32) for c in cols], 1)
    assert consts.shape == (P, NCONST)

    def dft(n, scale):
        a = 2 * np.pi * (np.outer(np.arange(n), np.arange(n)) % n) / n
        return np.cos(a) * scale, np.sin(a) * scale

    def tiles(a):
        return a.reshape(-1, P, a.shape[1]).transpose(1, 0, 2).reshape(P, -1)

    c5, s5 = dft(SEQ, (SEQ * 64) ** -0.5)
    c2, s2 = dft(CTX, (CTX * 64) ** -0.5)
    c6, s6 = dft(64, 1.0)
    two = np.zeros((P, 2, P))
    for h in range(2):
        two[64 * h:64 * h + 64, 0, 64 * h:64 * h + 64] = c6
        two[64 * h:64 * h + 64, 1, 64 * h:64 * h + 64] = s6
    tables = np.concatenate([tiles(c5), tiles(-s5), tiles(c2), tiles(-s2), two.reshape(P, -1)], 1).astype(np.float32)

    inv = (np.float32(10000.0) ** (-np.arange(8, dtype=np.float32) / np.float32(8))).astype(np.float32)
    pos = np.arange(SEQ)
    rope = np.zeros((P, 2, NTOK), np.float32)
    rope[64:96, 0, :CTX] = 1.0
    for half, q in enumerate((pos // 64, pos % 64)):
        ang = (q.astype(np.float32)[None, :] * inv[:, None]).astype(np.float32)
        for part in range(2):
            r = 64 + 16 * half + 8 * part
            rope[r:r + 8, 0, CTX:] = np.cos(ang)
            rope[r:r + 8, 1, CTX:] = np.sin(ang) * (1 if part else -1)
    rope[96:128] = rope[64:96]
    return consts, tables, rope.reshape(P, -1)


def kernel(**inputs):
    import numpy as np
    import concourse.bacc as bacc
    from concourse.bass_utils import run_bass_kernel_spmd as run

    a = {k: np.asarray(x) for k, x in inputs.items()}
    consts, tables, rope = shape_constants(np)

    def cols(x):
        return x.reshape(DEPTH, -1, P).transpose(0, 2, 1)

    cvec = np.stack([a["c"].reshape(KT, P).T, a["c_ctx"].reshape(KT, P).T], 2)
    vecs = np.concatenate([
        cols(a["b_mod"]), cols(a["g_pre_mix"]), cols(a["g_pre_ffn"]), cols(a["g_post_mix"]), cols(a["g_post_ffn"]),
        cols(a["conv_rkv"]), cols(a["rwkv_k_k"]), cols(a["rwkv_k_a"]), cols(a["rwkv_r_k"].reshape(DEPTH, -1)),
        cols(a["rwkv_a0"]), cols(a["mla_g_q"]), cols(a["mla_g_kv"])], 2)
    swap = np.concatenate([np.arange(8, 16), np.arange(0, 8), np.arange(24, 32), np.arange(16, 24)])
    w = a["w_in"]
    o_gd, o_q, o_kr, o_f = 3 * RW + 128, 3 * RW + 128 + GATE_LORA, 3 * RW + 128 + GATE_LORA + 384, 3 * RW + 128 + GATE_LORA + 416
    z = lambda n: np.zeros((DEPTH, D, n), np.float32)
    kr = w[:, :, o_kr:o_kr + 32]
    w_in = np.concatenate([w[:, :, 0:o_gd + GATE_LORA], z(32), kr[:, :, swap], z(32),
                           w[:, :, o_q:o_kr], z(64), kr, z(32), w[:, :, o_f:]], 2)
    assert w_in.shape[2] == NCHUNK_IN * P
    lora = np.concatenate([a["rwkv_w2"], a["rwkv_a2"]], 2).transpose(0, 2, 1, 3).reshape(DEPTH, P, 768)
    g2w0 = np.zeros((DEPTH, P, 2, RW), np.float32)
    g2w0[:, :, 0] = a["rwkv_g2"][:, :P]
    g2w0[:, 0:32, 1] = a["rwkv_g2"][:, P:]
    g2w0[:, 32, 1] = a["rwkv_w0"][:, 0]
    g2w0[:, 64, 1] = a["rwkv_w0"][:, 1]
    ln = np.stack([a["rwkv_lnx_w"], a["rwkv_lnx_b"]], 1).reshape(DEPTH, 2, PAIRS, 2, HD)
    lnx = np.repeat(ln.transpose(0, 3, 1, 2, 4).reshape(DEPTH, 2, -1), 64, axis=1)
    q6 = a["mla_w_qup"].reshape(DEPTH, 256, HEADS, 96)
    w_q = np.concatenate([q6, q6[:, :, :, 64:][:, :, :, swap]], 3).reshape(DEPTH, 256, HEADS * P)
    kv6 = a["mla_w_kvup"].reshape(DEPTH, P, HEADS, 2, HD)
    w_kv = kv6.transpose(0, 1, 3, 2, 4).reshape(DEPTH, P, 768)
    arrays = {
        "x_in": a["x"][0], "ctx_in": a["ctx"][0], "cvec": cvec, "consts": consts, "dft": tables, "rope": rope, "vecs": vecs,
        "w_mod": a["w_mod"], "w_in": w_in, "w_out": a["w_out"], "lora": lora, "g2w0": g2w0.reshape(DEPTH, P, -1),
        "lnx": lnx, "w_q": w_q, "w_kv": w_kv, "w_f": a["w_fourier"], "w_r": a["w_router"],
        "w_eg": a["w_expert_gate"].reshape(DEPTH * NE, D, FF), "w_eu": a["w_expert_up"].reshape(DEPTH * NE, D, FF),
        "w_ed": a["w_expert_down"].reshape(DEPTH * NE, FF, D),
    }
    nc = bacc.Bacc("TRN2", target_bir_lowering=False, num_devices=1)
    args, sent = [], {}
    for name, x in arrays.items():
        sent[f"{name}_dram"] = np.ascontiguousarray(x)
        args.append(nc.dram_tensor(f"{name}_dram", x.shape, F32, kind="ExternalInput").ap())
    out = nc.dram_tensor("out_dram", (SEQ, D), F32, kind="ExternalOutput").ap()
    hybrid_layers(nc, *args, out)
    r = run(nc, [sent], core_ids=[0])
    return r.results[0]["out_dram"].reshape(1, SEQ, D)
```
